# Optimizing a Trainium2 kernel written in Bass

```python
import math
import jax, jax.numpy as jnp
from jax import lax
import numpy as np

D_MODEL = 1024
BATCH = 1
SEQ = 1024
DEPTH = 1

N_MEM = 256
GM_GROUPS = 4
GM_DIM = 128
GM_CHUNK = 128
GM_WIDTH = GM_GROUPS * GM_DIM
DN_HEADS = 4
DN_DK = 128
DN_DV = 128
DN_CHUNK = 64
CONV_W = 4
DN_QK = DN_HEADS * DN_DK
DN_V = DN_HEADS * DN_DV
MIX_WIDTH = GM_WIDTH + DN_V
D_FF = 4 * D_MODEL
XA_HEADS = 4
XA_DIM = D_MODEL // XA_HEADS
EPS = 1e-6
IN_SIZES = (GM_WIDTH, GM_WIDTH, DN_QK, DN_QK, DN_V, DN_V, DN_HEADS, DN_HEADS)
D_IN = 2 * GM_WIDTH + 2 * DN_QK + 2 * DN_V + 2 * DN_HEADS


def rmsnorm(x, g):
    xf = x.astype(jnp.float32)
    y = xf * lax.rsqrt(jnp.mean(xf * xf, axis=-1, keepdims=True) + EPS)
    return (y * g.astype(jnp.float32)).astype(x.dtype)

def layernorm(x, g, b):
    xf = x.astype(jnp.float32)
    mu = jnp.mean(xf, axis=-1, keepdims=True)
    var = jnp.mean(jnp.square(xf - mu), axis=-1, keepdims=True)
    y = (xf - mu) * lax.rsqrt(var + EPS)
    return (y * g.astype(jnp.float32) + b.astype(jnp.float32)).astype(x.dtype)

def l2norm(x):
    return x * lax.rsqrt(jnp.sum(x * x, axis=-1, keepdims=True) + EPS)

def split_cols(t, sizes):
    idx = [int(i) for i in np.cumsum(np.array(sizes))[:-1]]
    return jnp.split(t, idx, axis=-1)

def chunk_spatial_gating(u, v, ln_g, ln_b, w_s, b_s):
    bsz, s, _ = u.shape
    nc = s // GM_CHUNK
    u = jax.nn.gelu(u).reshape(bsz, nc, GM_CHUNK, GM_GROUPS, GM_DIM)
    v = jax.nn.gelu(v).reshape(bsz, nc, GM_CHUNK, GM_GROUPS, GM_DIM)
    v = layernorm(v, ln_g, ln_b)
    causal = jnp.tril(jnp.ones((GM_CHUNK, GM_CHUNK), dtype=bool))
    w = jnp.where(causal, w_s, jnp.zeros_like(w_s))
    mixed = jnp.einsum('gts,bcsgd->bctgd', w, v) + jnp.transpose(b_s)[None, None, :, :, None]
    return (u * mixed).reshape(bsz, s, GM_WIDTH)

def causal_dwconv(x, w):
    c = x.shape[-1]
    return lax.conv_general_dilated(
        x, w[:, None, :].astype(x.dtype), window_strides=(1,), padding=[(CONV_W - 1, 0)],
        dimension_numbers=('NWC', 'WIO', 'NWC'), feature_group_count=c)

def gated_delta_rule(q, k, v, g, beta):
    f32 = jnp.float32
    bsz, s, h, dk = q.shape
    dv = v.shape[-1]
    c = DN_CHUNK
    n = s // c

    def chunks(t):
        return t.astype(f32).reshape(bsz, n, c, h, -1).transpose(0, 3, 1, 2, 4)

    q = chunks(q) * (dk ** -0.5)
    k = chunks(k)
    v = chunks(v)
    beta = beta.astype(f32).reshape(bsz, n, c, h).transpose(0, 3, 1, 2)[..., None]
    g = g.astype(f32).reshape(bsz, n, c, h).transpose(0, 3, 1, 2)
    decay = jnp.cumsum(g, axis=-1)
    tri = jnp.tril(jnp.ones((c, c), dtype=bool))
    strict = jnp.tril(jnp.ones((c, c), dtype=bool), -1)
    lmask = jnp.exp(jnp.where(tri, decay[..., :, None] - decay[..., None, :], -jnp.inf))

    k_beta = k * beta
    v_beta = v * beta
    m = jnp.where(strict, jnp.einsum('bhnid,bhnjd->bhnij', k_beta, k) * lmask, 0.0)
    a = m + jnp.eye(c, dtype=f32)
    rhs = jnp.concatenate([v_beta, k_beta * jnp.exp(decay)[..., None]], axis=-1)
    sol = lax.linalg.triangular_solve(a, rhs, left_side=True, lower=True, unit_diagonal=True)
    u_c = sol[..., :dv]
    w_c = sol[..., dv:]

    qk = jnp.where(tri, jnp.einsum('bhnid,bhnjd->bhnij', q, k) * lmask, 0.0)
    q_dec = q * jnp.exp(decay)[..., None]
    k_dec = k * jnp.exp(decay[..., -1:] - decay)[..., None]
    chunk_decay = jnp.exp(decay[..., -1])

    xs = tuple(jnp.moveaxis(t, 2, 0) for t in (qk, q_dec, k_dec, u_c, w_c, chunk_decay))

    def step(state, inp):
        qk_i, q_dec_i, k_dec_i, u_i, w_i, cd_i = inp
        v_new = u_i - jnp.einsum('bhck,bhkv->bhcv', w_i, state)
        o = jnp.einsum('bhck,bhkv->bhcv', q_dec_i, state) + jnp.einsum('bhij,bhjv->bhiv', qk_i, v_new)
        state = state * cd_i[..., None, None] + jnp.einsum('bhck,bhcv->bhkv', k_dec_i, v_new)
        return state, o

    s0 = jnp.zeros((bsz, h, dk, dv), f32)
    _, o = lax.scan(step, s0, xs)
    return o.transpose(1, 0, 3, 2, 4).reshape(bsz, s, h, dv)

def hybrid_mixer(h, w_in, gm_ln_g, gm_ln_b, gm_ws, gm_bs, dn_conv, dn_a_log, dn_dt_bias, dn_onorm, w_out):
    bsz, s, _ = h.shape
    proj = h @ w_in
    gu, gv, q, k, v, gate, b_logit, a_logit = split_cols(proj, IN_SIZES)

    y_a = chunk_spatial_gating(gu, gv, gm_ln_g, gm_ln_b, gm_ws, gm_bs)

    qkv = jax.nn.silu(causal_dwconv(jnp.concatenate([q, k, v], axis=-1), dn_conv))
    q, k, v = split_cols(qkv, (DN_QK, DN_QK, DN_V))
    q = l2norm(q.astype(jnp.float32).reshape(bsz, s, DN_HEADS, DN_DK))
    k = l2norm(k.astype(jnp.float32).reshape(bsz, s, DN_HEADS, DN_DK))
    v = v.reshape(bsz, s, DN_HEADS, DN_DV)
    beta = jax.nn.sigmoid(b_logit.astype(jnp.float32))
    g = -jnp.exp(dn_a_log.astype(jnp.float32)) * jax.nn.softplus(
        a_logit.astype(jnp.float32) + dn_dt_bias.astype(jnp.float32))
    o = gated_delta_rule(q, k, v, g, beta)
    o = rmsnorm(o, dn_onorm) * jax.nn.silu(gate.astype(jnp.float32).reshape(bsz, s, DN_HEADS, DN_DV))
    y_b = o.reshape(bsz, s, DN_V).astype(h.dtype)

    return jnp.concatenate([y_a, y_b], axis=-1) @ w_out

def memory_cross_attention(h, m, w_q, w_k, w_v, w_o):
    bsz, s, _ = h.shape
    nm = m.shape[1]
    q = (h @ w_q).reshape(bsz, s, XA_HEADS, XA_DIM)
    k = (m @ w_k).reshape(bsz, nm, XA_HEADS, XA_DIM)
    v = (m @ w_v).reshape(bsz, nm, XA_HEADS, XA_DIM)
    scores = jnp.einsum('bshd,bmhd->bhsm', q, k).astype(jnp.float32) * (XA_DIM ** -0.5)
    p = jax.nn.softmax(scores, axis=-1).astype(v.dtype)
    o = jnp.einsum('bhsm,bmhd->bshd', p, v).reshape(bsz, s, D_MODEL)
    return o @ w_o

def squared_relu_mlp(h, w1, w2):
    return jnp.square(jax.nn.relu(h @ w1)) @ w2

def first_inputs(seed: int = 0) -> dict:
    key = jax.random.key(seed)
    ks = jax.random.split(key, 26)
    f32 = jnp.float32
    L = DEPTH

    def nrm(k, shape, scale):
        return jax.random.normal(k, shape, f32) * scale

    def gain(k, shape):
        return 1.0 + 0.02 * jax.random.normal(k, shape, f32)

    dt = jnp.exp(jax.random.uniform(ks[11], (L, DN_HEADS), f32, math.log(1e-3), math.log(1e-1)))
    return {
        "x": nrm(ks[0], (BATCH, SEQ, D_MODEL), 1.0),
        "mem": nrm(ks[1], (BATCH, N_MEM, D_MODEL), 1.0),
        "norm_mix": gain(ks[2], (L, D_MODEL)),
        "w_in": nrm(ks[3], (L, D_MODEL, D_IN), D_MODEL ** -0.5),
        "gm_ln_g": gain(ks[4], (L, GM_GROUPS, GM_DIM)),
        "gm_ln_b": nrm(ks[5], (L, GM_GROUPS, GM_DIM), 0.02),
        "gm_ws": nrm(ks[6], (L, GM_GROUPS, GM_CHUNK, GM_CHUNK), GM_CHUNK ** -0.5),
        "gm_bs": gain(ks[7], (L, GM_GROUPS, GM_CHUNK)),
        "dn_conv": nrm(ks[8], (L, CONV_W, 2 * DN_QK + DN_V), CONV_W ** -0.5),
        "dn_a_log": jnp.log(jax.random.uniform(ks[9], (L, DN_HEADS), f32, 1.0, 16.0)),
        "dn_dt_bias": dt + jnp.log(-jnp.expm1(-dt)),
        "dn_onorm": gain(ks[10], (L, DN_DV)),
        "w_out": nrm(ks[12], (L, MIX_WIDTH, D_MODEL), MIX_WIDTH ** -0.5),
        "norm_xa": gain(ks[13], (L, D_MODEL)),
        "norm_mem": gain(ks[14], (L, D_MODEL)),
        "xa_wq": nrm(ks[15], (L, D_MODEL, D_MODEL), D_MODEL ** -0.5),
        "xa_wk": nrm(ks[16], (L, D_MODEL, D_MODEL), D_MODEL ** -0.5),
        "xa_wv": nrm(ks[17], (L, D_MODEL, D_MODEL), D_MODEL ** -0.5),
        "xa_wo": nrm(ks[18], (L, D_MODEL, D_MODEL), D_MODEL ** -0.5),
        "norm_ffn": gain(ks[19], (L, D_MODEL)),
        "ffn_w1": nrm(ks[20], (L, D_MODEL, D_FF), D_MODEL ** -0.5),
        "ffn_w2": nrm(ks[21], (L, D_FF, D_MODEL), D_FF ** -0.5),
        "norm_final": gain(ks[22], (D_MODEL,)),
    }

def first_block(x, mem, norm_mix, w_in, gm_ln_g, gm_ln_b, gm_ws, gm_bs, dn_conv, dn_a_log, dn_dt_bias,
              dn_onorm, w_out, norm_xa, norm_mem, xa_wq, xa_wk, xa_wv, xa_wo, norm_ffn, ffn_w1, ffn_w2,
              norm_final):
    for l in range(DEPTH):
        h = rmsnorm(x, norm_mix[l])
        x = x + hybrid_mixer(h, w_in[l], gm_ln_g[l], gm_ln_b[l], gm_ws[l], gm_bs[l], dn_conv[l],
                             dn_a_log[l], dn_dt_bias[l], dn_onorm[l], w_out[l])
        m = rmsnorm(mem, norm_mem[l])
        x = x + memory_cross_attention(rmsnorm(x, norm_xa[l]), m, xa_wq[l], xa_wk[l], xa_wv[l], xa_wo[l])
        x = x + squared_relu_mlp(rmsnorm(x, norm_ffn[l]), ffn_w1[l], ffn_w2[l])
    return rmsnorm(x, norm_final)


D_MIX = D_MODEL
W_POOL = D_MIX // 4
W_SCONV = D_MIX // 4
W_CONF = D_MIX // 4
W_ATTN = D_MIX // 4
POOL_WINDOWS = (2, 4, 8, 16)
N_POOL_GROUPS = len(POOL_WINDOWS)
POOL_GROUP = W_POOL // N_POOL_GROUPS
SCONV_K = 3
CONF_K = 31
N_HEADS = 4
HEAD_V = W_ATTN // N_HEADS
HEAD_QK = HEAD_V // 2
SPLIT_SIZES = (W_POOL, W_SCONV, W_SCONV, W_SCONV, W_CONF, W_CONF, W_ATTN, W_ATTN, W_ATTN)
D_IN_2 = sum(SPLIT_SIZES)
D_FF_2 = ((8 * D_MODEL + 3 * 256 - 1) // (3 * 256)) * 256
REL_BUCKETS = 32
REL_MAX_EXACT = REL_BUCKETS // 2
REL_MAX_DIST = 128
Q_BLOCK = 128
NEG_INF = -1e30


def rms_norm(x, g):
    xf = x.astype(jnp.float32)
    y = xf * lax.rsqrt(jnp.mean(xf * xf, axis=-1, keepdims=True) + EPS)
    return (y * g.astype(jnp.float32)).astype(x.dtype)

def layer_norm(x, g, b):
    xf = x.astype(jnp.float32)
    mu = jnp.mean(xf, axis=-1, keepdims=True)
    xc = xf - mu
    y = xc * lax.rsqrt(jnp.mean(xc * xc, axis=-1, keepdims=True) + EPS)
    return (y * g.astype(jnp.float32) + b.astype(jnp.float32)).astype(x.dtype)

def causal_dwconv_2(u, w):
    k = w.shape[0]
    return lax.conv_general_dilated(
        u, w[:, None, :].astype(u.dtype), window_strides=(1,), padding=[(k - 1, 0)],
        dimension_numbers=('NWC', 'WIO', 'NWC'), feature_group_count=u.shape[-1])

def pool_mixer(u, pool_w, pool_scale):
    b, s, _ = u.shape
    c = jnp.cumsum(u.astype(jnp.float32), axis=1)
    pos1 = jnp.arange(1, s + 1)
    parts = []
    for g, win in enumerate(POOL_WINDOWS):
        cg = c[..., g * POOL_GROUP:(g + 1) * POOL_GROUP]
        shifted = jnp.pad(cg, ((0, 0), (win, 0), (0, 0)))[:, :s]
        cnt = jnp.minimum(pos1, win).astype(jnp.float32)[:, None]
        parts.append((cg - shifted) / cnt)
    pooled = jnp.concatenate(parts, axis=-1).astype(u.dtype) - u
    y = jnp.einsum('bsgc,gcd->bsgd', pooled.reshape(b, s, N_POOL_GROUPS, POOL_GROUP), pool_w)
    return y.reshape(b, s, W_POOL) * pool_scale

def rel_bucket(n):
    nf = jnp.maximum(n, 1).astype(jnp.float32)
    large = REL_MAX_EXACT + (jnp.log(nf / REL_MAX_EXACT) / math.log(REL_MAX_DIST / REL_MAX_EXACT)
                             * (REL_BUCKETS - REL_MAX_EXACT)).astype(jnp.int32)
    large = jnp.minimum(large, REL_BUCKETS - 1)
    return jnp.where(n < REL_MAX_EXACT, n, large)

def diff_attention(q, k, v, q_norm_g, k_norm_g, lam, lam_init, subln_g, rel_bias):
    b, s = q.shape[:2]
    q = rms_norm(q, q_norm_g)
    k = rms_norm(k, k_norm_g)
    scale = HEAD_QK ** -0.5
    nb = s // Q_BLOCK
    qb = q.reshape(b, nb, Q_BLOCK, N_HEADS, 2, HEAD_QK).transpose(1, 0, 2, 3, 4, 5)
    starts = jnp.arange(nb, dtype=jnp.int32) * Q_BLOCK
    kpos = jnp.arange(s, dtype=jnp.int32)

    def block(args):
        qblk, start = args
        qpos = start + jnp.arange(Q_BLOCK, dtype=jnp.int32)
        dist = qpos[:, None] - kpos[None, :]
        bias = rel_bias[rel_bucket(jnp.maximum(dist, 0))].astype(jnp.float32)
        bias = bias.transpose(2, 0, 1)[:, None]
        sc = jnp.einsum('bqhmd,bkhmd->bhmqk', qblk, k).astype(jnp.float32) * scale + bias
        sc = jnp.where(dist >= 0, sc, NEG_INF)
        p = jax.nn.softmax(sc, axis=-1)
        a = p[:, :, 0] - lam * p[:, :, 1]
        return jnp.einsum('bhqk,bkhd->bqhd', a.astype(v.dtype), v)

    o = lax.map(block, (qb, starts))
    o = o.transpose(1, 0, 2, 3, 4).reshape(b, s, N_HEADS, HEAD_V)
    o = rms_norm(o, subln_g) * (1.0 - lam_init)
    return o.reshape(b, s, W_ATTN)

def hybrid_layer(x, norm1_g, w_in, pool_w, pool_scale, sconv_w, conf_dw_w, conf_dw_b,
                 conf_ln_g, conf_ln_b, q_norm_g, k_norm_g, lam_q1, lam_k1, lam_q2, lam_k2,
                 subln_g, w_out, norm2_g, w_gate, w_up, w_down, rel_bias, lam_init):
    b, s, _ = x.shape
    h = rms_norm(x, norm1_g)
    z = h @ w_in
    idx = [int(i) for i in np.cumsum(SPLIT_SIZES)[:-1]]
    z_pool, s_b, s_c, s_h, c_a, c_g, zq, zk, zv = jnp.split(z, idx, axis=-1)
    y_pool = pool_mixer(z_pool, pool_w, pool_scale)
    y_sconv = s_b * causal_dwconv_2(s_c * s_h, sconv_w)
    u = c_a * jax.nn.sigmoid(c_g)
    u = causal_dwconv_2(u, conf_dw_w) + conf_dw_b
    y_conf = jax.nn.silu(layer_norm(u, conf_ln_g, conf_ln_b))
    lam = (jnp.exp(jnp.sum(lam_q1.astype(jnp.float32) * lam_k1.astype(jnp.float32)))
           - jnp.exp(jnp.sum(lam_q2.astype(jnp.float32) * lam_k2.astype(jnp.float32))) + lam_init)
    q = zq.reshape(b, s, N_HEADS, 2, HEAD_QK)
    k = zk.reshape(b, s, N_HEADS, 2, HEAD_QK)
    v = zv.reshape(b, s, N_HEADS, HEAD_V)
    y_attn = diff_attention(q, k, v, q_norm_g, k_norm_g, lam, lam_init, subln_g, rel_bias)
    mix = jnp.concatenate([y_pool, y_sconv, y_conf, y_attn], axis=-1)
    x = x + mix @ w_out
    h2 = rms_norm(x, norm2_g)
    x = x + (jax.nn.silu(h2 @ w_gate) * (h2 @ w_up)) @ w_down
    return x

def second_inputs(seed: int = 0) -> dict:
    key = jax.random.key(seed)
    ks = jax.random.split(key, 24)
    f32 = jnp.float32
    nrm = lambda k, shape, sc: jax.random.normal(k, shape, f32) * sc
    L = DEPTH
    return {
        'x': nrm(ks[0], (BATCH, SEQ, D_MODEL), 1.0),
        'norm1_g': 1.0 + nrm(ks[1], (L, D_MODEL), 0.05),
        'w_in': nrm(ks[2], (L, D_MODEL, D_IN_2), D_MODEL ** -0.5),
        'pool_w': nrm(ks[3], (L, N_POOL_GROUPS, POOL_GROUP, POOL_GROUP), POOL_GROUP ** -0.5),
        'pool_scale': 1.0 + nrm(ks[4], (L, W_POOL), 0.1),
        'sconv_w': nrm(ks[5], (L, SCONV_K, W_SCONV), SCONV_K ** -0.5),
        'conf_dw_w': nrm(ks[6], (L, CONF_K, W_CONF), CONF_K ** -0.5),
        'conf_dw_b': nrm(ks[7], (L, W_CONF), 0.02),
        'conf_ln_g': 1.0 + nrm(ks[8], (L, W_CONF), 0.05),
        'conf_ln_b': nrm(ks[9], (L, W_CONF), 0.02),
        'q_norm_g': 1.0 + nrm(ks[10], (L, HEAD_QK), 0.05),
        'k_norm_g': 1.0 + nrm(ks[11], (L, HEAD_QK), 0.05),
        'lam_q1': nrm(ks[12], (L, HEAD_QK), 0.1),
        'lam_k1': nrm(ks[13], (L, HEAD_QK), 0.1),
        'lam_q2': nrm(ks[14], (L, HEAD_QK), 0.1),
        'lam_k2': nrm(ks[15], (L, HEAD_QK), 0.1),
        'subln_g': 1.0 + nrm(ks[16], (L, HEAD_V), 0.05),
        'w_out': nrm(ks[17], (L, D_MIX, D_MODEL), D_MIX ** -0.5),
        'norm2_g': 1.0 + nrm(ks[18], (L, D_MODEL), 0.05),
        'w_gate': nrm(ks[19], (L, D_MODEL, D_FF_2), D_MODEL ** -0.5),
        'w_up': nrm(ks[20], (L, D_MODEL, D_FF_2), D_MODEL ** -0.5),
        'w_down': nrm(ks[21], (L, D_FF_2, D_MODEL), D_FF_2 ** -0.5),
        'rel_bias': nrm(ks[22], (REL_BUCKETS, N_HEADS), 0.5),
    }

def second_block(x, norm1_g, w_in, pool_w, pool_scale, sconv_w, conf_dw_w, conf_dw_b, conf_ln_g,
              conf_ln_b, q_norm_g, k_norm_g, lam_q1, lam_k1, lam_q2, lam_k2, subln_g, w_out,
              norm2_g, w_gate, w_up, w_down, rel_bias):
    for l in range(DEPTH):
        lam_init = 0.8 - 0.6 * math.exp(-0.3 * l)
        x = hybrid_layer(x, norm1_g[l], w_in[l], pool_w[l], pool_scale[l], sconv_w[l],
                         conf_dw_w[l], conf_dw_b[l], conf_ln_g[l], conf_ln_b[l], q_norm_g[l],
                         k_norm_g[l], lam_q1[l], lam_k1[l], lam_q2[l], lam_k2[l], subln_g[l],
                         w_out[l], norm2_g[l], w_gate[l], w_up[l], w_down[l], rel_bias, lam_init)
    return x


def setup_inputs(seed=0):
    out = dict(first_inputs(seed))
    for name, value in second_inputs(seed + 1).items():
        if name != "x":
            out[name + "_2"] = value
    return out


def reference(
    x, mem, norm_mix, w_in, gm_ln_g, gm_ln_b, gm_ws, gm_bs, dn_conv, dn_a_log, dn_dt_bias,
    dn_onorm, w_out, norm_xa, norm_mem, xa_wq, xa_wk, xa_wv, xa_wo, norm_ffn, ffn_w1, ffn_w2,
    norm_final, norm1_g_2, w_in_2, pool_w_2, pool_scale_2, sconv_w_2, conf_dw_w_2, conf_dw_b_2,
    conf_ln_g_2, conf_ln_b_2, q_norm_g_2, k_norm_g_2, lam_q1_2, lam_k1_2, lam_q2_2, lam_k2_2,
    subln_g_2, w_out_2, norm2_g_2, w_gate_2, w_up_2, w_down_2, rel_bias_2,
):
    x = first_block(
        x, mem, norm_mix, w_in, gm_ln_g, gm_ln_b, gm_ws, gm_bs, dn_conv, dn_a_log, dn_dt_bias,
        dn_onorm, w_out, norm_xa, norm_mem, xa_wq, xa_wk, xa_wv, xa_wo, norm_ffn, ffn_w1,
        ffn_w2, norm_final,
    )
    return second_block(
        x, norm1_g_2, w_in_2, pool_w_2, pool_scale_2, sconv_w_2, conf_dw_w_2, conf_dw_b_2,
        conf_ln_g_2, conf_ln_b_2, q_norm_g_2, k_norm_g_2, lam_q1_2, lam_k1_2, lam_q2_2,
        lam_k2_2, subln_g_2, w_out_2, norm2_g_2, w_gate_2, w_up_2, w_down_2, rel_bias_2,
    )


_drawn_inputs = setup_inputs


def setup_inputs(seed=0):
    import zlib

    import numpy as np

    out = dict(_drawn_inputs(seed))
    spreads = {}
    factors = {'gm_ln_g': 8.0,
     'gm_ln_b': 7.494,
     'gm_bs': 5.808,
     'dn_onorm': 5.759,
     'norm_xa': 8.0,
     'norm_mem': 8.0,
     'norm_ffn': 2.83,
     'conf_dw_b_2': 5.957,
     'conf_ln_g_2': 3.995,
     'conf_ln_b_2': 8.0,
     'q_norm_g_2': 8.0,
     'k_norm_g_2': 8.0,
     'lam_q1_2': 41.648,
     'lam_k1_2': 41.424,
     'lam_q2_2': 6.651,
     'lam_k2_2': 178.248,
     'subln_g_2': 3.502,
     'pool_scale_2': 2.856,
     'norm2_g_2': 3.102,
     'rel_bias_2': 2.68}
    for name, (base, spread) in spreads.items():
        noise = np.random.default_rng([zlib.crc32(name.encode()), seed]).standard_normal(out[name].shape)
        drawn = base * np.exp(spread * noise) if base else spread * noise
        out[name] = __import__('jax').numpy.asarray(drawn.astype(out[name].dtype))
    for name, factor in factors.items():
        out[name] = (out[name] * factor).astype(out[name].dtype)
    return out
```

```python
from contextlib import ExitStack

import numpy as np

import concourse.bass as bass
from concourse import mybir

F32 = mybir.dt.float32
F32R = mybir.dt.float32r
ALU = mybir.AluOpType
ACT = mybir.ActivationFunctionType
AX = mybir.AxisListType

P = 128
D = 1024
KT = D // P
SEQ = 1024
HALF = 512
NB = SEQ // P
MEM = 256
EPS = 1e-6
CB = 256
SLAB = KT * CB
HEADS = 4
CONV_W = 4
FF1_CHUNKS = 4096 // CB
FF2_CHUNKS = 2816 // CB
XA_D = 256
LAM_INIT = 0.2
POOL_WINDOWS = (2, 4, 8, 16)
CONF_K = 31
QK2 = 32
HV2 = 64

PARAM_COLS = {}
_at = 0
for _name, _n in [("norm_mix", 8), ("norm_xa", 8), ("norm_mem", 8), ("norm_ffn", 8), ("norm_final", 8),
                  ("norm1_2", 8), ("norm2_2", 8), ("gm_ln_g", 4), ("dn_conv", 48), ("dn_a_log", 4),
                  ("dn_dt_bias", 4), ("dn_onorm", 1), ("w_logits", 64), ("pool_scale", 2), ("sconv_w", 6),
                  ("conf_dw_w", 62), ("conf_dw_b", 2), ("conf_ln_g", 2), ("conf_ln_b", 2), ("q_norm", 1),
                  ("k_norm", 1), ("subln", 1), ("lam", 128), ("rel_bias", 4)]:
    PARAM_COLS[_name] = (_at, _at + _n)
    _at += _n
N_PARAMS = _at

CONST_COLS = {}
_at = 0
for _name, _n in [("ident", 128), ("tri", 128), ("strict", 128), ("levels", 7 * 128), ("ones32", 128),
                  ("ones64", 128), ("pool_edge", 32), ("onehot", 384), ("causal", 128)]:
    CONST_COLS[_name] = (_at, _at + _n)
    _at += _n
N_CONSTS = _at


def constant_tables():
    c = np.zeros((P, N_CONSTS), np.float32)
    i = np.arange(P)

    def put(name, a):
        lo, hi = CONST_COLS[name]
        c[:a.shape[0], lo:hi] = a

    put("ident", np.eye(P))
    put("tri", (i[:, None] <= i[None, :]) * 1.0)
    put("strict", (i[:, None] < i[None, :]) * 1.0)
    lev = [((i[None, :] >> (l + 1)) == (i[:, None] >> (l + 1))) & ((i[None, :] >> l & 1) == 1)
           & ((i[:, None] >> l & 1) == 0) for l in range(7)]
    put("levels", np.stack(lev, 1).reshape(P, 7 * P) * 1.0)
    put("ones32", (i[:, None] // 32 == i[None, :] // 32) * 1.0)
    put("ones64", (i[:, None] // 64 == i[None, :] // 64) * 1.0)
    edge = np.zeros((P, 2, 16))
    for g, win in enumerate(POOL_WINDOWS):
        for t in range(16):
            edge[(g % 2) * 64:(g % 2) * 64 + 64, g // 2, t] = 1.0 / min(t + 1, win)
    put("pool_edge", edge.reshape(P, 32))
    n = np.maximum(255 - np.arange(384), 0)
    large = 16 + (np.log(np.maximum(n, 1).astype(np.float32) / np.float32(16)) / np.float32(np.log(8.0))
                  * np.float32(16)).astype(np.int32)
    bucket = np.where(n < 16, n, np.minimum(large, 31))
    put("onehot", (np.arange(32)[:, None] == bucket[None, :]) * 1.0)
    put("causal", np.where(i[:, None] >= i[None, :], 0.0, -1e30))
    return c


class Count:

    def __init__(self, sem, base=0):
        self.sem, self.base = sem, base

    def at(self, n):
        return self.base + n

    def advance(self, n):
        self.base += n


def build(nc, main, x_t, mem_t, slabs, params, row_params, gm_ws_t, pool_w, consts, x_spill, bias_skew, out_t):
    def sb(stack, name, shape, dt=F32):
        return stack.enter_context(nc.sbuf_tensor(name, shape, dt))

    counters = []

    def counter(name, start=1):
        counters.append(Count(main.enter_context(nc.semaphore(name)), start))
        return counters[-1]

    slab_raw = sb(main, "slab_raw", [P, 2, SLAB])
    slab_hi = sb(main, "slab_hi", [P, 2, SLAB], F32R)
    slab_lo = sb(main, "slab_lo", [P, 2, SLAB], F32R)
    ident = sb(main, "ident", [P, P])
    ones = sb(main, "ones", [P, P])
    par = sb(main, "par", [P, N_PARAMS])
    eps_tile = sb(main, "eps_tile", [P, 1])
    eps_col = eps_tile[:]
    xr = sb(main, "xr", [P, KT, SEQ])

    ps = main.enter_context(nc.psum_tensor("ps", [P, 8, HALF], F32))

    def param(name):
        a, b = PARAM_COLS[name]
        return par[:, a:b]

    def const(name):
        a, b = CONST_COLS[name]
        return consts[:, a:b]

    slab_loaded = [counter("slab_loaded0", 0), counter("slab_loaded1", 0)]
    slab_hi_done = counter("slab_hi_done", 0)
    slab_split = counter("slab_split", 0)
    group_done = counter("group_done")
    bank_free = counter("bank_free", 9)
    loaded = counter("loaded", 0)
    stored = counter("stored")
    sq_ready = counter("sq_ready")
    sum_done = counter("sum_done")
    log_done = counter("log_done")
    rstd_done = counter("rstd_done")
    value_done = counter("value_done")
    hi_done = counter("hi_done")
    lo_done = [counter("lo_done_dve"), counter("lo_done_pool")]
    a_step = counter("a_step")
    v_step = counter("v_step")
    g_step = counter("g_step")
    p_step = counter("p_step")
    def pair(name):
        return [counter(f"{name}{s}") for s in range(2)]

    block_loaded = pair("block_loaded")
    gtri_ready = pair("gtri_ready")
    rows_done = pair("rows_done")
    grams_done = pair("grams_done")
    arg_ready = pair("arg_ready")
    exp_done = pair("exp_done")
    raw_done = pair("raw_done")
    masked = pair("masked")
    turned = pair("turned")
    by_token = pair("by_token")
    level_ready = pair("level_ready")
    tt_ready = pair("tt_ready")
    first_turned = pair("first_turned")
    t_ready = pair("t_ready")
    x_done = pair("x_done")
    x_ready = pair("x_ready")
    prod_done = pair("prod_done")
    ks_done, resid_ready, tr_done, vnew_ready, step_done, state_ready, o_ready = (
        counter(n) for n in
        ("ks_done", "resid_ready", "tr_done", "vnew_ready", "step_done", "state_ready", "o_ready"))
    xa_head_loaded = pair("xa_head_loaded")
    (xa_score_done, xa_max_done, xa_bias_done, xa_exp_done, xa_inv_done, xa_p_ready, xa_pt_done, xa_pt_ready, xa_o_done, xa_o_copied) = (
        counter(n) for n in (
            "xa_score_done", "xa_max_done", "xa_bias_done", "xa_exp_done", "xa_inv_done", "xa_p_ready", "xa_pt_done", "xa_pt_ready", "xa_o_done", "xa_o_copied"))
    (pair_loaded, d_scores, d_biased, d_max, d_exp, d_inv, d_inv2, d_scaled, d_diff, d_turned, d_copied, d_out, d_stored) = (
        counter(n) for n in (
            "pair_loaded", "d_scores", "d_biased", "d_max", "d_exp", "d_inv", "d_inv2", "d_scaled", "d_diff", "d_turned", "d_copied", "d_out", "d_stored"))
    (gate_done, up_done, down_done, gate_read, relu_done, square_done, hid_hi, hid_ready) = (
        counter(n) for n in ("gate_done", "up_done", "down_done", "gate_read", "relu_done", "square_done",
                             "hid_hi", "hid_ready"))
    n_slabs = slabs.shape[0]

    def load_slab(sp, g, slot, check=True):
        if check:
            sp.wait_ge(slab_split.sem, g - 1)
        sp.dma_start(slab_raw[:, slot, :], slabs[bass.ds(g, 1)].rearrange("o p n -> p (o n)"))\
          .then_inc(slab_loaded[slot].sem, 16)

    def split_hi(act, g, g_half, slot):
        act.wait_ge(slab_loaded[slot].sem, 16 * g_half + 16)
        act.activation(slab_hi[:, slot, :], slab_raw[:, slot, :], ACT.Copy).then_inc(slab_hi_done.sem, 1)

    def split_lo(pool, g, slot):
        pool.wait_ge(slab_hi_done.sem, g + 1)
        pool.tensor_tensor(slab_lo[:, slot, :], slab_raw[:, slot, :], slab_hi[:, slot, :].bitcast(F32),
                           ALU.subtract).then_inc(slab_split.sem, 1)

    PASSES = ((0, 0), (0, 1), (1, 0))

    def slab_of(part, slot):
        return (slab_hi, slab_lo)[part][:, slot, :]

    starts = [(c, c.base) for c in counters]

    with nc.Block() as block:
        @block.sync
        def _(sp):
            sp.dma_start(ident[:], const("ident")).then_inc(loaded.sem, 16)
            sp.dma_start(par[:], params).then_inc(loaded.sem, 16)
            for k in range(KT):
                sp.dma_start(xr[:, k, :], x_t[:, k, :]).then_inc(loaded.sem, 16)
            for g in range(4):
                load_slab(sp, g, g % 2, check=g >= 2)
            sp.wait_ge(loaded.sem, 16 * (2 + KT))

        @block.scalar
        def _(act):
            for g in range(2):
                split_hi(act, g, 0, g)

        @block.gpsimd
        def _(pool):
            pool.memset(ones[:], 1.0)
            pool.memset(eps_tile[:], EPS)
            for g in range(2):
                split_lo(pool, g, g)

        @block.tensor
        def _(pe):
            for c, start in starts:
                if start:
                    pe.sem_inc(c.sem, start)
    loaded.advance(16 * (2 + KT))

    def rms_norm(src, gain, tmp, dst, tokens=SEQ):
        w = min(tokens, HALF)
        n_half = tokens // w
        split = isinstance(dst, tuple)
        sq, val, rstd = tmp[:, 0:2], tmp[:, 2:4], tmp[:, 4]
        with nc.Block() as block:
            @block.scalar
            def _(act):
                with act.Fori(0, n_half) as h:
                    tok = bass.ds(h * w, w)
                    for k in range(KT):
                        act.wait_ge(sum_done.sem, sum_done.at(h * KT + k - 1) if k >= 2 else
                                    sum_done.at(h * KT))
                        act.activation(sq[:, k % 2, 0:w], src[:, k, tok], ACT.Square).then_inc(sq_ready.sem, 1)
                    act.wait_ge(sum_done.sem, sum_done.at(h * KT + KT))
                    act.wait_ge(value_done.sem, value_done.at(h * KT))
                    act.activation(rstd[:, 0:w], ps[:, 0, 0:w], ACT.Ln, scale=1.0 / D, bias=eps_col)\
                       .then_inc(log_done.sem, 1)
                    act.wait_ge(log_done.sem, log_done.at(h + 1))
                    act.activation(rstd[:, 0:w], rstd[:, 0:w], ACT.Exp, scale=-0.5).then_inc(rstd_done.sem, 1)
                    if split:
                        for k in range(KT):
                            act.wait_ge(value_done.sem, value_done.at(h * KT + k + 1))
                            act.activation(dst[0][:, k, tok], val[:, k % 2, 0:w], ACT.Copy)\
                               .then_inc(hi_done.sem, 1)

            @block.tensor
            def _(pe):
                with pe.Fori(0, n_half) as h:
                    pe.wait_ge(log_done.sem, log_done.at(h))
                    for k in range(KT):
                        pe.wait_ge(sq_ready.sem, sq_ready.at(h * KT + k + 1))
                        pe.matmul(ps[:, 0, 0:w], ones[:], sq[:, k % 2, 0:w], start=(k == 0),
                                  stop=(k == KT - 1)).then_inc(sum_done.sem, 1)

            @block.vector
            def _(dve):
                with dve.Fori(0, n_half) as h:
                    tok = bass.ds(h * w, w)
                    dve.wait_ge(rstd_done.sem, rstd_done.at(h + 1))
                    for k in range(KT):
                        if split:
                            own = k % 2
                            dve.wait_ge(lo_done[own].sem, lo_done[own].at(h * (KT // 2) + k // 2))
                            o = val[:, k % 2, 0:w]
                        else:
                            o = dst[:, k, tok]
                        dve.scalar_tensor_tensor(out=o, in0=src[:, k, tok], scalar=gain[:, k:k + 1],
                                                 in1=rstd[:, 0:w], op0=ALU.mult, op1=ALU.mult)\
                           .then_inc(value_done.sem, 1)
                        if split and k % 2 == 1:
                            dve.wait_ge(hi_done.sem, hi_done.at(h * KT + k))
                            dve.tensor_tensor(dst[1][:, k - 1, tok], val[:, 0, 0:w],
                                              dst[0][:, k - 1, tok].bitcast(F32), ALU.subtract)\
                               .then_inc(lo_done[0].sem, 1)

            if split:
                @block.gpsimd
                def _(pool):
                    with pool.Fori(0, n_half) as h:
                        tok = bass.ds(h * w, w)
                        for k in range(1, KT, 2):
                            pool.wait_ge(hi_done.sem, hi_done.at(h * KT + k + 1))
                            pool.tensor_tensor(dst[1][:, k, tok], val[:, 1, 0:w],
                                               dst[0][:, k, tok].bitcast(F32), ALU.subtract)\
                                .then_inc(lo_done[1].sem, 1)
        for c, n in ((sq_ready, KT), (sum_done, KT), (log_done, 1), (rstd_done, 1),
                     (value_done, KT)):
            c.advance(n_half * n)
        if split:
            hi_done.advance(n_half * KT)
            for c in lo_done:
                c.advance(n_half * KT // 2)

    slab_at = [0]

    def dense(act_in, n, evacuate, tokens=SEQ, token_major=False, engine="act",
              before=None, after=None):
        base = slab_at[0]
        w = CB if token_major else min(tokens, HALF)
        if token_major:
            groups = [(t,) for t in range(tokens // P)]
        else:
            groups = [(m, h) for m in range(2) for h in range(tokens // w)]
        G = len(groups)

        def passes(f):
            def run(eng):
                if n >= 2:
                    with eng.Fori(0, n // 2) as it:
                        for slot in range(2):
                            f(eng, it * 2 + slot, it, slot)
                if n % 2:
                    f(eng, n - 1, n // 2, 0)
            return run

        flip = base % 2

        @passes
        def sync_step(sp, s, it, par_):
            g = base + s + 4
            load_slab(sp, g, (flip + par_) % 2)

        @passes
        def act_step(act, s, it, par_):
            slot = (flip + par_) % 2
            if engine == "act":
                for j in range(G):
                    act.wait_ge(group_done.sem, group_done.at(s * G + j + 1))
                    evacuate(act, s, j, ps[:, (s_bank(par_, j)), 0:w]).then_inc(bank_free.sem, 1)
            else:
                act.wait_ge(group_done.sem, group_done.at(s * G + G))
            half = it + (base + par_ + 2) // 2
            split_hi(act, base + s + 2, half, slot)

        def s_bank(par_, j):
            return (par_ * G + j) % 8

        @passes
        def dve_step(dve, s, it, par_):
            for j in range(G):
                dve.wait_ge(group_done.sem, group_done.at(s * G + j + 1))
                evacuate(dve, s, j, ps[:, s_bank(par_, j), 0:w]).then_inc(bank_free.sem, 1)

        @passes
        def pool_step(pool, s, it, par_):
            split_lo(pool, base + s + 2, (flip + par_) % 2)

        @passes
        def pe_step(pe, s, it, par_):
            slot = (flip + par_) % 2
            pe.wait_ge(slab_split.sem, base + s + 1)
            for j, grp in enumerate(groups):
                depth = 8 if G >= 4 else 2 * G
                pe.wait_ge(bank_free.sem, bank_free.at(s * G + j + 1 - depth))
                o = ps[:, s_bank(par_, j), 0:w]
                for i, (wp, ap) in enumerate(PASSES):
                    for k in range(KT):
                        if token_major:
                            t, = grp
                            mm = pe.matmul(o, act_in[ap][:, k, t * P:(t + 1) * P],
                                           slab_of(wp, slot)[:, k * CB:(k + 1) * CB],
                                           start=(i == 0 and k == 0), stop=(i == 2 and k == KT - 1))
                        else:
                            m, h = grp
                            mm = pe.matmul(o, slab_of(wp, slot)[:, k * CB + m * P:k * CB + (m + 1) * P],
                                           act_in[ap][:, k, h * w:(h + 1) * w],
                                           start=(i == 0 and k == 0), stop=(i == 2 and k == KT - 1))
                mm.then_inc(group_done.sem, 1)

        with nc.Block() as block:
            @block.sync
            def _(sp):
                if before:
                    before[0](sp)
                sync_step(sp)
                if after:
                    after(sp)

            block.scalar(act_step)
            block.gpsimd(pool_step)
            block.tensor(pe_step)
            if engine == "dve":
                @block.vector
                def _(dve):
                    if before:
                        before[1](dve)
                    dve_step(dve)
        group_done.advance(n * G)
        bank_free.advance(n * G)
        slab_at[0] += n

    def to_tiles(dst, func):
        def ev(eng, s, j, psum):
            m, h = j // 2, j % 2
            return eng.activation(dst[:, bass.ds(s * 2 + m, 1), h * HALF:(h + 1) * HALF]
                                  .rearrange("p o n -> p (o n)"), psum, func)
        return ev

    def to_tokens(dst, func):
        def ev(eng, s, j, psum):
            return eng.activation(dst[:, j, bass.ds(s * CB, CB)], psum, func)
        return ev

    def add_residual(eng, s, j, psum):
        m, h = j // 2, j % 2
        t = xr[:, bass.ds(s * 2 + m, 1), h * HALF:(h + 1) * HALF].rearrange("p o n -> p (o n)")
        return eng.tensor_tensor(t, psum, t, ALU.add)


    def split_tiles(pairs):
        with nc.Block() as block:
            @block.scalar
            def _(act):
                for src, hi, lo in pairs:
                    act.activation(hi, src, ACT.Copy).then_inc(hi_done.sem, 1)

            def subtract(eng, own):
                for n, (src, hi, lo) in enumerate(pairs):
                    if n % 2 == own:
                        eng.wait_ge(hi_done.sem, hi_done.at(n + 1))
                        eng.tensor_tensor(lo, src, hi.bitcast(F32), ALU.subtract)

            block.vector(lambda dve: subtract(dve, 0))
            block.gpsimd(lambda pool: subtract(pool, 1))
        hi_done.advance(len(pairs))

    def norm_units(units, block_ones, tmp, wide=False):
        sq = [tmp[:, 0, 0:HALF], tmp[:, 0, HALF:SEQ]]
        root = [tmp[:, 1, 0:HALF], tmp[:, 1, HALF:SEQ]]
        with nc.Block() as block:
            @block.gpsimd
            def _(pool):
                for n, u in enumerate(units):
                    if n >= 2:
                        pool.wait_ge(p_step.sem, p_step.at(n - 1))
                    pool.tensor_tensor(sq[n % 2], u["src"], u["src"], ALU.mult).then_inc(g_step.sem, 1)

            @block.tensor
            def _(pe):
                for n, u in enumerate(units):
                    pe.wait_ge(g_step.sem, g_step.at(n + 1))
                    if n >= 2:
                        pe.wait_ge(log_done.sem, log_done.at(n - 1))
                    pe.matmul(ps[:, n % 2, :], block_ones, sq[n % 2], start=True, stop=True)\
                      .then_inc(p_step.sem, 1)

            @block.scalar
            def _(act):
                for n, u in enumerate(units):
                    act.wait_ge(p_step.sem, p_step.at(n + 1))
                    if n >= 2:
                        act.wait_ge(v_step.sem, v_step.at(n - 1))
                    act.activation(root[n % 2], ps[:, n % 2, :], ACT.Sqrt if wide else ACT.Ln, scale=u["scale"],
                                   bias=eps_col).then_inc(log_done.sem, 1)
                    if wide:
                        continue
                    act.wait_ge(log_done.sem, log_done.at(n + 1))
                    act.activation(root[n % 2], root[n % 2], ACT.Exp, scale=-0.5).then_inc(rstd_done.sem, 1)

            @block.vector
            def _(dve):
                for n, u in enumerate(units):
                    if wide:
                        dve.wait_ge(log_done.sem, log_done.at(n + 1))
                        dve.reciprocal(root[n % 2], root[n % 2]).then_inc(rstd_done.sem, 1)
                    dve.wait_ge(rstd_done.sem, rstd_done.at(n + 1))
                    if "times" in u:
                        dve.tensor_tensor(root[n % 2], root[n % 2], u["times"], ALU.mult)\
                           .then_inc(value_done.sem, 1)
                        dve.wait_ge(value_done.sem, value_done.at(n + 1))
                    dve.scalar_tensor_tensor(out=u["out"], in0=u["src"], scalar=u["gain"], in1=root[n % 2],
                                             op0=ALU.mult, op1=ALU.mult).then_inc(v_step.sem, 1)
        for c in (g_step, p_step, log_done, rstd_done, v_step):
            c.advance(len(units))
        if "times" in units[0]:
            value_done.advance(len(units))

    def conv(z, n_tiles, weight, taps, tmp, func, bias=None):
        with nc.Block() as block:
            @block.scalar
            def _(act):
                for i in range(n_tiles // 2):
                    for b in range(2):
                        t = i * 2 + b
                        act.wait_ge(a_step.sem, a_step.at(i * 4))
                        act.activation(tmp[:, b], z[:, t], ACT.Copy,
                                       scale=weight[:, (t + 1) * taps - 1:(t + 1) * taps]).then_inc(a_step.sem, 1)
                    for b in range(2):
                        t = i * 2 + b
                        act.wait_ge(v_step.sem, v_step.at(i * 2 * (taps - 1) + (b + 1) * (taps - 1)))
                        act.activation(z[:, t], tmp[:, b], func,
                                       bias=0.0 if bias is None else bias[:, t:t + 1]).then_inc(a_step.sem, 1)

            @block.vector
            def _(dve):
                for i in range(n_tiles // 2):
                    for b in range(2):
                        t = i * 2 + b
                        dve.wait_ge(a_step.sem, a_step.at(i * 4 + b + 1))
                        for back in range(1, taps):
                            if back > 1:
                                dve.wait_ge(v_step.sem, v_step.at(i * 2 * (taps - 1) + b * (taps - 1) + back - 1))
                            dve.scalar_tensor_tensor(
                                out=tmp[:, b, back:SEQ],
                                in0=z[:, t, 0:SEQ - back],
                                scalar=weight[:, (t + 1) * taps - 1 - back:(t + 1) * taps - back],
                                in1=tmp[:, b, back:SEQ], op0=ALU.mult, op1=ALU.add).then_inc(v_step.sem, 1)
        a_step.advance(n_tiles * 2)
        v_step.advance(n_tiles * (taps - 1))

    mix_stack = main.enter_context(ExitStack())
    mix = sb(mix_stack, "mix", [P, 13, SEQ])
    qk = xr
    vv = mix[:, 0:4]
    gate = mix[:, 4:8]
    ya = mix[:, 8:12]
    small = mix[:, 12]

    h_stack = main.enter_context(ExitStack())
    act_hi = sb(h_stack, "h1_hi", [P, KT, SEQ], F32R)
    act_lo = sb(h_stack, "h1_lo", [P, KT, SEQ], F32R)
    tmp = mix[:, 0:3].rearrange("p a (b n) -> p (a b) n", b=2)
    rms_norm(xr, param("norm_mix"), tmp, (act_hi, act_lo))
    h = (act_hi, act_lo)

    dense(h, 2, to_tiles(ya, ACT.Gelu_apprx_tanh))
    gv = mix[:, 0:4].rearrange("p a n -> p (a n)").rearrange("p (t c) -> p t c", t=NB)
    dense(h, 2, to_tokens(gv, ACT.Gelu_apprx_tanh), token_major=True)

    gvn = gv.rearrange("p t (g d) -> p (t g) d", g=4)
    gsq = qk[:, 0:4].rearrange("p a n -> p (a n)").rearrange("p (m d) -> p m d", m=32)
    wT = qk[:, 4, 0:512]
    tri_s = qk[:, 4, 512:640]
    gstat = qk[:, 4, 640:1024]
    rows = qk[:, 5:7].rearrange("p a n -> p (a n)")
    R = qk[:, 7, 0:512]
    gmix = qk[:, 7, 512:1024]
    with nc.Block() as block:
        gsum, gmean, gvar, grstd = (gstat[:, 32 * n:32 * n + 32] for n in range(4))

        @block.sync
        def _(sp):
            sp.dma_start(wT, gm_ws_t).then_inc(loaded.sem, 16)
            sp.dma_start(tri_s, const("tri")).then_inc(loaded.sem, 16)
            sp.dma_start(rows[0:1, 0:1024], row_params).then_inc(loaded.sem, 16)
            sp.wait_ge(loaded.sem, loaded.at(48))

        @block.vector
        def _(dve):
            n = [0]

            def then(ins):
                n[0] += 1
                ins.then_inc(v_step.sem, 1)
                dve.wait_ge(v_step.sem, v_step.at(n[0]))

            then(dve.tensor_reduce(gsum, gvn, AX.X, ALU.add))
            then(dve.tensor_scalar(gmean, gsum, 1.0 / 128, None, ALU.mult))
            then(dve.tensor_tensor(gvn, gvn, gmean.unsqueeze(2).to_broadcast([P, 32, P]), ALU.subtract))
            dve.wait_ge(loaded.sem, loaded.at(48))
            then(dve.tensor_tensor(wT.rearrange("p (g t) -> p g t", g=4), wT.rearrange("p (g t) -> p g t", g=4),
                                   tri_s.unsqueeze(1).to_broadcast([P, 4, P]), ALU.mult))
            dve.wait_ge(a_step.sem, a_step.at(1))
            then(dve.tensor_reduce(gvar, gsq, AX.X, ALU.add))
            then(dve.tensor_scalar(gvar, gvar, 1.0 / 128, EPS, ALU.mult, ALU.add))
            dve.wait_ge(a_step.sem, a_step.at(2))
            then(dve.reciprocal(grstd, grstd))
            then(dve.tensor_tensor(gvn, gvn, grstd.unsqueeze(2).to_broadcast([P, 32, P]), ALU.mult))
            dve.wait_ge(p_step.sem, p_step.at(1))
            then(dve.tensor_copy(rows[0:1, 1024:1536], ps[0:1, 0, 0:512]))
            dve.wait_ge(p_step.sem, p_step.at(2))
            then(dve.tensor_copy(R, ps[:, 1, 0:512]))
            for t in range(NB):
                dve.wait_ge(p_step.sem, p_step.at(3 + t))
                for g in range(4):
                    last = dve.scalar_tensor_tensor(
                        out=gmix[:, g * P:(g + 1) * P], in0=ps[:, 2 + t % 4, g * P:(g + 1) * P],
                        scalar=param("gm_ln_g")[:, g:g + 1], in1=R[:, g * P:(g + 1) * P],
                        op0=ALU.mult, op1=ALU.add)
                then(last)
                u = ya[:, :, t * P:(t + 1) * P]
                then(dve.tensor_tensor(u, u, gmix.rearrange("p (g t) -> p g t", g=4), ALU.mult))

        @block.scalar
        def _(act):
            act.wait_ge(v_step.sem, v_step.at(3))
            act.activation(gsq, gvn, ACT.Square).then_inc(a_step.sem, 1)
            act.wait_ge(v_step.sem, v_step.at(6))
            act.activation(grstd, gvar, ACT.Sqrt).then_inc(a_step.sem, 1)

        @block.tensor
        def _(pe):
            pe.wait_ge(v_step.sem, v_step.at(4))
            pe.matmul(ps[0:1, 0, 0:512], ones[:, 0:1], wT, start=True, stop=True).then_inc(p_step.sem, 1)
            pe.wait_ge(v_step.sem, v_step.at(9))
            for g in range(4):
                c = slice(g * P, (g + 1) * P)
                pe.matmul(ps[:, 1, c], rows[0:1, c], rows[0:1, 1024 + g * P:1024 + (g + 1) * P],
                          start=True, stop=False)
                mm = pe.matmul(ps[:, 1, c], ones[0:1, :], rows[0:1, 512 + g * P:512 + (g + 1) * P],
                               start=False, stop=True)
            mm.then_inc(p_step.sem, 1)
            for t in range(NB):
                if t >= 4:
                    pe.wait_ge(v_step.sem, v_step.at(10 + 2 * (t - 4) + 1))
                for g in range(4):
                    mm = pe.matmul(ps[:, 2 + t % 4, g * P:(g + 1) * P], gv[:, t, g * P:(g + 1) * P],
                                   wT[:, g * P:(g + 1) * P], start=True, stop=True)
                mm.then_inc(p_step.sem, 1)
    loaded.advance(48)
    v_step.advance(10 + 2 * NB)
    a_step.advance(2)
    p_step.advance(2 + NB)

    dense(h, 4, to_tiles(qk, ACT.Copy))
    dense(h, 2, to_tiles(vv, ACT.Copy))
    dense(h, 2, to_tiles(gate, ACT.Silu))
    logits = small[:, 0:64]
    wl_stack = main.enter_context(ExitStack())
    wl_hi = sb(wl_stack, "wl_hi", [P, 64], F32R)
    wl_lo = sb(wl_stack, "wl_lo", [P, 64], F32R)
    with nc.Block() as block:
        @block.scalar
        def _(act):
            act.activation(wl_hi[:], param("w_logits"), ACT.Copy).then_inc(a_step.sem, 1)

        @block.vector
        def _(dve):
            dve.wait_ge(a_step.sem, a_step.at(1))
            dve.tensor_tensor(wl_lo[:], param("w_logits"), wl_hi[:].bitcast(F32), ALU.subtract)\
               .then_inc(v_step.sem, 1)
            dve.wait_ge(p_step.sem, p_step.at(1))
            dve.tensor_copy(logits, ps[:, 0, 0:64])

        @block.tensor
        def _(pe):
            pe.wait_ge(v_step.sem, v_step.at(1))
            for t in range(NB):
                for i, (wp, ap) in enumerate(((0, 0), (0, 1), (1, 0))):
                    for k in range(KT):
                        mm = pe.matmul(ps[:, 0, t * 8:t * 8 + 8], h[ap][:, k, t * P:(t + 1) * P],
                                       (wl_hi, wl_lo)[wp][:, k * 8:k * 8 + 8],
                                       start=(i == 0 and k == 0), stop=(i == 2 and k == KT - 1))
            mm.then_inc(p_step.sem, 1)
    a_step.advance(1)
    v_step.advance(1)
    p_step.advance(1)
    wl_stack.close()
    h_stack.close()

    t_stack = main.enter_context(ExitStack())
    tmp = sb(t_stack, "conv_tmp", [P, 4, SEQ])
    conv(qk, 8, param("dn_conv"), CONV_W, tmp[:, 0:2], ACT.Silu)
    conv(vv, 4, param("dn_conv")[:, 32:48], CONV_W, tmp[:, 0:2], ACT.Silu)
    norm_units([dict(src=z, out=z, scale=1.0, gain=128.0 ** -0.5 if t < 4 else 1.0)
                for t in range(8) for z in (qk[:, t, 0:HALF], qk[:, t, HALF:SEQ])], ones[:], tmp)
    t_stack.close()
    st = main.enter_context(ExitStack())
    W = HEADS * P
    tri = sb(st, "tri", [P, P])
    strict = sb(st, "strict", [P, P])
    levels = sb(st, "levels", [P, 7, P])
    state = sb(st, "state", [P, W])
    resid = sb(st, "resid", [P, W])
    v_new = sb(st, "v_new", [P, W])

    def per_slot(name, n=1):
        return [sb(st, f"{name}{s}", [P, n, W] if n > 1 else [P, W]) for s in range(2)]

    decay = per_slot("decay")
    q_dec = per_slot("q_dec")
    n_mat = per_slot("n_mat")
    qk_mat = per_slot("qk_mat")
    n_lev = per_slot("n_lev", 2)
    k_dec = per_slot("k_dec")
    v_tok = per_slot("v_tok")
    k_cur = per_slot("k_cur")
    x_mat = per_slot("x_mat")
    t_mat = per_slot("t_mat")
    tt_mat = per_slot("tt_mat")
    v_cur = t_mat

    def col(n):
        return small[:, 64 + 32 * n:96 + 32 * n]

    beta, g_log, dec, neg_ed, cd, kd, nbeta, t_abs, t_exp = (col(n) for n in range(9))
    a_exp = small[:, 400:404]

    lg = logits.rearrange("p (b c) -> p b c", c=8)
    with nc.Block() as block:
        three = lambda x: x.rearrange("p (b h) -> p b h", h=4)

        @block.sync
        def _(sp):
            sp.dma_start(tri[:], const("tri")).then_inc(loaded.sem, 16)
            sp.dma_start(strict[:], const("strict")).then_inc(loaded.sem, 16)
            sp.dma_start(levels[:].rearrange("p l n -> p (l n)"), const("levels")).then_inc(loaded.sem, 16)
            sp.wait_ge(loaded.sem, loaded.at(48))

        @block.scalar
        def _(act):
            n = [0]

            def then(ins):
                n[0] += 1
                ins.then_inc(a_step.sem, 1)
                act.wait_ge(a_step.sem, a_step.at(n[0]))

            then(act.activation(three(beta), lg[:, :, 0:4], ACT.Sigmoid))
            act.wait_ge(v_step.sem, v_step.at(1))
            then(act.activation(t_abs, g_log, ACT.Abs))
            then(act.activation(t_exp, t_abs, ACT.Exp, scale=-1.0))
            then(act.activation(t_exp, t_exp, ACT.Ln, bias=1.0))
            then(act.activation(a_exp, param("dn_a_log"), ACT.Exp))
            act.wait_ge(v_step.sem, v_step.at(6))
            then(act.activation(neg_ed, dec, ACT.Exp))
            then(act.activation(cd, ps[:, 1, 0:32], ACT.Exp))
            then(act.activation(kd, kd, ACT.Exp))

        @block.vector
        def _(dve):
            n = [0]

            def then(ins):
                n[0] += 1
                ins.then_inc(v_step.sem, 1)
                dve.wait_ge(v_step.sem, v_step.at(n[0]))

            then(dve.tensor_tensor(three(g_log), lg[:, :, 4:8],
                                   param("dn_dt_bias").unsqueeze(1).to_broadcast([P, NB, 4]), ALU.add))
            dve.wait_ge(a_step.sem, a_step.at(4))
            then(dve.scalar_tensor_tensor(out=g_log, in0=g_log, scalar=0.0, in1=t_exp, op0=ALU.max, op1=ALU.add))
            dve.wait_ge(a_step.sem, a_step.at(5))
            then(dve.scalar_tensor_tensor(out=three(g_log), in0=three(g_log), scalar=-1.0,
                                          in1=a_exp.unsqueeze(1).to_broadcast([P, NB, 4]),
                                          op0=ALU.mult, op1=ALU.mult))
            then(dve.tensor_scalar(nbeta, beta, -1.0, None, ALU.mult))
            dve.wait_ge(p_step.sem, p_step.at(1))
            then(dve.tensor_copy(dec, ps[:, 0, 0:32]))
            then(dve.scalar_tensor_tensor(out=kd, in0=dec, scalar=-1.0, in1=ps[:, 1, 0:32],
                                          op0=ALU.mult, op1=ALU.add))
            dve.wait_ge(a_step.sem, a_step.at(6))
            then(dve.tensor_scalar(neg_ed, neg_ed, -1.0, None, ALU.mult))
            then(dve.memset(state[:], 0.0))

        @block.tensor
        def _(pe):
            pe.wait_ge(v_step.sem, v_step.at(3))
            pe.wait_ge(loaded.sem, loaded.at(48))
            pe.matmul(ps[:, 0, 0:32], tri[:], g_log, start=True, stop=True)
            pe.matmul(ps[:, 1, 0:32], ones[:], g_log, start=True, stop=True).then_inc(p_step.sem, 1)
    loaded.advance(48)
    a_step.advance(8)
    v_step.advance(8)
    p_step.advance(1)


    hs = lambda h: slice(h * P, (h + 1) * P)
    heads = lambda ap: ap.rearrange("p (h n) -> p h n", h=HEADS)
    over_heads = lambda ap: ap.unsqueeze(1).to_broadcast([P, HEADS, P])
    n_it = NB // 2

    def head_block(it, s, h):
        return qk[:, h, bass.ds(it * 256 + s * P, P)]

    def blk(z, it, s):
        return z[:, 0:4, bass.ds(it * 256 + s * P, P)]

    def scal(c, it, s, h):
        return c[:, bass.ds(it * 8 + s * 4 + h, 1)]

    with nc.Block() as block:
        @block.vector
        def _(dve):
            with dve.Fori(0, n_it) as it:
                for s in range(2):
                    dve.wait_ge(o_ready.sem, o_ready.at(it * 2))
                    g4 = g_log[:, bass.ds(it * 8 + s * 4, 4)]
                    dve.tensor_tensor(heads(decay[s][:]), over_heads(tri[:]),
                                      g4.unsqueeze(2).to_broadcast([P, HEADS, P]), ALU.mult)\
                       .then_inc(gtri_ready[s].sem, 1)
                for s in range(2):
                    dve.wait_ge(exp_done[s].sem, exp_done[s].at(it * 2 + 1))
                    for h in range(HEADS):
                        last = dve.tensor_scalar(decay[s][:, hs(h)], ps[:, 3 * s, hs(h)], scal(dec, it, s, h), 0.0,
                                                 ALU.subtract, ALU.min)
                    last.then_inc(arg_ready[s].sem, 1)
                for s in range(2):
                    dve.wait_ge(exp_done[s].sem, exp_done[s].at(it * 2 + 2))
                    dve.wait_ge(grams_done[s].sem, grams_done[s].at(it + 1))
                    for h in range(HEADS):
                        last = dve.scalar_tensor_tensor(out=n_mat[s][:, hs(h)], in0=ps[:, 3 * s + 1, hs(h)],
                                                        scalar=scal(nbeta, it, s, h), in1=decay[s][:, hs(h)],
                                                        op0=ALU.mult, op1=ALU.mult)
                    last.then_inc(raw_done[s].sem, 1)
                    dve.tensor_tensor(qk_mat[s][:], ps[:, 3 * s + 2, :], decay[s][:], ALU.mult)\
                       .then_inc(raw_done[s].sem, 1)
                for s in range(2):
                    dve.wait_ge(level_ready[s].sem, level_ready[s].at(it * 7 + 1))
                    dve.tensor_tensor(heads(tt_mat[s][:]), heads(n_lev[s][:, 0]), over_heads(ident[:]), ALU.add)\
                       .then_inc(tt_ready[s].sem, 1)
                for s in range(2):
                    dve.wait_ge(first_turned[s].sem, first_turned[s].at(it + 1))
                    dve.tensor_copy(t_mat[s][:], ps[:, 3 * s + 2, :]).then_inc(t_ready[s].sem, 1)
                for lev in range(1, 7):
                    for s in range(2):
                        dve.wait_ge(prod_done[s].sem, prod_done[s].at(it * 6 + lev))
                        if lev < 6:
                            dve.tensor_tensor(t_mat[s][:], ps[:, 3 * s + 1, :], t_mat[s][:], ALU.add)\
                               .then_inc(t_ready[s].sem, 1)
                        dve.tensor_tensor(tt_mat[s][:], ps[:, 3 * s + 2, :], tt_mat[s][:], ALU.add)\
                           .then_inc(tt_ready[s].sem, 1)
                for s in range(2):
                    n = it * 2 + s
                    dve.wait_ge(by_token[s].sem, by_token[s].at(it * 2 + 2))
                    dve.wait_ge(ks_done.sem, ks_done.at(n + 1))
                    for h in range(HEADS):
                        last = dve.scalar_tensor_tensor(out=resid[:, hs(h)], in0=ps[:, 6, hs(h)],
                                                        scalar=scal(neg_ed, it, s, h), in1=v_tok[s][:, hs(h)],
                                                        op0=ALU.mult, op1=ALU.add)
                    last.then_inc(resid_ready.sem, 1)
                    dve.wait_ge(step_done.sem, step_done.at(n + 1))
                    for h in range(HEADS):
                        last = dve.scalar_tensor_tensor(out=state[:, hs(h)], in0=state[:, hs(h)],
                                                        scalar=scal(cd, it, s, h), in1=ps[:, 7, hs(h)],
                                                        op0=ALU.mult, op1=ALU.add)
                    last.then_inc(state_ready.sem, 1)

        @block.scalar
        def _(act):
            with act.Fori(0, n_it) as it:
                for s in range(2):
                    act.wait_ge(rows_done[s].sem, rows_done[s].at(it + 1))
                    act.activation(q_dec[s][:], ps[:, 3 * s, :], ACT.Exp).then_inc(exp_done[s].sem, 1)
                    act.wait_ge(arg_ready[s].sem, arg_ready[s].at(it + 1))
                    act.activation(decay[s][:], decay[s][:], ACT.Exp).then_inc(exp_done[s].sem, 1)
                for s in range(2):
                    act.wait_ge(turned[s].sem, turned[s].at(it * 2 + 1))
                    for h in range(HEADS):
                        last = act.activation(k_dec[s][:, hs(h)], ps[:, 3 * s, hs(h)], ACT.Copy,
                                              scale=scal(kd, it, s, h))
                    last.then_inc(by_token[s].sem, 1)
                    act.wait_ge(turned[s].sem, turned[s].at(it * 2 + 2))
                    act.activation(v_tok[s][:], ps[:, 3 * s + 1, :], ACT.Copy).then_inc(by_token[s].sem, 1)
                for lev in range(1, 7):
                    for s in range(2):
                        act.wait_ge(x_done[s].sem, x_done[s].at(it * 6 + lev))
                        act.activation(x_mat[s][:], ps[:, 3 * s, :], ACT.Copy).then_inc(x_ready[s].sem, 1)
                for s in range(2):
                    n = it * 2 + s
                    act.wait_ge(tr_done.sem, tr_done.at(n + 1))
                    for h in range(HEADS):
                        last = act.activation(v_new[:, hs(h)], ps[:, 7, hs(h)], ACT.Copy, scale=scal(beta, it, s, h))
                    last.then_inc(vnew_ready.sem, 1)
                    act.wait_ge(step_done.sem, step_done.at(n + 1))
                    act.activation(blk(qk, it, s), heads(ps[:, 6, :]), ACT.Copy).then_inc(o_ready.sem, 1)

        @block.gpsimd
        def _(pool):
            with pool.Fori(0, n_it) as it:
                for s in range(2):
                    pool.wait_ge(raw_done[s].sem, raw_done[s].at(it * 2 + 1))
                    pool.tensor_tensor(heads(n_mat[s][:]), heads(n_mat[s][:]), over_heads(strict[:]), ALU.mult)\
                        .then_inc(masked[s].sem, 1)
                    pool.wait_ge(masked[s].sem, masked[s].at(it * 3 + 1))
                    pool.tensor_tensor(heads(n_lev[s][:, 0]), heads(n_mat[s][:]), over_heads(levels[:, 0]), ALU.mult)\
                        .then_inc(level_ready[s].sem, 1)
                for s in range(2):
                    pool.wait_ge(raw_done[s].sem, raw_done[s].at(it * 2 + 2))
                    pool.tensor_tensor(heads(n_lev[s][:, 1]), heads(n_mat[s][:]), over_heads(levels[:, 1]), ALU.mult)\
                        .then_inc(level_ready[s].sem, 1)
                for s in range(2):
                    pool.tensor_tensor(heads(qk_mat[s][:]), heads(qk_mat[s][:]), over_heads(tri[:]), ALU.mult)\
                        .then_inc(masked[s].sem, 1)
                for lev in range(2, 7):
                    for s in range(2):
                        if lev == 2:
                            pool.wait_ge(tt_ready[s].sem, tt_ready[s].at(it * 7 + 1))
                        else:
                            pool.wait_ge(x_done[s].sem, x_done[s].at(it * 6 + lev - 2))
                        pool.tensor_tensor(heads(n_lev[s][:, lev % 2]), heads(n_mat[s][:]), over_heads(levels[:, lev]),
                                           ALU.mult).then_inc(level_ready[s].sem, 1)
                for s in range(2):
                    pool.wait_ge(exp_done[s].sem, exp_done[s].at(it * 2 + 1))
                    pool.tensor_tensor(heads(q_dec[s][:]), heads(q_dec[s][:]), blk(qk, it, s), ALU.mult)\
                        .then_inc(masked[s].sem, 1)

        @block.tensor
        def _(pe):
            with pe.Fori(0, n_it) as it:
                for s in range(2):
                    pe.wait_ge(gtri_ready[s].sem, gtri_ready[s].at(it + 1))
                    pe.matmul(ps[:, 3 * s, :], ones[:], decay[s][:], start=True, stop=True).then_inc(rows_done[s].sem, 1)
                for s in range(2):
                    pe.wait_ge(block_loaded[s].sem, block_loaded[s].at(it * 32 + 32))
                    for h in range(HEADS):
                        pe.matmul(ps[:, 3 * s + 1, hs(h)], k_cur[s][:, hs(h)], k_cur[s][:, hs(h)],
                                  start=True, stop=True)
                    for h in range(HEADS):
                        mm = pe.matmul(ps[:, 3 * s + 2, hs(h)], k_cur[s][:, hs(h)], head_block(it, s, h),
                                       start=True, stop=True)
                    mm.then_inc(grams_done[s].sem, 1)
                for s in range(2):
                    pe.wait_ge(arg_ready[s].sem, arg_ready[s].at(it + 1))
                    pe.wait_ge(exp_done[s].sem, exp_done[s].at(it * 2 + 1))
                    for h in range(HEADS):
                        mm = pe.transpose(ps[:, 3 * s, hs(h)], k_cur[s][:, hs(h)], ident[:])
                    mm.then_inc(turned[s].sem, 1)
                    pe.wait_ge(raw_done[s].sem, raw_done[s].at(it * 2 + 1))
                    for h in range(HEADS):
                        mm = pe.transpose(ps[:, 3 * s + 1, hs(h)], v_cur[s][:, hs(h)], ident[:])
                    mm.then_inc(turned[s].sem, 1)
                for s in range(2):
                    pe.wait_ge(tt_ready[s].sem, tt_ready[s].at(it * 7 + 1))
                    pe.wait_ge(raw_done[s].sem, raw_done[s].at(it * 2 + 2))
                    for h in range(HEADS):
                        mm = pe.transpose(ps[:, 3 * s + 2, hs(h)], tt_mat[s][:, hs(h)], ident[:])
                    mm.then_inc(first_turned[s].sem, 1)
                for lev in range(1, 7):
                    for s in range(2):
                        pe.wait_ge(level_ready[s].sem, level_ready[s].at(it * 7 + lev + 1))
                        pe.wait_ge(t_ready[s].sem, t_ready[s].at(it * 6 + lev))
                        if lev == 1:
                            pe.wait_ge(by_token[s].sem, by_token[s].at(it * 2 + 2))
                        for h in range(HEADS):
                            mm = pe.matmul(ps[:, 3 * s, hs(h)], n_lev[s][:, lev % 2, hs(h)], t_mat[s][:, hs(h)],
                                           start=True, stop=True)
                        mm.then_inc(x_done[s].sem, 1)
                    for s in range(2):
                        pe.wait_ge(x_ready[s].sem, x_ready[s].at(it * 6 + lev))
                        pe.wait_ge(tt_ready[s].sem, tt_ready[s].at(it * 7 + lev))
                        if lev < 6:
                            for h in range(HEADS):
                                pe.matmul(ps[:, 3 * s + 1, hs(h)], tt_mat[s][:, hs(h)], x_mat[s][:, hs(h)],
                                          start=True, stop=True)
                        for h in range(HEADS):
                            mm = pe.matmul(ps[:, 3 * s + 2, hs(h)], x_mat[s][:, hs(h)], tt_mat[s][:, hs(h)],
                                           start=True, stop=True)
                        mm.then_inc(prod_done[s].sem, 1)
                for s in range(2):
                    n = it * 2 + s
                    pe.wait_ge(state_ready.sem, state_ready.at(n))
                    pe.wait_ge(o_ready.sem, o_ready.at(n))
                    for h in range(HEADS):
                        mm = pe.matmul(ps[:, 6, hs(h)], k_cur[s][:, hs(h)], state[:, hs(h)], start=True, stop=True)
                    mm.then_inc(ks_done.sem, 1)
                    pe.wait_ge(resid_ready.sem, resid_ready.at(n + 1))
                    pe.wait_ge(tt_ready[s].sem, tt_ready[s].at(it * 7 + 7))
                    for h in range(HEADS):
                        mm = pe.matmul(ps[:, 7, hs(h)], tt_mat[s][:, hs(h)], resid[:, hs(h)], start=True, stop=True)
                    mm.then_inc(tr_done.sem, 1)
                    pe.wait_ge(vnew_ready.sem, vnew_ready.at(n + 1))
                    pe.wait_ge(masked[s].sem, masked[s].at(it * 3 + 3))
                    for h in range(HEADS):
                        pe.matmul(ps[:, 6, hs(h)], state[:, hs(h)], q_dec[s][:, hs(h)], start=True, stop=False)
                        pe.matmul(ps[:, 6, hs(h)], v_new[:, hs(h)], qk_mat[s][:, hs(h)], start=False, stop=True)
                    for h in range(HEADS):
                        mm = pe.matmul(ps[:, 7, hs(h)], k_dec[s][:, hs(h)], v_new[:, hs(h)], start=True, stop=True)
                    mm.then_inc(step_done.sem, 1)

        @block.sync
        def _(sp):
            with sp.Fori(0, n_it) as it:
                for s in range(2):
                    sp.wait_ge(o_ready.sem, o_ready.at(it * 2))
                    sp.wait_ge(state_ready.sem, state_ready.at(it * 2))
                    sp.dma_start(heads(k_cur[s][:]), qk[:, 4:8, bass.ds(it * 256 + s * P, P)])\
                      .then_inc(block_loaded[s].sem, 16)
                    sp.dma_start(heads(v_cur[s][:]), vv[:, 0:4, bass.ds(it * 256 + s * P, P)])\
                      .then_inc(block_loaded[s].sem, 16)
    st.close()

    norm_units([dict(src=z[:, hf * HALF:(hf + 1) * HALF], out=z[:, hf * HALF:(hf + 1) * HALF], scale=1.0 / 128,
                     gain=param("dn_onorm"), times=gate[:, t, hf * HALF:(hf + 1) * HALF])
                for t in range(HEADS) for z in [qk[:, t]] for hf in range(2)], ones[:], vv[:, 0:2])
    y_stack = main.enter_context(ExitStack())
    y = (sb(y_stack, "y1_hi", [P, KT, SEQ], F32R), sb(y_stack, "y1_lo", [P, KT, SEQ], F32R))
    halves = [slice(0, HALF), slice(HALF, SEQ)]
    split_tiles([((ya if t < 4 else qk)[:, t % 4, c], y[0][:, t, c], y[1][:, t, c]) for t in range(KT) for c in halves])

    def reload_x(src):
        def start(sp):
            for k in range(KT):
                sp.dma_start(xr[:, k, :], src[:, k, :]).then_inc(loaded.sem, 16)

        def wait(dve):
            dve.wait_ge(loaded.sem, loaded.at(16 * KT))
        return start, wait

    dense(y, 4, add_residual, engine="dve", before=reload_x(x_t))
    loaded.advance(16 * KT)
    y_stack.close()
    mix_stack.close()

    def scope():
        return main.enter_context(ExitStack())

    xa = scope()
    q_t = sb(xa, "xa_q", [P, KT, SEQ])
    k_t = sb(xa, "xa_k", [P, KT, MEM])
    v_m = sb(xa, "xa_v", [P, 2, D])
    mem = scope()
    mem_x = sb(mem, "mem_x", [P, KT, MEM])
    m = (sb(mem, "mem_hi", [P, KT, MEM], F32R), sb(mem, "mem_lo", [P, KT, MEM], F32R))
    with nc.Block() as block:
        @block.sync
        def _(sp):
            sp.dma_start(mem_x[:], mem_t).then_inc(loaded.sem, 16)
            sp.wait_ge(loaded.sem, loaded.at(16))
    loaded.advance(16)
    tmp = q_t[:, 0:3].rearrange("p a (b n) -> p (a b) n", b=2)
    rms_norm(mem_x, param("norm_mem"), tmp, m, tokens=MEM)
    dense(m, 4, lambda eng, s, j, psum: eng.activation(
        k_t[:, bass.ds(s * 2 + j, 1), :].rearrange("p o n -> p (o n)"), psum, ACT.Copy), tokens=MEM)
    dense(m, 4, to_tokens(v_m, ACT.Copy), tokens=MEM, token_major=True)
    mem.close()

    h_stack = scope()
    h = (sb(h_stack, "h2_hi", [P, KT, SEQ], F32R), sb(h_stack, "h2_lo", [P, KT, SEQ], F32R))
    rms_norm(xr, param("norm_xa"), tmp, h)
    dense(h, 4, to_tiles(q_t, ACT.Copy))
    h_stack.close()

    at = scope()
    q_h = sb(at, "q_h", [P, 2, 2, SEQ])
    k_h = sb(at, "k_h", [P, 2, 2, MEM])
    v_h = sb(at, "v_h", [P, 2, 2, XA_D])
    prob = sb(at, "prob", [P, 2, MEM])
    prob_t = sb(at, "prob_t", [P, 2, 2, HALF])
    stat = sb(at, "stat", [P, 2, 4])

    scale = XA_D ** -0.5
    with nc.Block() as block:
        @block.sync
        def _(sp):
            with sp.Fori(0, 2) as it:
                for s in range(2):
                    sp.wait_ge(xa_o_copied.sem, xa_o_copied.at(it * 8))
                    sp.dma_start(q_h[:, s], q_t[:, bass.ds(it * 4 + s * 2, 2), :]).then_inc(xa_head_loaded[s].sem, 16)
                    sp.dma_start(k_h[:, s], k_t[:, bass.ds(it * 4 + s * 2, 2), :]).then_inc(xa_head_loaded[s].sem, 16)
                    sp.dma_start(v_h[:, s], v_m[:, :, bass.ds(it * 512 + s * 256, 256)])\
                      .then_inc(xa_head_loaded[s].sem, 16)

        @block.tensor
        def _(pe):
            with pe.Fori(0, 2) as it:
                for s in range(2):
                    pe.wait_ge(xa_head_loaded[s].sem, xa_head_loaded[s].at(it * 48 + 48))
                    n0 = it * 16 + s * 8

                    def scores(u):
                        pe.wait_ge(xa_exp_done.sem, xa_exp_done.at(n0 + u - 1 if u >= 1 else n0))
                        for t in range(2):
                            mm = pe.matmul(ps[:, u % 2, 0:MEM], q_h[:, s, t, u * P:(u + 1) * P], k_h[:, s, t, :],
                                           start=(t == 0), stop=(t == 1))
                        mm.then_inc(xa_score_done.sem, 1)

                    scores(0)
                    for u in range(8):
                        if u < 7:
                            scores(u + 1)
                        pe.wait_ge(xa_p_ready.sem, xa_p_ready.at(n0 + u + 1))
                        pe.wait_ge(xa_pt_ready.sem, xa_pt_ready.at(n0 + u - 1 if u >= 1 else n0))
                        for t in range(2):
                            mm = pe.transpose(ps[:, 2 + u % 2, t * P:(t + 1) * P], prob[:, u % 2, t * P:(t + 1) * P],
                                              ident[:])
                        mm.then_inc(xa_pt_done.sem, 1)
                        if u % 4 == 3:
                            hf = u // 4
                            pe.wait_ge(xa_pt_ready.sem, xa_pt_ready.at(n0 + u + 1))
                            pe.wait_ge(xa_o_copied.sem, xa_o_copied.at(it * 8 + s * 4))
                            for dt in range(2):
                                for t in range(2):
                                    mm = pe.matmul(ps[:, 4 + 2 * hf + dt, :], v_h[:, s, t, dt * P:(dt + 1) * P],
                                                   prob_t[:, hf, t, :], start=(t == 0), stop=(t == 1))
                                mm.then_inc(xa_o_done.sem, 1)

        @block.vector
        def _(dve):
            with dve.Fori(0, 2) as it:
                for s in range(2):
                    for u in range(8):
                        n = it * 16 + s * 8 + u
                        st = stat[:, u % 2]
                        dve.wait_ge(xa_score_done.sem, xa_score_done.at(n + 1))
                        dve.tensor_reduce(st[:, 0:1], ps[:, u % 2, 0:MEM], AX.X, ALU.max).then_inc(xa_max_done.sem, 1)
                        dve.wait_ge(xa_max_done.sem, xa_max_done.at(n + 1))
                        dve.tensor_scalar(st[:, 1:2], st[:, 0:1], -scale, None, ALU.mult).then_inc(xa_bias_done.sem, 1)
                        dve.wait_ge(xa_exp_done.sem, xa_exp_done.at(n + 1))
                        dve.reciprocal(st[:, 3:4], st[:, 2:3]).then_inc(xa_inv_done.sem, 1)
                        dve.wait_ge(xa_inv_done.sem, xa_inv_done.at(n + 1))
                        dve.tensor_scalar(prob[:, u % 2], prob[:, u % 2], st[:, 3:4], None, ALU.mult)\
                           .then_inc(xa_p_ready.sem, 1)
                        if u % 4 == 3:
                            for dt in range(2):
                                hf = u // 4
                                dve.wait_ge(xa_o_done.sem, xa_o_done.at(it * 8 + s * 4 + 2 * hf + dt + 1))
                                dve.tensor_copy(q_t[:, bass.ds(it * 4 + s * 2 + dt, 1), halves[hf]]
                                                .rearrange("p o n -> p (o n)"), ps[:, 4 + 2 * hf + dt, :])\
                                   .then_inc(xa_o_copied.sem, 1)

        @block.scalar
        def _(act):
            with act.Fori(0, 2) as it:
                for s in range(2):
                    for u in range(8):
                        n = it * 16 + s * 8 + u
                        st = stat[:, u % 2]
                        act.wait_ge(xa_bias_done.sem, xa_bias_done.at(n + 1))
                        act.wait_ge(xa_pt_done.sem, xa_pt_done.at(n - 1 if u >= 1 else it * 16 + s * 8))
                        act.activation(prob[:, u % 2], ps[:, u % 2, 0:MEM], ACT.Exp, bias=st[:, 1:2], scale=scale,
                                       accum_out=st[:, 2:3]).then_inc(xa_exp_done.sem, 1)
                        act.wait_ge(xa_pt_done.sem, xa_pt_done.at(n + 1))
                        if u % 4 == 0:
                            act.wait_ge(xa_o_done.sem, xa_o_done.at(it * 8 + s * 4))
                        act.activation(prob_t[:, u // 4, :, (u % 4) * P:(u % 4 + 1) * P],
                                       ps[:, 2 + u % 2, 0:MEM].rearrange("p (t n) -> p t n", t=2), ACT.Copy)\
                           .then_inc(xa_pt_ready.sem, 1)
    at.close()
    y_stack = scope()
    y = (sb(y_stack, "y2_hi", [P, KT, SEQ], F32R), sb(y_stack, "y2_lo", [P, KT, SEQ], F32R))
    split_tiles([(q_t[:, t, c], y[0][:, t, c], y[1][:, t, c]) for t in range(KT) for c in halves])
    dense(y, 4, add_residual, engine="dve")
    y_stack.close()
    xa.close()


    def mlp(h, n_chunks, gated, name):
        st = scope()
        hid = [[sb(st, f"{name}_hid{p}{c}", [P, 2, SEQ], F32R) for c in range(2)] for p in range(2)]
        val = sb(st, f"{name}_val", [P, 4, HALF])
        per = 3 if gated else 2
        base = slab_at[0]
        total = per * n_chunks
        ends = base + total == n_slabs
        loops = (n_chunks - 1) // 2 - (1 if ends and (n_chunks - 1) % 2 == 0 else 0)

        def sequence(eng, step):
            def chunk(c0, s0, it, kc, ks):
                for n, (op, dc) in enumerate(([("gate", 0)] if gated else []) + [("up", 0), ("down", -1)]):
                    step(eng, op, kc * it + (c0 + dc), ks * it + (s0 + n), c0 + dc, s0 + n, it)
            if gated:
                step(eng, "gate", 0, 0, 0, 0, 0)
            step(eng, "up", 0, per - 2, 0, per - 2, 0)
            with eng.Fori(0, loops) as it:
                for cc in range(2):
                    chunk(1 + cc, per - 1 + cc * per, it, 2, 2 * per)
            for c in range(1 + 2 * loops, n_chunks):
                chunk(c, per - 1 + (c - 1) * per, 0, 0, 0)
            step(eng, "down", n_chunks - 1, total - 1, n_chunks - 1, total - 1, 0)

        def wait_group(eng, op, c, j):
            sem, n = {"gate": (gate_done, 4), "up": (up_done, 4), "down": (down_done, 16)}[op]
            eng.wait_ge(sem.sem, sem.at(c * n + j + 1))

        def hidden(part, cf, j):
            return hid[part][cf % 2][:, j // 2, halves[j % 2]]

        def act_step(act, op, c, s, cf, sf, it):
            if op == "gate":
                act.wait_ge(hid_ready.sem, hid_ready.at(c * 4))
                for j in range(4):
                    wait_group(act, op, c, j)
                    act.activation(val[:, j], ps[:, j, :], ACT.Silu).then_inc(gate_read.sem, 1)
            if op == "up":
                if not gated:
                    act.wait_ge(hid_ready.sem, hid_ready.at(c * 4))
                    for j in range(4):
                        wait_group(act, op, c, j)
                        act.activation(val[:, j], ps[:, j, :], ACT.Relu).then_inc(relu_done.sem, 1)
                for j in range(4):
                    act.wait_ge(square_done.sem, square_done.at(c * 4 + j + 1))
                    act.activation(hidden(0, cf, j), val[:, j], ACT.Copy).then_inc(hid_hi.sem, 1)
            if sf + base + 2 < n_slabs:
                wait_group(act, op, c, 15 if op == "down" else 3)
                g = base + sf + 2
                split_hi(act, base + 2 + s, it * per + g // 2, g % 2)

        def dve_step(dve, op, c, s, cf, sf, it):
            if op == "up":
                for j in range(4):
                    if gated:
                        dve.wait_ge(gate_read.sem, gate_read.at(c * 4 + j + 1))
                        wait_group(dve, op, c, j)
                        dve.tensor_tensor(val[:, j], ps[:, j, :], val[:, j], ALU.mult).then_inc(square_done.sem, 1)
                    else:
                        dve.wait_ge(relu_done.sem, relu_done.at(c * 4 + j + 1))
                        dve.tensor_tensor(val[:, j], val[:, j], val[:, j], ALU.mult).then_inc(square_done.sem, 1)
                for j in range(4):
                    dve.wait_ge(hid_hi.sem, hid_hi.at(c * 4 + j + 1))
                    dve.tensor_tensor(hidden(1, cf, j), val[:, j], hidden(0, cf, j).bitcast(F32), ALU.subtract)\
                       .then_inc(hid_ready.sem, 1)
            if op == "down":
                for j in range(16):
                    wait_group(dve, op, c, j)
                    t = xr[:, j // 2, halves[j % 2]]
                    dve.tensor_tensor(t, ps[:, 4 + j % 4, :], t, ALU.add).then_inc(bank_free.sem, 1)

        def pe_step(pe, op, c, s, cf, sf, it):
            slot = (base + sf) % 2
            pe.wait_ge(slab_split.sem, base + 1 + s)
            if op != "down":
                done = gate_done if op == "gate" else up_done
                for j in range(4):
                    if op == "up" and gated:
                        pe.wait_ge(gate_read.sem, gate_read.at(c * 4 + j + 1))
                    elif cf > 0:
                        last = square_done if gated else relu_done
                        pe.wait_ge(last.sem, last.at(c * 4 + j - 3))
                    m, hf = j // 2, j % 2
                    for i, (wp, ap) in enumerate(((0, 0), (0, 1), (1, 0))):
                        for k in range(KT):
                            mm = pe.matmul(ps[:, j, :], slab_of(wp, slot)[:, k * CB + m * P:k * CB + (m + 1) * P],
                                           h[ap][:, k, halves[hf]],
                                           start=(i == 0 and k == 0), stop=(i == 2 and k == KT - 1))
                    mm.then_inc(done.sem, 1)
            else:
                pe.wait_ge(hid_ready.sem, hid_ready.at(c * 4 + 4))
                for j in range(16):
                    pe.wait_ge(bank_free.sem, bank_free.at(c * 16 + j - 3))
                    m, hf = j // 2, j % 2
                    for i, (wp, ap) in enumerate(((0, 0), (0, 1), (1, 0))):
                        for k in range(2):
                            mm = pe.matmul(ps[:, 4 + j % 4, :], slab_of(wp, slot)[:, k * D + m * P:k * D + (m + 1) * P],
                                           hid[ap][cf % 2][:, k, halves[hf]],
                                           start=(i == 0 and k == 0), stop=(i == 2 and k == 1))
                    mm.then_inc(down_done.sem, 1)

        def pool_step(pool, op, c, s, cf, sf, it):
            if sf + base + 2 < n_slabs:
                split_lo(pool, base + 2 + s, (base + sf) % 2)

        def sync_step(sp, op, c, s, cf, sf, it):
            if sf + base + 4 < n_slabs:
                load_slab(sp, base + 4 + s, (base + sf) % 2)

        with nc.Block() as block:
            for eng, step in ((block.scalar, act_step), (block.vector, dve_step), (block.tensor, pe_step),
                              (block.gpsimd, pool_step), (block.sync, sync_step)):
                eng(lambda x, step=step: sequence(x, step))
        for c, n in ((gate_done, 4 if gated else 0), (gate_read, 4 if gated else 0), (up_done, 4), (down_done, 16),
                     (relu_done, 0 if gated else 4), (square_done, 4), (hid_hi, 4), (hid_ready, 4), (bank_free, 16)):
            c.advance(n * n_chunks)
        slab_at[0] += total
        st.close()

    def normed(gain, name):
        st = scope()
        h = (sb(st, name + "_hi", [P, KT, SEQ], F32R), sb(st, name + "_lo", [P, KT, SEQ], F32R))
        t = scope()
        rms_norm(xr, gain, sb(t, name + "_tmp", [P, 5, HALF]), h)
        t.close()
        return st, h

    st, h = normed(param("norm_ffn"), "h3")
    mlp(h, FF1_CHUNKS, False, "ff1")
    st.close()

    st = scope()
    rms_norm(xr, param("norm_final"), sb(st, "final_tmp", [P, 5, HALF]), xr)
    st.close()
    m2 = scope()
    mix = sb(m2, "mix2", [P, 13, SEQ])
    zq, zk, c_a, c_g = mix[:, 0:2], mix[:, 2:4], mix[:, 6:8], mix[:, 8:10]
    zv = mix[:, 4:6].rearrange("p a n -> p (a n)").rearrange("p (t c) -> p t c", t=NB)
    attn_out = c_g
    st = scope()
    h = (sb(st, "h5_hi", [P, KT, SEQ], F32R), sb(st, "h5_lo", [P, KT, SEQ], F32R))
    rms_norm(xr, param("norm1_2"), mix[:, 0:3].rearrange("p a (b n) -> p (a b) n", b=2), h)

    def spill(sp):
        for k in range(KT):
            sp.dma_start(x_spill[:, k, :], xr[:, k, :]).then_inc(stored.sem, 16)

    def spilled(sp):
        sp.wait_ge(stored.sem, stored.at(16 * KT))

    dense(h, 2, to_tiles(mix[:, 0:4], ACT.Copy), before=(spill, None), after=spilled)
    stored.advance(16 * KT)
    dense(h, 1, to_tokens(zv, ACT.Copy), token_major=True)
    dense(h, 2, to_tiles(mix[:, 6:10], ACT.Copy))
    dense(h, 4, to_tiles(xr, ACT.Copy))
    st.close()
    s_b, s_c, s_h = xr[:, 2:4], xr[:, 4:6], xr[:, 6:8]

    st = scope()
    tmp = sb(st, "m2_tmp", [P, 6, SEQ])
    edge = sb(st, "edge", [P, 2, 16])
    pw = sb(st, "pw", [P, 2, P])
    with nc.Block() as block:
        @block.sync
        def _(sp):
            sp.dma_start(edge[:].rearrange("p a n -> p (a n)"), const("pool_edge")).then_inc(loaded.sem, 16)
            sp.dma_start(pw[:].rearrange("p a n -> p (a n)"), pool_w).then_inc(loaded.sem, 16)
            sp.wait_ge(loaded.sem, loaded.at(32))

        @block.scalar
        def _(act):
            act.activation(c_g, c_g, ACT.Sigmoid).then_inc(a_step.sem, 1)
            for t in range(2):
                for hf in range(2):
                    act.wait_ge(p_step.sem, p_step.at(2 * t + hf + 1))
                    act.activation(xr[:, t, halves[hf]], ps[:, 2 * t + hf, :], ACT.Copy,
                                   scale=param("pool_scale")[:, t:t + 1])

        @block.gpsimd
        def _(pool):
            pool.tensor_tensor(s_c, s_c, s_h, ALU.mult)
            pool.wait_ge(a_step.sem, a_step.at(1))
            pool.tensor_tensor(c_a, c_a, c_g, ALU.mult)

        @block.vector
        def _(dve):
            n = [0]

            def then(ins):
                n[0] += 1
                ins.then_inc(v_step.sem, 1)
                dve.wait_ge(v_step.sem, v_step.at(n[0]))

            dve.wait_ge(loaded.sem, loaded.at(32))
            for t in range(2):
                u = xr[:, t]
                src, bufs = u, [tmp[:, 0], tmp[:, 1]]
                for d in range(4 if t else 2):
                    w, o = 2 ** d, bufs[d % 2]
                    then(dve.tensor_copy(o[:, 0:w], src[:, 0:w]))
                    then(dve.tensor_tensor(o[:, w:SEQ], src[:, w:SEQ], src[:, 0:SEQ - w], ALU.add))
                    src = o
                for half in range(2):
                    c = slice(64 * half, 64 * half + 64)
                    s = bufs[half]
                    then(dve.scalar_tensor_tensor(out=tmp[c, 2 + t, :], in0=s[c], scalar=edge[c, t, 15:16], in1=u[c],
                                                  op0=ALU.mult, op1=ALU.subtract))
                    then(dve.tensor_tensor(s[c, 0:16], s[c, 0:16], edge[c, t, :], ALU.mult))
                    then(dve.tensor_tensor(tmp[c, 2 + t, 0:16], s[c, 0:16], u[c, 0:16], ALU.subtract))

        @block.tensor
        def _(pe):
            for t in range(2):
                pe.wait_ge(v_step.sem, v_step.at(10 if t == 0 else 24))
                for hf in range(2):
                    pe.matmul(ps[:, 2 * t + hf, :], pw[:, t, :], tmp[:, 2 + t, halves[hf]], start=True, stop=True)\
                      .then_inc(p_step.sem, 1)
    loaded.advance(32)
    a_step.advance(1)
    v_step.advance(24)
    p_step.advance(4)
    conv(s_c, 2, param("sconv_w"), 3, tmp[:, 0:2], ACT.Copy)
    conv(c_a, 2, param("conf_dw_w"), CONF_K, tmp[:, 0:2], ACT.Identity, bias=param("conf_dw_b"))

    with nc.Block() as block:
        @block.gpsimd
        def _(pool):
            for hf in range(2):
                for t in range(2):
                    pool.wait_ge(v_step.sem, v_step.at(4 * hf + t + 1))
                    pool.tensor_tensor(tmp[:, t, halves[hf]], c_a[:, t, halves[hf]], c_a[:, t, halves[hf]],
                                       ALU.mult).then_inc(g_step.sem, 1)
            pool.tensor_tensor(s_c, s_c, s_b, ALU.mult)

        @block.tensor
        def _(pe):
            for hf in range(2):
                for t in range(2):
                    mm = pe.matmul(ps[:, hf, :], ones[:], c_a[:, t, halves[hf]], start=(t == 0), stop=(t == 1))
                mm.then_inc(p_step.sem, 1)
            for hf in range(2):
                for t in range(2):
                    pe.wait_ge(g_step.sem, g_step.at(2 * hf + t + 1))
                    mm = pe.matmul(ps[:, 2 + hf, :], ones[:], tmp[:, t, halves[hf]], start=(t == 0), stop=(t == 1))
                mm.then_inc(p_step.sem, 1)

        @block.vector
        def _(dve):
            for hf in range(2):
                dve.wait_ge(p_step.sem, p_step.at(hf + 1))
                for t in range(2):
                    dve.scalar_tensor_tensor(out=c_a[:, t, halves[hf]], in0=ps[:, hf, :], scalar=-1.0 / 256,
                                             in1=c_a[:, t, halves[hf]], op0=ALU.mult, op1=ALU.add)\
                       .then_inc(v_step.sem, 1)
                dve.wait_ge(rstd_done.sem, rstd_done.at(hf + 1))
                for t in range(2):
                    dve.scalar_tensor_tensor(out=c_a[:, t, halves[hf]], in0=c_a[:, t, halves[hf]],
                                             scalar=param("conf_ln_g")[:, t:t + 1], in1=tmp[:, 2, halves[hf]],
                                             op0=ALU.mult, op1=ALU.mult).then_inc(v_step.sem, 1)

        @block.scalar
        def _(act):
            for hf in range(2):
                r = tmp[:, 2, halves[hf]]
                act.wait_ge(p_step.sem, p_step.at(3 + hf))
                act.activation(r, ps[:, 2 + hf, :], ACT.Ln, scale=1.0 / 256, bias=eps_col).then_inc(log_done.sem, 1)
                act.wait_ge(log_done.sem, log_done.at(hf + 1))
                act.activation(r, r, ACT.Exp, scale=-0.5).then_inc(rstd_done.sem, 1)
            for hf in range(2):
                act.wait_ge(v_step.sem, v_step.at(4 * hf + 4))
                for t in range(2):
                    z = c_a[:, t, halves[hf]]
                    act.activation(z, z, ACT.Silu, bias=param("conf_ln_b")[:, t:t + 1])
    g_step.advance(4)
    p_step.advance(4)
    v_step.advance(8)
    log_done.advance(2)
    rstd_done.advance(2)
    st.close()

    st = scope()
    tmp = sb(st, "at_tmp", [P, 2, SEQ])
    causal = sb(st, "causal", [P, P])
    hot = sb(st, "hot", [P, 384])
    rel = sb(st, "rel", [P, HEADS, P])
    table = sb(st, "table", [P, HEADS, 400])
    bias = sb(st, "bias", [P, HEADS, 256])
    ones32 = sb(st, "ones32", [P, P])
    ones64 = sb(st, "ones64", [P, P])
    lam = sb(st, "lam", [P, 80])
    neg_lam, q_gain, o_gain = lam[:, 70:71], lam[:, 71:72], lam[:, 72:73]
    with nc.Block() as block:
        @block.sync
        def _(sp):
            for dst, name in ((causal, "causal"), (hot, "onehot"), (ones32, "ones32"), (ones64, "ones64")):
                sp.dma_start(dst[:], const(name)).then_inc(loaded.sem, 16)
            sp.wait_ge(v_step.sem, v_step.at(3))
            sp.dma_start(bias_skew.rearrange("h p n -> p h n"), table[:]).then_inc(stored.sem, 16)
            sp.wait_ge(stored.sem, stored.at(16))
            for hd in range(HEADS):
                skewed = bias_skew[hd].rearrange("p n -> (p n)")[127:127 + P * 399]\
                    .rearrange("(p n) -> p n", n=399)[:, 0:256]
                sp.dma_start(bias[:, hd, :], skewed).then_inc(loaded.sem, 16)
            sp.wait_ge(loaded.sem, loaded.at(16 * 8))

        @block.vector
        def _(dve):
            lam_v = param("lam").rearrange("p (a b n) -> p a b n", a=2, b=2)
            prod = lam[:, 0:64].rearrange("p (a n) -> p a n", a=2)
            dve.memset(table[:], 0.0).then_inc(v_step.sem, 1)
            dve.wait_ge(v_step.sem, v_step.at(1))
            dve.tensor_copy(rel[0:32], param("rel_bias")[0:32].unsqueeze(2).to_broadcast([32, HEADS, P]))\
               .then_inc(v_step.sem, 1)
            for hd in range(HEADS):
                dve.wait_ge(p_step.sem, p_step.at(hd + 1))
                dve.tensor_copy(lam[:, 74 + hd:75 + hd], ps[:, hd, 0:1]).then_inc(value_done.sem, 1)
                dve.wait_ge(value_done.sem, value_done.at(hd + 1))
                last = dve.tensor_scalar(table[:, hd, 0:384], ps[:, hd, 0:384], lam[:, 74 + hd:75 + hd], None,
                                         ALU.subtract)
            last.then_inc(v_step.sem, 1)
            dve.tensor_tensor(prod, lam_v[:, :, 0], lam_v[:, :, 1], ALU.mult).then_inc(v_step.sem, 1)
            dve.wait_ge(v_step.sem, v_step.at(4))
            dve.tensor_reduce(lam[:, 64:66], prod, AX.X, ALU.add).then_inc(v_step.sem, 1)
            dve.tensor_scalar(q_gain, param("q_norm"), QK2 ** -0.5, None, ALU.mult)
            dve.tensor_scalar(o_gain, param("subln"), 1.0 - LAM_INIT, None, ALU.mult)
            dve.wait_ge(a_step.sem, a_step.at(1))
            dve.tensor_tensor(lam[:, 68:69], lam[:, 67:68], lam[:, 66:67], ALU.subtract).then_inc(v_step.sem, 1)
            dve.wait_ge(v_step.sem, v_step.at(6))
            dve.tensor_scalar(neg_lam, lam[:, 68:69], -LAM_INIT, None, ALU.add)
            dve.wait_ge(loaded.sem, loaded.at(16 * 8))
            d = bias[:, :, P:2 * P]
            dve.tensor_tensor(d, d, causal[:].unsqueeze(1).to_broadcast([P, HEADS, P]), ALU.add)

        @block.scalar
        def _(act):
            act.wait_ge(v_step.sem, v_step.at(5))
            act.activation(lam[:, 66:68], lam[:, 64:66], ACT.Exp).then_inc(a_step.sem, 1)

        @block.tensor
        def _(pe):
            pe.wait_ge(loaded.sem, loaded.at(64))
            pe.wait_ge(v_step.sem, v_step.at(2))
            for hd in range(HEADS):
                pe.matmul(ps[:, hd, 0:384], rel[0:32, hd, :], hot[0:32, :], start=True, stop=True)\
                  .then_inc(p_step.sem, 1)
    loaded.advance(16 * 8)
    stored.advance(16)
    v_step.advance(6)
    value_done.advance(4)
    a_step.advance(1)
    p_step.advance(4)
    norm_units([dict(src=z[:, t, c], out=z[:, t, c], scale=1.0 / QK2, gain=g)
                for z, g in ((zq, q_gain), (zk, param("k_norm"))) for t in range(2) for c in halves],
               ones32[:], tmp)

    q_p = sb(st, "q_p", [P, SEQ])
    k_p = sb(st, "k_p", [P, SEQ])
    v_p = sb(st, "v_p", [P, NB, P])
    bias_p = sb(st, "bias_p", [P, 2, 256])
    prob = [sb(st, f"diff_prob{b}", [P, 2, SEQ]) for b in range(2)]
    a_t = sb(st, "a_t", [P, 2, NB, P])
    stat = sb(st, "diff_stat", [P, 2, 2, 4])
    units = [(hd, qb) for hd in range(2) for qb in range(NB)]
    NU = len(units)
    turn_groups = [(qb + 4) // 4 for _, qb in units]
    turns_before = [sum(turn_groups[:u]) for u in range(NU + 1)]
    NT = turns_before[-1]
    with nc.Block() as block:
        @block.sync
        def _(sp):
            with sp.Fori(0, 2) as it:
                sp.wait_ge(d_stored.sem, d_stored.at(it * NU))
                for dst, src in ((q_p[:], zq[:, bass.ds(it, 1), :].rearrange("p o n -> p (o n)")),
                                 (k_p[:], zk[:, bass.ds(it, 1), :].rearrange("p o n -> p (o n)")),
                                 (v_p[:], zv[:, :, bass.ds(it * P, P)]),
                                 (bias_p[:], bias[:, bass.ds(it * 2, 2), :])):
                    sp.dma_start(dst, src).then_inc(pair_loaded.sem, 16)

        @block.tensor
        def _(pe):
            with pe.Fori(0, 2) as it:
                pe.wait_ge(pair_loaded.sem, pair_loaded.at(it * 64 + 64))

                def scores(u):
                    hd, qb = units[u]
                    w = (qb + 1) * P
                    for m in range(2):
                        pe.wait_ge(d_exp.sem, d_exp.at(it * 2 * NU + (2 * (u - 1) + m + 1 if u else 0)))
                        r = slice(64 * hd + 32 * m, 64 * hd + 32 * m + 32)
                        for a in range(0, w, HALF):
                            b = min(w, a + HALF)
                            mm = pe.matmul(ps[:, 2 * m + a // HALF, 0:b - a], q_p[r, qb * P:(qb + 1) * P],
                                           k_p[r, a:b], start=True, stop=True)
                        mm.then_inc(d_scores.sem, 1)

                scores(0)
                for u, (hd, qb) in enumerate(units):
                    if u + 1 < NU:
                        scores(u + 1)
                    pe.wait_ge(d_diff.sem, d_diff.at(it * NU + u + 1))
                    for a in range(0, qb + 1, 4):
                        n = turns_before[u] + a // 4
                        pe.wait_ge(d_copied.sem, d_copied.at(it * NT + max(n - 1, 0)))
                        for kb in range(a, min(a + 4, qb + 1)):
                            mm = pe.transpose(ps[:, 4 + n % 2, (kb - a) * P:(kb - a + 1) * P],
                                              prob[u % 2][:, 0, kb * P:(kb + 1) * P], ident[:])
                        mm.then_inc(d_turned.sem, 1)
                    pe.wait_ge(d_copied.sem, d_copied.at(it * NT + turns_before[u + 1]))
                    pe.wait_ge(d_stored.sem, d_stored.at(it * NU + max(u - 1, 0)))
                    for kb in range(qb + 1):
                        mm = pe.matmul(ps[64 * hd:64 * hd + 64, 6 + u % 2, 0:P], v_p[:, kb, 64 * hd:64 * hd + 64],
                                       a_t[:, u % 2, kb, :], start=(kb == 0), stop=(kb == qb))
                    mm.then_inc(d_out.sem, 1)

        @block.vector
        def _(dve):
            with dve.Fori(0, 2) as it:
                def soft(u):
                    hd, qb = units[u]
                    w, near = (qb + 1) * P, min(qb + 1, 2) * P
                    for m in range(2):
                        n = it * 2 * NU + 2 * u + m + 1
                        sc = ps[:, 2 * m:2 * m + 2, :].rearrange("p a n -> p (a n)")
                        dve.wait_ge(d_scores.sem, d_scores.at(n))
                        dve.wait_ge(pair_loaded.sem, pair_loaded.at(it * 64 + 64))
                        dve.tensor_tensor(sc[:, w - near:w], sc[:, w - near:w], bias_p[:, hd, 256 - near:256],
                                          ALU.add).then_inc(d_biased.sem, 1)
                        dve.wait_ge(d_biased.sem, d_biased.at(n))
                        dve.tensor_reduce(stat[:, u % 2, m, 0:1], sc[:, 0:w], AX.X, ALU.max, negate=True)\
                           .then_inc(d_max.sem, 1)

                def combine(u):
                    hd, qb = units[u]
                    w = (qb + 1) * P
                    s = stat[:, u % 2]
                    dve.wait_ge(d_exp.sem, d_exp.at(it * 2 * NU + 2 * u + 2))
                    dve.reciprocal(s[:, :, 2:3], s[:, :, 1:2]).then_inc(d_inv.sem, 1)
                    dve.wait_ge(d_inv.sem, d_inv.at(it * NU + u + 1))
                    dve.tensor_scalar(s[:, 1, 3:4], s[:, 1, 2:3], neg_lam, None, ALU.mult).then_inc(d_inv2.sem, 1)
                    dve.wait_ge(d_inv2.sem, d_inv2.at(it * NU + u + 1))
                    dve.tensor_scalar(prob[u % 2][:, 1, 0:w], prob[u % 2][:, 1, 0:w], s[:, 1, 3:4], None, ALU.mult)\
                       .then_inc(d_scaled.sem, 1)
                    dve.wait_ge(d_scaled.sem, d_scaled.at(it * NU + u + 1))
                    dve.scalar_tensor_tensor(out=prob[u % 2][:, 0, 0:w], in0=prob[u % 2][:, 0, 0:w],
                                             scalar=s[:, 0, 2:3], in1=prob[u % 2][:, 1, 0:w],
                                             op0=ALU.mult, op1=ALU.add).then_inc(d_diff.sem, 1)

                def store(u):
                    hd, qb = units[u]
                    r = slice(64 * hd, 64 * hd + 64)
                    dve.wait_ge(d_out.sem, d_out.at(it * NU + u + 1))
                    dve.tensor_copy(attn_out[r, bass.ds(it, 1), qb * P:(qb + 1) * P].rearrange("p o n -> p (o n)"),
                                    ps[r, 6 + u % 2, 0:P]).then_inc(d_stored.sem, 1)

                soft(0)
                for u in range(NU):
                    if u + 1 < NU:
                        soft(u + 1)
                    combine(u)
                    if u:
                        store(u - 1)
                store(NU - 1)

        @block.scalar
        def _(act):
            with act.Fori(0, 2) as it:
                def exps(u):
                    hd, qb = units[u]
                    w = (qb + 1) * P
                    for m in range(2):
                        sc = ps[:, 2 * m:2 * m + 2, :].rearrange("p a n -> p (a n)")
                        act.wait_ge(d_max.sem, d_max.at(it * 2 * NU + 2 * u + m + 1))
                        act.wait_ge(d_turned.sem, d_turned.at(it * NT + (turns_before[u - 1] if u >= 2 else 0)))
                        act.activation(prob[u % 2][:, m, 0:w], sc[:, 0:w], ACT.Exp, bias=stat[:, u % 2, m, 0:1],
                                       accum_out=stat[:, u % 2, m, 1:2]).then_inc(d_exp.sem, 1)

                exps(0)
                for u, (hd, qb) in enumerate(units):
                    if u + 1 < NU:
                        exps(u + 1)
                    act.wait_ge(d_out.sem, d_out.at(it * NU + max(u - 1, 0)))
                    for a in range(0, qb + 1, 4):
                        n = turns_before[u] + a // 4
                        b = min(a + 4, qb + 1)
                        act.wait_ge(d_turned.sem, d_turned.at(it * NT + n + 1))
                        act.activation(a_t[:, u % 2, a:b, :].rearrange("p a n -> p (a n)"),
                                       ps[:, 4 + n % 2, 0:(b - a) * P], ACT.Copy).then_inc(d_copied.sem, 1)
    norm_units([dict(src=attn_out[:, t, c], out=attn_out[:, t, c], scale=1.0 / HV2, gain=o_gain)
                for t in range(2) for c in halves], ones64[:], tmp, wide=True)
    st.close()

    y_stack = scope()
    y = (sb(y_stack, "y3_hi", [P, KT, SEQ], F32R), sb(y_stack, "y3_lo", [P, KT, SEQ], F32R))
    parts = [xr[:, 0], xr[:, 1], s_c[:, 0], s_c[:, 1], c_a[:, 0], c_a[:, 1], attn_out[:, 0], attn_out[:, 1]]
    split_tiles([(z[:, c], y[0][:, t, c], y[1][:, t, c]) for t, z in enumerate(parts) for c in halves])
    dense(y, 4, add_residual, engine="dve", before=reload_x(x_spill))
    loaded.advance(16 * KT)
    y_stack.close()
    m2.close()

    st, h = normed(param("norm2_2"), "h6")
    mlp(h, FF2_CHUNKS, True, "ff2")
    st.close()
    with nc.Block() as block:
        @block.sync
        def _(sp):
            for k in range(KT):
                sp.dma_start(out_t[:, k, :], xr[:, k, :]).then_inc(stored.sem, 16)
            sp.wait_ge(stored.sem, stored.at(16 * KT))


def slab_up(w, c):
    return w[:, c:c + CB].reshape(KT, P, CB).transpose(1, 0, 2).reshape(P, SLAB)


def slab_down(w, r):
    return w[r:r + CB].reshape(2, P, D).transpose(1, 0, 2).reshape(P, SLAB)


def feature_columns(v, n):
    return np.reshape(v, (n, P)).T


def lay_out(a):
    a = {k: np.asarray(v) for k, v in a.items()}
    m = {k: (v[0] if v.ndim > 1 and v.shape[0] == 1 else v) for k, v in a.items()}

    def ups(w, c0=0, c1=None):
        return [slab_up(w, c) for c in range(c0, w.shape[1] if c1 is None else c1, CB)]

    slabs = ups(m["w_in"], 0, 3072)
    for name in ("w_out", "xa_wk", "xa_wv", "xa_wq", "xa_wo"):
        slabs += ups(m[name])
    up, down = ups(m["ffn_w1"]), [slab_down(m["ffn_w2"], r) for r in range(0, 4096, CB)]
    slabs.append(up[0])
    for c in range(1, FF1_CHUNKS):
        slabs += [up[c], down[c - 1]]
    slabs.append(down[-1])
    pool, s_b, s_c, s_h, c_a, c_g, zq, zk, zv = ups(m["w_in_2"])
    slabs += [zq, zk, zv, c_a, c_g, pool, s_b, s_c, s_h] + ups(m["w_out_2"])
    gate, up = ups(m["w_gate_2"]), ups(m["w_up_2"])
    down = [slab_down(m["w_down_2"], r) for r in range(0, 2816, CB)]
    slabs += [gate[0], up[0]]
    for c in range(1, FF2_CHUNKS):
        slabs += [gate[c], up[c], down[c - 1]]
    slabs.append(down[-1])

    params = np.zeros((P, N_PARAMS), np.float32)

    def put(name, v):
        lo, hi = PARAM_COLS[name]
        params[:v.shape[0], lo:hi] = v

    for name, src in (("norm_mix", "norm_mix"), ("norm_xa", "norm_xa"), ("norm_mem", "norm_mem"),
                      ("norm_ffn", "norm_ffn"), ("norm_final", "norm_final"), ("norm1_2", "norm1_g_2"),
                      ("norm2_2", "norm2_g_2")):
        put(name, feature_columns(m[src], 8))
    put("gm_ln_g", m["gm_ln_g"].T)
    put("dn_conv", m["dn_conv"].reshape(CONV_W, 12, P).transpose(2, 1, 0).reshape(P, 48))
    put("dn_a_log", np.tile(np.reshape(m["dn_a_log"], (1, 4)), (P, 1)))
    put("dn_dt_bias", np.tile(np.reshape(m["dn_dt_bias"], (1, 4)), (P, 1)))
    put("dn_onorm", np.reshape(m["dn_onorm"], (P, 1)))
    put("w_logits", m["w_in"][:, 3072:3080].reshape(KT, P, 8).transpose(1, 0, 2).reshape(P, 64))
    put("pool_scale", feature_columns(m["pool_scale_2"], 2))
    put("sconv_w", m["sconv_w_2"].reshape(3, 2, P).transpose(2, 1, 0).reshape(P, 6))
    put("conf_dw_w", m["conf_dw_w_2"].reshape(CONF_K, 2, P).transpose(2, 1, 0).reshape(P, 62))
    put("conf_dw_b", feature_columns(m["conf_dw_b_2"], 2))
    put("conf_ln_g", feature_columns(m["conf_ln_g_2"], 2))
    put("conf_ln_b", feature_columns(m["conf_ln_b_2"], 2))
    put("q_norm", np.tile(np.reshape(m["q_norm_g_2"], (QK2, 1)), (4, 1)))
    put("k_norm", np.tile(np.reshape(m["k_norm_g_2"], (QK2, 1)), (4, 1)))
    put("subln", np.tile(np.reshape(m["subln_g_2"], (HV2, 1)), (2, 1)))
    put("lam", np.tile(np.concatenate([np.reshape(m[n], (1, QK2)) for n in
                                       ("lam_q1_2", "lam_k1_2", "lam_q2_2", "lam_k2_2")], 1), (P, 1)))
    put("rel_bias", m["rel_bias_2"])

    pool_w = np.zeros((P, 2, P), np.float32)
    for g in range(4):
        o = (g % 2) * 64
        pool_w[o:o + 64, g // 2, o:o + 64] = m["pool_w_2"][g]
    return {
        "x_t": m["x"].T.reshape(KT, P, SEQ).transpose(1, 0, 2),
        "mem_t": m["mem"].T.reshape(KT, P, MEM).transpose(1, 0, 2),
        "slabs": np.stack(slabs),
        "params": params,
        "row_params": np.concatenate([m["gm_ln_b"].reshape(1, 512), m["gm_bs"].reshape(1, 512)], 1),
        "gm_ws_t": m["gm_ws"].transpose(2, 0, 1).reshape(P, 512),
        "pool_w": pool_w.reshape(P, 2 * P),
        "consts": constant_tables(),
    }


def kernel(**inputs):
    import concourse.bacc as bacc
    from concourse.bass_utils import run_bass_kernel_spmd

    arrays = {f"in_{k}_dram": np.ascontiguousarray(v) for k, v in lay_out(inputs).items()}
    nc = bacc.Bacc("TRN2", target_bir_lowering=False, num_devices=1)
    ins = {k[3:-5]: nc.dram_tensor(k, v.shape, F32, kind="ExternalInput").ap() for k, v in arrays.items()}
    out_t = nc.dram_tensor("out_0_dram", (P, KT, SEQ), F32, kind="ExternalOutput").ap()
    x_spill = nc.dram_tensor("x_spill", (P, KT, SEQ), F32, kind="Internal").ap()
    bias_skew = nc.dram_tensor("bias_skew", (HEADS, P, 400), F32, kind="Internal").ap()
    with ExitStack() as main:
        build(nc, main, **ins, x_spill=x_spill, bias_skew=bias_skew, out_t=out_t)
    r = run_bass_kernel_spmd(nc, [arrays], core_ids=[0])
    return np.ascontiguousarray(r.results[0]["out_0_dram"].transpose(2, 1, 0).reshape(1, SEQ, D))
```

```python
from contextlib import ExitStack

import numpy as np

import concourse.bass as bass
from concourse import mybir

F32 = mybir.dt.float32
F32R = mybir.dt.float32r
ALU = mybir.AluOpType
ACT = mybir.ActivationFunctionType
AX = mybir.AxisListType

P = 128
D = 1024
KT = D // P
SEQ = 1024
HALF = 512
NB = SEQ // P
MEM = 256
EPS = 1e-6
CB = 256
SLAB = KT * CB
HEADS = 4
CONV_W = 4
FF1_CHUNKS = 4096 // CB
FF2_CHUNKS = 2816 // CB
XA_D = 256
LAM_INIT = 0.2
POOL_WINDOWS = (2, 4, 8, 16)
CONF_K = 31
QK2 = 32
HV2 = 64

PARAM_COLS = {}
_at = 0
for _name, _n in [("norm_mix", 8), ("norm_xa", 8), ("norm_mem", 8), ("norm_ffn", 8), ("norm_final", 8),
                  ("norm1_2", 8), ("norm2_2", 8), ("gm_ln_g", 4), ("dn_conv", 48), ("dn_a_log", 4),
                  ("dn_dt_bias", 4), ("dn_onorm", 1), ("w_logits", 64), ("pool_scale", 2), ("sconv_w", 6),
                  ("conf_dw_w", 62), ("conf_dw_b", 2), ("conf_ln_g", 2), ("conf_ln_b", 2), ("q_norm", 1),
                  ("k_norm", 1), ("subln", 1), ("lam", 128), ("rel_bias", 4)]:
    PARAM_COLS[_name] = (_at, _at + _n)
    _at += _n
N_PARAMS = _at

CONST_COLS = {}
_at = 0
for _name, _n in [("ident", 128), ("tri", 128), ("strict", 128), ("levels", 7 * 128), ("ones32", 128),
                  ("ones64", 128), ("pool_edge", 32), ("onehot", 384), ("causal", 128)]:
    CONST_COLS[_name] = (_at, _at + _n)
    _at += _n
N_CONSTS = _at


def constant_tables():
    c = np.zeros((P, N_CONSTS), np.float32)
    i = np.arange(P)

    def put(name, a):
        lo, hi = CONST_COLS[name]
        c[:a.shape[0], lo:hi] = a

    put("ident", np.eye(P))
    put("tri", (i[:, None] <= i[None, :]) * 1.0)
    put("strict", (i[:, None] < i[None, :]) * 1.0)
    lev = [((i[None, :] >> (l + 1)) == (i[:, None] >> (l + 1))) & ((i[None, :] >> l & 1) == 1)
           & ((i[:, None] >> l & 1) == 0) for l in range(7)]
    put("levels", np.stack(lev, 1).reshape(P, 7 * P) * 1.0)
    put("ones32", (i[:, None] // 32 == i[None, :] // 32) * 1.0)
    put("ones64", (i[:, None] // 64 == i[None, :] // 64) * 1.0)
    edge = np.zeros((P, 2, 16))
    for g, win in enumerate(POOL_WINDOWS):
        for t in range(16):
            edge[(g % 2) * 64:(g % 2) * 64 + 64, g // 2, t] = 1.0 / min(t + 1, win)
    put("pool_edge", edge.reshape(P, 32))
    n = np.maximum(255 - np.arange(384), 0)
    large = 16 + (np.log(np.maximum(n, 1).astype(np.float32) / np.float32(16)) / np.float32(np.log(8.0))
                  * np.float32(16)).astype(np.int32)
    bucket = np.where(n < 16, n, np.minimum(large, 31))
    put("onehot", (np.arange(32)[:, None] == bucket[None, :]) * 1.0)
    put("causal", np.where(i[:, None] >= i[None, :], 0.0, -1e30))
    return c


class Count:

    def __init__(self, sem, base=0):
        self.sem, self.base = sem, base

    def at(self, n):
        return self.base + n

    def advance(self, n):
        self.base += n


def build(nc, main, x_t, mem_t, slabs, params, row_params, gm_ws_t, pool_w, consts, x_spill, bias_skew, out_t):
    def sb(stack, name, shape, dt=F32):
        return stack.enter_context(nc.sbuf_tensor(name, shape, dt))

    counters = []

    def counter(name, start=1):
        counters.append(Count(main.enter_context(nc.semaphore(name)), start))
        return counters[-1]

    slab_raw = sb(main, "slab_raw", [P, 2, SLAB])
    slab_hi = sb(main, "slab_hi", [P, 2, SLAB], F32R)
    slab_lo = sb(main, "slab_lo", [P, 2, SLAB], F32R)
    ident = sb(main, "ident", [P, P])
    ones = sb(main, "ones", [P, P])
    par = sb(main, "par", [P, N_PARAMS])
    eps_tile = sb(main, "eps_tile", [P, 1])
    eps_col = eps_tile[:]
    xr = sb(main, "xr", [P, KT, SEQ])

    ps = main.enter_context(nc.psum_tensor("ps", [P, 8, HALF], F32))

    def param(name):
        a, b = PARAM_COLS[name]
        return par[:, a:b]

    def const(name):
        a, b = CONST_COLS[name]
        return consts[:, a:b]

    slab_loaded = [counter("slab_loaded0", 0), counter("slab_loaded1", 0)]
    slab_hi_done = counter("slab_hi_done", 0)
    slab_split = counter("slab_split", 0)
    group_done = counter("group_done")
    bank_free = counter("bank_free", 9)
    loaded = counter("loaded", 0)
    stored = counter("stored")
    sq_ready = counter("sq_ready")
    sum_done = counter("sum_done")
    log_done = counter("log_done")
    rstd_done = counter("rstd_done")
    value_done = counter("value_done")
    hi_done = counter("hi_done")
    lo_done = counter("lo_done")
    a_step = counter("a_step")
    v_step = counter("v_step")
    g_step = counter("g_step")
    p_step = counter("p_step")
    def pair(name):
        return [counter(f"{name}{s}") for s in range(2)]

    block_loaded = pair("block_loaded")
    gtri_ready = pair("gtri_ready")
    rows_done = pair("rows_done")
    grams_done = pair("grams_done")
    arg_ready = pair("arg_ready")
    exp_done = pair("exp_done")
    raw_done = pair("raw_done")
    masked = pair("masked")
    turned = pair("turned")
    by_token = pair("by_token")
    level_ready = pair("level_ready")
    tt_ready = pair("tt_ready")
    first_turned = pair("first_turned")
    t_ready = pair("t_ready")
    x_done = pair("x_done")
    x_ready = pair("x_ready")
    prod_done = pair("prod_done")
    ks_done, resid_ready, tr_done, vnew_ready, step_done, state_ready, o_ready = (
        counter(n) for n in
        ("ks_done", "resid_ready", "tr_done", "vnew_ready", "step_done", "state_ready", "o_ready"))
    xa_head_loaded = pair("xa_head_loaded")
    (xa_score_done, xa_max_done, xa_bias_done, xa_exp_done, xa_inv_done, xa_p_ready, xa_pt_done, xa_pt_ready, xa_o_done, xa_o_copied) = (
        counter(n) for n in (
            "xa_score_done", "xa_max_done", "xa_bias_done", "xa_exp_done", "xa_inv_done", "xa_p_ready", "xa_pt_done", "xa_pt_ready", "xa_o_done", "xa_o_copied"))
    (pair_loaded, d_scores, d_biased, d_max, d_exp, d_inv, d_inv2, d_scaled, d_diff, d_turned, d_copied, d_out, d_stored) = (
        counter(n) for n in (
            "pair_loaded", "d_scores", "d_biased", "d_max", "d_exp", "d_inv", "d_inv2", "d_scaled", "d_diff", "d_turned", "d_copied", "d_out", "d_stored"))
    (gate_done, up_done, down_done, gate_read, silu_done, silu_scaled, relu_done, square_done, hid_hi, hid_ready) = (
        counter(n) for n in ("gate_done", "up_done", "down_done", "gate_read", "silu_done", "silu_scaled",
                             "relu_done", "square_done", "hid_hi", "hid_ready"))
    n_slabs = slabs.shape[0]

    def load_slab(sp, g, slot, check=True):
        if check:
            sp.wait_ge(slab_split.sem, g - 1)
        sp.dma_start(slab_raw[:, slot, :], slabs[bass.ds(g, 1)].rearrange("o p n -> p (o n)"))\
          .then_inc(slab_loaded[slot].sem, 16)

    def split_hi(act, g, g_half, slot):
        act.wait_ge(slab_loaded[slot].sem, 16 * g_half + 16)
        act.activation(slab_hi[:, slot, :], slab_raw[:, slot, :], ACT.Copy).then_inc(slab_hi_done.sem, 1)

    def split_lo(pool, g, slot):
        pool.wait_ge(slab_hi_done.sem, g + 1)
        pool.tensor_tensor(slab_lo[:, slot, :], slab_raw[:, slot, :], slab_hi[:, slot, :].bitcast(F32),
                           ALU.subtract).then_inc(slab_split.sem, 1)

    PASSES = ((0, 0), (0, 1), (1, 0))

    def slab_of(part, slot):
        return (slab_hi, slab_lo)[part][:, slot, :]

    starts = [(c, c.base) for c in counters]

    with nc.Block() as block:
        @block.sync
        def _(sp):
            sp.dma_start(ident[:], const("ident")).then_inc(loaded.sem, 16)
            sp.dma_start(par[:], params).then_inc(loaded.sem, 16)
            for k in range(KT):
                sp.dma_start(xr[:, k, :], x_t[:, k, :]).then_inc(loaded.sem, 16)
            for g in range(4):
                load_slab(sp, g, g % 2, check=g >= 2)
            sp.wait_ge(loaded.sem, 16 * (2 + KT))

        @block.scalar
        def _(act):
            for g in range(2):
                split_hi(act, g, 0, g)

        @block.gpsimd
        def _(pool):
            pool.memset(ones[:], 1.0)
            pool.memset(eps_tile[:], EPS)
            for g in range(2):
                split_lo(pool, g, g)

        @block.tensor
        def _(pe):
            for c, start in starts:
                if start:
                    pe.sem_inc(c.sem, start)
    loaded.advance(16 * (2 + KT))

    class Feed:

        def __init__(self, dst, src, gain=None, norm=None, tokens=SEQ):
            self.dst, self.src, self.gain, self.norm, self.tokens = dst, src, gain, norm, tokens
            self.w = min(tokens, HALF)
            self.n_half = tokens // self.w
            self.parts = self.n_half + (1 if norm and norm["rcol"] is not None else 0)

        def act_split(self, act):
            for k in range(KT):
                act.activation(self.dst[0][:, k, :], self.src[k], ACT.Copy,
                               scale=1.0 if self.gain is None else self.gain[:, k:k + 1]).then_inc(hi_done.sem, 1)
            if self.norm:
                self.act_squares(act)

        def act_squares(self, act):
            for k in range(KT):
                if k >= 2:
                    act.wait_ge(value_done.sem, value_done.at(max(k - 2, 1)))
                act.activation(self.norm["squares"][:, k % 2, :], self.src[k], ACT.Square).then_inc(sq_ready.sem, 1)

        def act_root(self, act):
            rstd, rcol = self.norm["rstd"], self.norm["rcol"]
            for hf in range(self.n_half):
                act.wait_ge(sum_done.sem, sum_done.at(hf + 1))
                act.activation(rstd[:, hf * self.w:(hf + 1) * self.w], ps[:, 6 + hf, 0:self.w], ACT.Ln,
                               scale=1.0 / D, bias=eps_col).then_inc(log_done.sem, 1)
            if rcol is not None:
                act.wait_ge(sum_done.sem, sum_done.at(self.parts))
                act.activation(rcol, ps[:, 5, 0:self.tokens // P], ACT.Ln, scale=1.0 / D, bias=eps_col)\
                   .then_inc(log_done.sem, 1)
            act.wait_ge(log_done.sem, log_done.at(self.parts))
            act.activation(rstd, rstd, ACT.Exp, scale=-0.5).then_inc(rstd_done.sem, 1)
            if rcol is not None:
                act.activation(rcol, rcol, ACT.Exp, scale=-0.5).then_inc(rstd_done.sem, 1)

        def dve_split(self, dve):
            for k in range(KT):
                dve.wait_ge(hi_done.sem, hi_done.at(k + 1))
                lo, hi = self.dst[1][:, k, :], self.dst[0][:, k, :].bitcast(F32)
                if self.gain is None:
                    dve.tensor_tensor(lo, self.src[k], hi, ALU.subtract).then_inc(lo_done.sem, 1)
                else:
                    dve.scalar_tensor_tensor(out=lo, in0=self.src[k], scalar=self.gain[:, k:k + 1], in1=hi,
                                             op0=ALU.mult, op1=ALU.subtract).then_inc(lo_done.sem, 1)
            if self.norm:
                self.dve_add_squares(dve)

        def dve_add_squares(self, dve):
            sq, total = self.norm["squares"], self.norm["sum"]
            for k in range(1, KT):
                dve.wait_ge(sq_ready.sem, sq_ready.at(k + 1))
                if k > 1:
                    dve.wait_ge(value_done.sem, value_done.at(k - 1))
                dve.tensor_tensor(total, sq[:, 0, :] if k == 1 else total, sq[:, k % 2, :], ALU.add)\
                   .then_inc(value_done.sem, 1)

        def dve_wait_root(self, dve):
            if self.norm:
                dve.wait_ge(rstd_done.sem, rstd_done.at(1 if self.norm["rcol"] is None else 2))

        def pe_sums(self, pe):
            total = self.norm["sum"]
            pe.wait_ge(value_done.sem, value_done.at(KT - 1))
            for hf in range(self.n_half):
                pe.matmul(ps[:, 6 + hf, 0:self.w], ones[:], total[:, hf * self.w:(hf + 1) * self.w],
                          start=True, stop=True).then_inc(sum_done.sem, 1)
            if self.norm["rcol"] is not None:
                for t in range(self.tokens // P):
                    mm = pe.matmul(ps[:, 5, t:t + 1], total[:, t * P:(t + 1) * P], ones[:, 0:1], start=True, stop=True)
                mm.then_inc(sum_done.sem, 1)

        def pe_wait_sums_read(self, pe):
            if self.norm:
                pe.wait_ge(log_done.sem, log_done.at(self.parts))

        def pe_first(self, pe, slot, outputs, done):
            for i, (wp, ap) in enumerate(((0, 0), (1, 0), (0, 1))):
                for k in range(KT):
                    if i == 0:
                        pe.wait_ge(hi_done.sem, hi_done.at(k + 1))
                    if i == 2:
                        pe.wait_ge(lo_done.sem, lo_done.at(k + 1))
                    for o, m, h in outputs:
                        mm = pe.matmul(o, slab_of(wp, slot)[:, k * CB + m * P:k * CB + (m + 1) * P],
                                       self.dst[ap][:, k, h * self.w:(h + 1) * self.w],
                                       start=(i == 0 and k == 0), stop=(i == 2 and k == KT - 1))
                        if i == 2 and k == KT - 1:
                            mm.then_inc(done.sem, 1)

        def advance(self):
            if self.dst:
                hi_done.advance(KT)
                lo_done.advance(KT)
            if self.norm:
                sq_ready.advance(KT)
                value_done.advance(KT - 1)
                sum_done.advance(self.parts)
                log_done.advance(self.parts)
                rstd_done.advance(1 if self.norm["rcol"] is None else 2)

    slab_at = [0]

    def dense(act_in, segments, feed=None, rstd=None, tokens=SEQ, before=None):
        if feed and feed.norm:
            rstd = (feed.norm["rstd"], feed.norm["rcol"])
        first_slab = slab_at[0]
        plan = []
        at, done = first_slab, 0
        for seg in segments:
            token_major = seg.get("token_major", False)
            w = CB if token_major else min(tokens, HALF)
            groups = [(t, None) for t in range(tokens // P)] if token_major else \
                     [(m, h) for m in range(2) for h in range(tokens // w)]
            plan.append(dict(seg, base=at, done=done, w=w, groups=groups, token_major=token_major))
            at, done = at + seg["n"], done + seg["n"] * len(groups)
        n_all = at - first_slab
        depth = 8 if tokens == SEQ else 4

        def passes(step):
            def run(eng):
                for p in plan:
                    n = p["n"]
                    head = min(n, 2) if p is plan[0] else 0
                    for s in range(head):
                        step(eng, p, s, s // 2, s % 2)
                    loops = (n - head) // 2
                    if loops:
                        with eng.Fori(0, loops) as it:
                            for parity in range(2):
                                step(eng, p, it * 2 + (head + parity), it + head // 2, parity)
                    if (n - head) % 2:
                        step(eng, p, n - 1, (n - 1) // 2, (n - 1) % 2)
            return run

        def slot_of(p, parity):
            return (p["base"] + parity) % 2

        def bank(p, parity, j):
            return (p["done"] + parity * len(p["groups"]) + j) % depth

        def count(p, s, j):
            return s * len(p["groups"]) + (p["done"] + j + 1)

        def destination(p, s, j):
            a, h = p["groups"][j]
            if p["token_major"]:
                return p["dst"][:, a, bass.ds(s * CB, CB)]
            return p["dst"][:, bass.ds(s * 2 + a, 1), h * p["w"]:(h + 1) * p["w"]].rearrange("p o n -> p (o n)")

        def is_first(p, s):
            return feed and p is plan[0] and isinstance(s, int) and s == 0

        def sync_step(sp, p, s, pair, parity):
            load_slab(sp, s + (p["base"] + 4), slot_of(p, parity))

        def act_step(act, p, s, pair, parity):
            if is_first(p, s):
                feed.act_split(act)
                if feed.norm:
                    feed.act_root(act)
            G = len(p["groups"])
            if p.get("func"):
                for j in range(G):
                    act.wait_ge(bank_free.sem, bank_free.at(count(p, s, j)))
                    o = destination(p, s, j)
                    act.activation(o, o, p["func"])
            act.wait_ge(group_done.sem, group_done.at(count(p, s, G - 1)))
            split_hi(act, s + (p["base"] + 2), pair + (p["base"] + parity + 2) // 2, slot_of(p, parity))

        def dve_step(dve, p, s, pair, parity):
            if is_first(p, s):
                feed.dve_split(dve)
                feed.dve_wait_root(dve)
            if p.get("wait") and (not isinstance(s, int) or s == 0) and parity == 0:
                p["wait"](dve)
            for j, (a, h) in enumerate(p["groups"]):
                dve.wait_ge(group_done.sem, group_done.at(count(p, s, j)))
                o, psum = destination(p, s, j), ps[:, bank(p, parity, j), 0:p["w"]]
                if p.get("add"):
                    ins = dve.tensor_tensor(o, psum, o, ALU.add)
                elif p["token_major"]:
                    ins = dve.tensor_scalar(o, psum, rstd[1][:, a:a + 1], None, ALU.mult)
                else:
                    ins = dve.tensor_tensor(o, psum, rstd[0][:, h * p["w"]:(h + 1) * p["w"]], ALU.mult)
                ins.then_inc(bank_free.sem, 1)

        def pool_step(pool, p, s, pair, parity):
            split_lo(pool, s + (p["base"] + 2), slot_of(p, parity))

        def pe_step(pe, p, s, pair, parity):
            slot, w = slot_of(p, parity), p["w"]
            pe.wait_ge(slab_split.sem, s + (p["base"] + 1))
            if is_first(p, s):
                feed.pe_first(pe, slot, [(ps[:, bank(p, 0, j), 0:w], m, h) for j, (m, h) in enumerate(p["groups"])],
                              group_done)
                if feed.norm:
                    feed.pe_sums(pe)
                return
            for j, (a, h) in enumerate(p["groups"]):
                if feed and p is plan[0] and isinstance(s, int) and s == 1 and j == 1:
                    feed.pe_wait_sums_read(pe)
                pe.wait_ge(bank_free.sem, bank_free.at(count(p, s, j) - depth))
                o = ps[:, bank(p, parity, j), 0:w]
                for i, (wp, ap) in enumerate(PASSES):
                    for k in range(KT):
                        flags = dict(start=(i == 0 and k == 0), stop=(i == 2 and k == KT - 1))
                        if p["token_major"]:
                            mm = pe.matmul(o, act_in[ap][:, k, a * P:(a + 1) * P],
                                           slab_of(wp, slot)[:, k * CB:(k + 1) * CB], **flags)
                        else:
                            mm = pe.matmul(o, slab_of(wp, slot)[:, k * CB + a * P:k * CB + (a + 1) * P],
                                           act_in[ap][:, k, h * w:(h + 1) * w], **flags)
                mm.then_inc(group_done.sem, 1)

        with nc.Block() as block:
            @block.sync
            def _(sp):
                if before:
                    before(sp)
                passes(sync_step)(sp)

            block.scalar(passes(act_step))
            block.vector(passes(dve_step))
            block.gpsimd(passes(pool_step))
            block.tensor(passes(pe_step))
        group_done.advance(done)
        bank_free.advance(done)
        if feed:
            feed.advance()
        slab_at[0] += n_all

    def norm_units(units, block_ones, tmp, wide=False):
        sq = [tmp[:, 0, 0:HALF], tmp[:, 0, HALF:SEQ]]
        root = [tmp[:, 1, 0:HALF], tmp[:, 1, HALF:SEQ]]
        with nc.Block() as block:
            @block.gpsimd
            def _(pool):
                for n, u in enumerate(units):
                    if n >= 2:
                        pool.wait_ge(p_step.sem, p_step.at(n - 1))
                    pool.tensor_tensor(sq[n % 2], u["src"], u["src"], ALU.mult).then_inc(g_step.sem, 1)

            @block.tensor
            def _(pe):
                for n, u in enumerate(units):
                    pe.wait_ge(g_step.sem, g_step.at(n + 1))
                    if n >= 2:
                        pe.wait_ge(log_done.sem, log_done.at(n - 1))
                    pe.matmul(ps[:, n % 2, :], block_ones, sq[n % 2], start=True, stop=True)\
                      .then_inc(p_step.sem, 1)

            @block.scalar
            def _(act):
                for n, u in enumerate(units):
                    act.wait_ge(p_step.sem, p_step.at(n + 1))
                    if n >= 2:
                        act.wait_ge(v_step.sem, v_step.at(n - 1))
                    act.activation(root[n % 2], ps[:, n % 2, :], ACT.Sqrt if wide else ACT.Ln, scale=u["scale"],
                                   bias=eps_col).then_inc(log_done.sem, 1)
                    if wide:
                        continue
                    act.wait_ge(log_done.sem, log_done.at(n + 1))
                    act.activation(root[n % 2], root[n % 2], ACT.Exp, scale=-0.5).then_inc(rstd_done.sem, 1)

            @block.vector
            def _(dve):
                for n, u in enumerate(units):
                    if wide:
                        dve.wait_ge(log_done.sem, log_done.at(n + 1))
                        dve.reciprocal(root[n % 2], root[n % 2]).then_inc(rstd_done.sem, 1)
                    dve.wait_ge(rstd_done.sem, rstd_done.at(n + 1))
                    if "times" in u:
                        dve.tensor_tensor(root[n % 2], root[n % 2], u["times"], ALU.mult)\
                           .then_inc(value_done.sem, 1)
                        dve.wait_ge(value_done.sem, value_done.at(n + 1))
                    dve.scalar_tensor_tensor(out=u["out"], in0=u["src"], scalar=u["gain"], in1=root[n % 2],
                                             op0=ALU.mult, op1=ALU.mult).then_inc(v_step.sem, 1)
        for c in (g_step, p_step, log_done, rstd_done, v_step):
            c.advance(len(units))
        if "times" in units[0]:
            value_done.advance(len(units))

    def conv(z, n_tiles, weight, taps, tmp, func, bias=None):
        with nc.Block() as block:
            @block.scalar
            def _(act):
                for i in range(n_tiles // 2):
                    for b in range(2):
                        t = i * 2 + b
                        act.wait_ge(a_step.sem, a_step.at(i * 4))
                        act.activation(tmp[:, b], z[:, t], ACT.Copy,
                                       scale=weight[:, (t + 1) * taps - 1:(t + 1) * taps]).then_inc(a_step.sem, 1)
                    for b in range(2):
                        t = i * 2 + b
                        act.wait_ge(v_step.sem, v_step.at(i * 2 * (taps - 1) + (b + 1) * (taps - 1)))
                        act.activation(z[:, t], tmp[:, b], func,
                                       bias=0.0 if bias is None else bias[:, t:t + 1]).then_inc(a_step.sem, 1)

            @block.vector
            def _(dve):
                for i in range(n_tiles // 2):
                    for b in range(2):
                        t = i * 2 + b
                        dve.wait_ge(a_step.sem, a_step.at(i * 4 + b + 1))
                        for back in range(1, taps):
                            if back > 1:
                                dve.wait_ge(v_step.sem, v_step.at(i * 2 * (taps - 1) + b * (taps - 1) + back - 1))
                            dve.scalar_tensor_tensor(
                                out=tmp[:, b, back:SEQ],
                                in0=z[:, t, 0:SEQ - back],
                                scalar=weight[:, (t + 1) * taps - 1 - back:(t + 1) * taps - back],
                                in1=tmp[:, b, back:SEQ], op0=ALU.mult, op1=ALU.add).then_inc(v_step.sem, 1)
        a_step.advance(n_tiles * 2)
        v_step.advance(n_tiles * (taps - 1))

    mix_stack = main.enter_context(ExitStack())
    mix = sb(mix_stack, "mix", [P, 13, SEQ])
    qk = xr
    vv = mix[:, 0:4]
    gate = mix[:, 4:8]
    ya = mix[:, 8:12]
    small = mix[:, 12]

    h_stack = main.enter_context(ExitStack())
    act_hi = sb(h_stack, "h1_hi", [P, KT, SEQ], F32R)
    act_lo = sb(h_stack, "h1_lo", [P, KT, SEQ], F32R)
    h = (act_hi, act_lo)
    rstd = sb(h_stack, "h1_rstd", [P, SEQ])
    rcol = sb(h_stack, "h1_rcol", [P, NB])
    x_tiles = [xr[:, k] for k in range(KT)]

    gv = mix[:, 0:4].rearrange("p a n -> p (a n)").rearrange("p (t c) -> p t c", t=NB)
    dense(h, [dict(n=2, dst=ya, func=ACT.Gelu_apprx_tanh),
              dict(n=2, dst=gv, token_major=True, func=ACT.Gelu_apprx_tanh)],
          feed=Feed(h, x_tiles, param("norm_mix"),
                    dict(squares=mix[:, 4:6], sum=mix[:, 6], rstd=rstd[:], rcol=rcol[:])))

    gvn = gv.rearrange("p t (g d) -> p (t g) d", g=4)
    gsq = qk[:, 0:4].rearrange("p a n -> p (a n)").rearrange("p (m d) -> p m d", m=32)
    wT = qk[:, 4, 0:512]
    tri_s = qk[:, 4, 512:640]
    gstat = qk[:, 4, 640:1024]
    rows = qk[:, 5:7].rearrange("p a n -> p (a n)")
    R = qk[:, 7, 0:512]
    gmix = qk[:, 7, 512:1024]
    with nc.Block() as block:
        gsum, gmean, gvar, grstd = (gstat[:, 32 * n:32 * n + 32] for n in range(4))

        @block.sync
        def _(sp):
            sp.dma_start(wT, gm_ws_t).then_inc(loaded.sem, 16)
            sp.dma_start(tri_s, const("tri")).then_inc(loaded.sem, 16)
            sp.dma_start(rows[0:1, 0:1024], row_params).then_inc(loaded.sem, 16)
            sp.wait_ge(loaded.sem, loaded.at(48))

        @block.vector
        def _(dve):
            n = [0]

            def then(ins):
                n[0] += 1
                ins.then_inc(v_step.sem, 1)
                dve.wait_ge(v_step.sem, v_step.at(n[0]))

            then(dve.tensor_reduce(gsum, gvn, AX.X, ALU.add))
            then(dve.tensor_scalar(gmean, gsum, 1.0 / 128, None, ALU.mult))
            then(dve.tensor_tensor(gvn, gvn, gmean.unsqueeze(2).to_broadcast([P, 32, P]), ALU.subtract))
            dve.wait_ge(loaded.sem, loaded.at(48))
            then(dve.tensor_tensor(wT.rearrange("p (g t) -> p g t", g=4), wT.rearrange("p (g t) -> p g t", g=4),
                                   tri_s.unsqueeze(1).to_broadcast([P, 4, P]), ALU.mult))
            dve.wait_ge(a_step.sem, a_step.at(1))
            then(dve.tensor_reduce(gvar, gsq, AX.X, ALU.add))
            then(dve.tensor_scalar(gvar, gvar, 1.0 / 128, EPS, ALU.mult, ALU.add))
            dve.wait_ge(a_step.sem, a_step.at(2))
            then(dve.reciprocal(grstd, grstd))
            then(dve.tensor_tensor(gvn, gvn, grstd.unsqueeze(2).to_broadcast([P, 32, P]), ALU.mult))
            dve.wait_ge(p_step.sem, p_step.at(1))
            then(dve.tensor_copy(rows[0:1, 1024:1536], ps[0:1, 0, 0:512]))
            dve.wait_ge(p_step.sem, p_step.at(2))
            then(dve.tensor_copy(R, ps[:, 1, 0:512]))
            for t in range(NB):
                dve.wait_ge(p_step.sem, p_step.at(3 + t))
                for g in range(4):
                    last = dve.scalar_tensor_tensor(
                        out=gmix[:, g * P:(g + 1) * P], in0=ps[:, 2 + t % 4, g * P:(g + 1) * P],
                        scalar=param("gm_ln_g")[:, g:g + 1], in1=R[:, g * P:(g + 1) * P],
                        op0=ALU.mult, op1=ALU.add)
                then(last)
                u = ya[:, :, t * P:(t + 1) * P]
                then(dve.tensor_tensor(u, u, gmix.rearrange("p (g t) -> p g t", g=4), ALU.mult))

        @block.scalar
        def _(act):
            act.wait_ge(v_step.sem, v_step.at(3))
            act.activation(gsq, gvn, ACT.Square).then_inc(a_step.sem, 1)
            act.wait_ge(v_step.sem, v_step.at(6))
            act.activation(grstd, gvar, ACT.Sqrt).then_inc(a_step.sem, 1)

        @block.tensor
        def _(pe):
            pe.wait_ge(v_step.sem, v_step.at(4))
            pe.matmul(ps[0:1, 0, 0:512], ones[:, 0:1], wT, start=True, stop=True).then_inc(p_step.sem, 1)
            pe.wait_ge(v_step.sem, v_step.at(9))
            for g in range(4):
                c = slice(g * P, (g + 1) * P)
                pe.matmul(ps[:, 1, c], rows[0:1, c], rows[0:1, 1024 + g * P:1024 + (g + 1) * P],
                          start=True, stop=False)
                mm = pe.matmul(ps[:, 1, c], ones[0:1, :], rows[0:1, 512 + g * P:512 + (g + 1) * P],
                               start=False, stop=True)
            mm.then_inc(p_step.sem, 1)
            for t in range(NB):
                if t >= 4:
                    pe.wait_ge(v_step.sem, v_step.at(10 + 2 * (t - 4) + 1))
                for g in range(4):
                    mm = pe.matmul(ps[:, 2 + t % 4, g * P:(g + 1) * P], gv[:, t, g * P:(g + 1) * P],
                                   wT[:, g * P:(g + 1) * P], start=True, stop=True)
                mm.then_inc(p_step.sem, 1)
    loaded.advance(48)
    v_step.advance(10 + 2 * NB)
    a_step.advance(2)
    p_step.advance(2 + NB)

    dense(h, [dict(n=4, dst=qk), dict(n=2, dst=vv), dict(n=2, dst=gate, func=ACT.Silu)], rstd=(rstd, rcol))
    logits = small[:, 0:64]
    wl_stack = main.enter_context(ExitStack())
    wl_hi = sb(wl_stack, "wl_hi", [P, 64], F32R)
    wl_lo = sb(wl_stack, "wl_lo", [P, 64], F32R)
    with nc.Block() as block:
        @block.scalar
        def _(act):
            act.activation(wl_hi[:], param("w_logits"), ACT.Copy).then_inc(a_step.sem, 1)

        @block.vector
        def _(dve):
            dve.wait_ge(a_step.sem, a_step.at(1))
            dve.tensor_tensor(wl_lo[:], param("w_logits"), wl_hi[:].bitcast(F32), ALU.subtract)\
               .then_inc(v_step.sem, 1)
            dve.wait_ge(p_step.sem, p_step.at(1))
            dve.tensor_tensor(logits.rearrange("p (t c) -> p t c", t=NB),
                              ps[:, 0, 0:64].rearrange("p (t c) -> p t c", t=NB),
                              rcol[:].unsqueeze(2).to_broadcast([P, NB, 8]), ALU.mult)

        @block.tensor
        def _(pe):
            pe.wait_ge(v_step.sem, v_step.at(1))
            for t in range(NB):
                for i, (wp, ap) in enumerate(((0, 0), (0, 1), (1, 0))):
                    for k in range(KT):
                        mm = pe.matmul(ps[:, 0, t * 8:t * 8 + 8], h[ap][:, k, t * P:(t + 1) * P],
                                       (wl_hi, wl_lo)[wp][:, k * 8:k * 8 + 8],
                                       start=(i == 0 and k == 0), stop=(i == 2 and k == KT - 1))
            mm.then_inc(p_step.sem, 1)
    a_step.advance(1)
    v_step.advance(1)
    p_step.advance(1)
    wl_stack.close()
    h_stack.close()

    t_stack = main.enter_context(ExitStack())
    tmp = sb(t_stack, "conv_tmp", [P, 4, SEQ])
    conv(qk, 8, param("dn_conv"), CONV_W, tmp[:, 0:2], ACT.Silu)
    conv(vv, 4, param("dn_conv")[:, 32:48], CONV_W, tmp[:, 0:2], ACT.Silu)
    norm_units([dict(src=z, out=z, scale=1.0, gain=128.0 ** -0.5 if t < 4 else 1.0)
                for t in range(8) for z in (qk[:, t, 0:HALF], qk[:, t, HALF:SEQ])], ones[:], tmp)
    t_stack.close()
    st = main.enter_context(ExitStack())
    W = HEADS * P
    tri = sb(st, "tri", [P, P])
    strict = sb(st, "strict", [P, P])
    levels = sb(st, "levels", [P, 7, P])
    state = sb(st, "state", [P, W])
    resid = sb(st, "resid", [P, W])
    v_new = sb(st, "v_new", [P, W])

    def per_slot(name, n=1):
        return [sb(st, f"{name}{s}", [P, n, W] if n > 1 else [P, W]) for s in range(2)]

    decay = per_slot("decay")
    q_dec = per_slot("q_dec")
    n_mat = per_slot("n_mat")
    qk_mat = per_slot("qk_mat")
    n_lev = per_slot("n_lev", 2)
    k_dec = per_slot("k_dec")
    v_tok = per_slot("v_tok")
    k_cur = per_slot("k_cur")
    x_mat = per_slot("x_mat")
    t_mat = per_slot("t_mat")
    tt_mat = per_slot("tt_mat")
    v_cur = t_mat

    def col(n):
        return small[:, 64 + 32 * n:96 + 32 * n]

    beta, g_log, dec, neg_ed, cd, kd, nbeta, t_abs, t_exp = (col(n) for n in range(9))
    a_exp = small[:, 400:404]

    lg = logits.rearrange("p (b c) -> p b c", c=8)
    with nc.Block() as block:
        three = lambda x: x.rearrange("p (b h) -> p b h", h=4)

        @block.sync
        def _(sp):
            sp.dma_start(tri[:], const("tri")).then_inc(loaded.sem, 16)
            sp.dma_start(strict[:], const("strict")).then_inc(loaded.sem, 16)
            sp.dma_start(levels[:].rearrange("p l n -> p (l n)"), const("levels")).then_inc(loaded.sem, 16)
            sp.wait_ge(loaded.sem, loaded.at(48))

        @block.scalar
        def _(act):
            n = [0]

            def then(ins):
                n[0] += 1
                ins.then_inc(a_step.sem, 1)
                act.wait_ge(a_step.sem, a_step.at(n[0]))

            then(act.activation(three(beta), lg[:, :, 0:4], ACT.Sigmoid))
            act.wait_ge(v_step.sem, v_step.at(1))
            then(act.activation(t_abs, g_log, ACT.Abs))
            then(act.activation(t_exp, t_abs, ACT.Exp, scale=-1.0))
            then(act.activation(t_exp, t_exp, ACT.Ln, bias=1.0))
            then(act.activation(a_exp, param("dn_a_log"), ACT.Exp))
            act.wait_ge(v_step.sem, v_step.at(6))
            then(act.activation(neg_ed, dec, ACT.Exp))
            then(act.activation(cd, ps[:, 1, 0:32], ACT.Exp))
            then(act.activation(kd, kd, ACT.Exp))

        @block.vector
        def _(dve):
            n = [0]

            def then(ins):
                n[0] += 1
                ins.then_inc(v_step.sem, 1)
                dve.wait_ge(v_step.sem, v_step.at(n[0]))

            then(dve.tensor_tensor(three(g_log), lg[:, :, 4:8],
                                   param("dn_dt_bias").unsqueeze(1).to_broadcast([P, NB, 4]), ALU.add))
            dve.wait_ge(a_step.sem, a_step.at(4))
            then(dve.scalar_tensor_tensor(out=g_log, in0=g_log, scalar=0.0, in1=t_exp, op0=ALU.max, op1=ALU.add))
            dve.wait_ge(a_step.sem, a_step.at(5))
            then(dve.scalar_tensor_tensor(out=three(g_log), in0=three(g_log), scalar=-1.0,
                                          in1=a_exp.unsqueeze(1).to_broadcast([P, NB, 4]),
                                          op0=ALU.mult, op1=ALU.mult))
            then(dve.tensor_scalar(nbeta, beta, -1.0, None, ALU.mult))
            dve.wait_ge(p_step.sem, p_step.at(1))
            then(dve.tensor_copy(dec, ps[:, 0, 0:32]))
            then(dve.scalar_tensor_tensor(out=kd, in0=dec, scalar=-1.0, in1=ps[:, 1, 0:32],
                                          op0=ALU.mult, op1=ALU.add))
            dve.wait_ge(a_step.sem, a_step.at(6))
            then(dve.tensor_scalar(neg_ed, neg_ed, -1.0, None, ALU.mult))
            then(dve.memset(state[:], 0.0))

        @block.tensor
        def _(pe):
            pe.wait_ge(v_step.sem, v_step.at(3))
            pe.wait_ge(loaded.sem, loaded.at(48))
            pe.matmul(ps[:, 0, 0:32], tri[:], g_log, start=True, stop=True)
            pe.matmul(ps[:, 1, 0:32], ones[:], g_log, start=True, stop=True).then_inc(p_step.sem, 1)
    loaded.advance(48)
    a_step.advance(8)
    v_step.advance(8)
    p_step.advance(1)


    hs = lambda h: slice(h * P, (h + 1) * P)
    heads = lambda ap: ap.rearrange("p (h n) -> p h n", h=HEADS)
    over_heads = lambda ap: ap.unsqueeze(1).to_broadcast([P, HEADS, P])
    n_it = NB // 2

    def head_block(it, s, h):
        return qk[:, h, bass.ds(it * 256 + s * P, P)]

    def blk(z, it, s):
        return z[:, 0:4, bass.ds(it * 256 + s * P, P)]

    def scal(c, it, s, h):
        return c[:, bass.ds(it * 8 + s * 4 + h, 1)]

    with nc.Block() as block:
        @block.vector
        def _(dve):
            with dve.Fori(0, n_it) as it:
                for s in range(2):
                    dve.wait_ge(o_ready.sem, o_ready.at(it * 2))
                    g4 = g_log[:, bass.ds(it * 8 + s * 4, 4)]
                    dve.tensor_tensor(heads(decay[s][:]), over_heads(tri[:]),
                                      g4.unsqueeze(2).to_broadcast([P, HEADS, P]), ALU.mult)\
                       .then_inc(gtri_ready[s].sem, 1)
                for s in range(2):
                    dve.wait_ge(exp_done[s].sem, exp_done[s].at(it * 2 + 1))
                    for h in range(HEADS):
                        last = dve.tensor_scalar(decay[s][:, hs(h)], ps[:, 3 * s, hs(h)], scal(dec, it, s, h), 0.0,
                                                 ALU.subtract, ALU.min)
                    last.then_inc(arg_ready[s].sem, 1)
                for s in range(2):
                    dve.wait_ge(exp_done[s].sem, exp_done[s].at(it * 2 + 2))
                    dve.wait_ge(grams_done[s].sem, grams_done[s].at(it + 1))
                    for h in range(HEADS):
                        last = dve.scalar_tensor_tensor(out=n_mat[s][:, hs(h)], in0=ps[:, 3 * s + 1, hs(h)],
                                                        scalar=scal(nbeta, it, s, h), in1=decay[s][:, hs(h)],
                                                        op0=ALU.mult, op1=ALU.mult)
                    last.then_inc(raw_done[s].sem, 1)
                    dve.tensor_tensor(qk_mat[s][:], ps[:, 3 * s + 2, :], decay[s][:], ALU.mult)\
                       .then_inc(raw_done[s].sem, 1)
                for s in range(2):
                    dve.wait_ge(level_ready[s].sem, level_ready[s].at(it * 7 + 1))
                    dve.tensor_tensor(heads(tt_mat[s][:]), heads(n_lev[s][:, 0]), over_heads(ident[:]), ALU.add)\
                       .then_inc(tt_ready[s].sem, 1)
                for s in range(2):
                    dve.wait_ge(first_turned[s].sem, first_turned[s].at(it + 1))
                    dve.tensor_copy(t_mat[s][:], ps[:, 3 * s + 2, :]).then_inc(t_ready[s].sem, 1)
                for lev in range(1, 7):
                    for s in range(2):
                        dve.wait_ge(prod_done[s].sem, prod_done[s].at(it * 6 + lev))
                        if lev < 6:
                            dve.tensor_tensor(t_mat[s][:], ps[:, 3 * s + 1, :], t_mat[s][:], ALU.add)\
                               .then_inc(t_ready[s].sem, 1)
                        dve.tensor_tensor(tt_mat[s][:], ps[:, 3 * s + 2, :], tt_mat[s][:], ALU.add)\
                           .then_inc(tt_ready[s].sem, 1)
                for s in range(2):
                    n = it * 2 + s
                    dve.wait_ge(by_token[s].sem, by_token[s].at(it * 2 + 2))
                    dve.wait_ge(ks_done.sem, ks_done.at(n + 1))
                    for h in range(HEADS):
                        last = dve.scalar_tensor_tensor(out=resid[:, hs(h)], in0=ps[:, 6, hs(h)],
                                                        scalar=scal(neg_ed, it, s, h), in1=v_tok[s][:, hs(h)],
                                                        op0=ALU.mult, op1=ALU.add)
                    last.then_inc(resid_ready.sem, 1)
                    dve.wait_ge(step_done.sem, step_done.at(n + 1))
                    for h in range(HEADS):
                        last = dve.scalar_tensor_tensor(out=state[:, hs(h)], in0=state[:, hs(h)],
                                                        scalar=scal(cd, it, s, h), in1=ps[:, 7, hs(h)],
                                                        op0=ALU.mult, op1=ALU.add)
                    last.then_inc(state_ready.sem, 1)

        @block.scalar
        def _(act):
            with act.Fori(0, n_it) as it:
                for s in range(2):
                    act.wait_ge(rows_done[s].sem, rows_done[s].at(it + 1))
                    act.activation(q_dec[s][:], ps[:, 3 * s, :], ACT.Exp).then_inc(exp_done[s].sem, 1)
                    act.wait_ge(arg_ready[s].sem, arg_ready[s].at(it + 1))
                    act.activation(decay[s][:], decay[s][:], ACT.Exp).then_inc(exp_done[s].sem, 1)
                for s in range(2):
                    act.wait_ge(turned[s].sem, turned[s].at(it * 2 + 1))
                    for h in range(HEADS):
                        last = act.activation(k_dec[s][:, hs(h)], ps[:, 3 * s, hs(h)], ACT.Copy,
                                              scale=scal(kd, it, s, h))
                    last.then_inc(by_token[s].sem, 1)
                    act.wait_ge(turned[s].sem, turned[s].at(it * 2 + 2))
                    act.activation(v_tok[s][:], ps[:, 3 * s + 1, :], ACT.Copy).then_inc(by_token[s].sem, 1)
                for lev in range(1, 7):
                    for s in range(2):
                        act.wait_ge(x_done[s].sem, x_done[s].at(it * 6 + lev))
                        act.activation(x_mat[s][:], ps[:, 3 * s, :], ACT.Copy).then_inc(x_ready[s].sem, 1)
                for s in range(2):
                    n = it * 2 + s
                    act.wait_ge(tr_done.sem, tr_done.at(n + 1))
                    for h in range(HEADS):
                        last = act.activation(v_new[:, hs(h)], ps[:, 7, hs(h)], ACT.Copy, scale=scal(beta, it, s, h))
                    last.then_inc(vnew_ready.sem, 1)
                    act.wait_ge(step_done.sem, step_done.at(n + 1))
                    act.activation(blk(qk, it, s), heads(ps[:, 6, :]), ACT.Copy).then_inc(o_ready.sem, 1)

        @block.gpsimd
        def _(pool):
            with pool.Fori(0, n_it) as it:
                for s in range(2):
                    pool.wait_ge(raw_done[s].sem, raw_done[s].at(it * 2 + 1))
                    pool.tensor_tensor(heads(n_mat[s][:]), heads(n_mat[s][:]), over_heads(strict[:]), ALU.mult)\
                        .then_inc(masked[s].sem, 1)
                    pool.wait_ge(masked[s].sem, masked[s].at(it * 3 + 1))
                    pool.tensor_tensor(heads(n_lev[s][:, 0]), heads(n_mat[s][:]), over_heads(levels[:, 0]), ALU.mult)\
                        .then_inc(level_ready[s].sem, 1)
                for s in range(2):
                    pool.wait_ge(raw_done[s].sem, raw_done[s].at(it * 2 + 2))
                    pool.tensor_tensor(heads(n_lev[s][:, 1]), heads(n_mat[s][:]), over_heads(levels[:, 1]), ALU.mult)\
                        .then_inc(level_ready[s].sem, 1)
                for s in range(2):
                    pool.tensor_tensor(heads(qk_mat[s][:]), heads(qk_mat[s][:]), over_heads(tri[:]), ALU.mult)\
                        .then_inc(masked[s].sem, 1)
                for lev in range(2, 7):
                    for s in range(2):
                        if lev == 2:
                            pool.wait_ge(tt_ready[s].sem, tt_ready[s].at(it * 7 + 1))
                        else:
                            pool.wait_ge(x_done[s].sem, x_done[s].at(it * 6 + lev - 2))
                        pool.tensor_tensor(heads(n_lev[s][:, lev % 2]), heads(n_mat[s][:]), over_heads(levels[:, lev]),
                                           ALU.mult).then_inc(level_ready[s].sem, 1)
                for s in range(2):
                    pool.wait_ge(exp_done[s].sem, exp_done[s].at(it * 2 + 1))
                    pool.tensor_tensor(heads(q_dec[s][:]), heads(q_dec[s][:]), blk(qk, it, s), ALU.mult)\
                        .then_inc(masked[s].sem, 1)

        @block.tensor
        def _(pe):
            with pe.Fori(0, n_it) as it:
                for s in range(2):
                    pe.wait_ge(gtri_ready[s].sem, gtri_ready[s].at(it + 1))
                    pe.matmul(ps[:, 3 * s, :], ones[:], decay[s][:], start=True, stop=True).then_inc(rows_done[s].sem, 1)
                for s in range(2):
                    pe.wait_ge(block_loaded[s].sem, block_loaded[s].at(it * 32 + 32))
                    for h in range(HEADS):
                        pe.matmul(ps[:, 3 * s + 1, hs(h)], k_cur[s][:, hs(h)], k_cur[s][:, hs(h)],
                                  start=True, stop=True)
                    for h in range(HEADS):
                        mm = pe.matmul(ps[:, 3 * s + 2, hs(h)], k_cur[s][:, hs(h)], head_block(it, s, h),
                                       start=True, stop=True)
                    mm.then_inc(grams_done[s].sem, 1)
                for s in range(2):
                    pe.wait_ge(arg_ready[s].sem, arg_ready[s].at(it + 1))
                    pe.wait_ge(exp_done[s].sem, exp_done[s].at(it * 2 + 1))
                    for h in range(HEADS):
                        mm = pe.transpose(ps[:, 3 * s, hs(h)], k_cur[s][:, hs(h)], ident[:])
                    mm.then_inc(turned[s].sem, 1)
                    pe.wait_ge(raw_done[s].sem, raw_done[s].at(it * 2 + 1))
                    for h in range(HEADS):
                        mm = pe.transpose(ps[:, 3 * s + 1, hs(h)], v_cur[s][:, hs(h)], ident[:])
                    mm.then_inc(turned[s].sem, 1)
                for s in range(2):
                    pe.wait_ge(tt_ready[s].sem, tt_ready[s].at(it * 7 + 1))
                    pe.wait_ge(raw_done[s].sem, raw_done[s].at(it * 2 + 2))
                    for h in range(HEADS):
                        mm = pe.transpose(ps[:, 3 * s + 2, hs(h)], tt_mat[s][:, hs(h)], ident[:])
                    mm.then_inc(first_turned[s].sem, 1)
                for lev in range(1, 7):
                    for s in range(2):
                        pe.wait_ge(level_ready[s].sem, level_ready[s].at(it * 7 + lev + 1))
                        pe.wait_ge(t_ready[s].sem, t_ready[s].at(it * 6 + lev))
                        if lev == 1:
                            pe.wait_ge(by_token[s].sem, by_token[s].at(it * 2 + 2))
                        for h in range(HEADS):
                            mm = pe.matmul(ps[:, 3 * s, hs(h)], n_lev[s][:, lev % 2, hs(h)], t_mat[s][:, hs(h)],
                                           start=True, stop=True)
                        mm.then_inc(x_done[s].sem, 1)
                    for s in range(2):
                        pe.wait_ge(x_ready[s].sem, x_ready[s].at(it * 6 + lev))
                        pe.wait_ge(tt_ready[s].sem, tt_ready[s].at(it * 7 + lev))
                        if lev < 6:
                            for h in range(HEADS):
                                pe.matmul(ps[:, 3 * s + 1, hs(h)], tt_mat[s][:, hs(h)], x_mat[s][:, hs(h)],
                                          start=True, stop=True)
                        for h in range(HEADS):
                            mm = pe.matmul(ps[:, 3 * s + 2, hs(h)], x_mat[s][:, hs(h)], tt_mat[s][:, hs(h)],
                                           start=True, stop=True)
                        mm.then_inc(prod_done[s].sem, 1)
                for s in range(2):
                    n = it * 2 + s
                    pe.wait_ge(state_ready.sem, state_ready.at(n))
                    pe.wait_ge(o_ready.sem, o_ready.at(n))
                    for h in range(HEADS):
                        mm = pe.matmul(ps[:, 6, hs(h)], k_cur[s][:, hs(h)], state[:, hs(h)], start=True, stop=True)
                    mm.then_inc(ks_done.sem, 1)
                    pe.wait_ge(resid_ready.sem, resid_ready.at(n + 1))
                    pe.wait_ge(tt_ready[s].sem, tt_ready[s].at(it * 7 + 7))
                    for h in range(HEADS):
                        mm = pe.matmul(ps[:, 7, hs(h)], tt_mat[s][:, hs(h)], resid[:, hs(h)], start=True, stop=True)
                    mm.then_inc(tr_done.sem, 1)
                    pe.wait_ge(vnew_ready.sem, vnew_ready.at(n + 1))
                    pe.wait_ge(masked[s].sem, masked[s].at(it * 3 + 3))
                    for h in range(HEADS):
                        pe.matmul(ps[:, 6, hs(h)], state[:, hs(h)], q_dec[s][:, hs(h)], start=True, stop=False)
                        pe.matmul(ps[:, 6, hs(h)], v_new[:, hs(h)], qk_mat[s][:, hs(h)], start=False, stop=True)
                    for h in range(HEADS):
                        mm = pe.matmul(ps[:, 7, hs(h)], k_dec[s][:, hs(h)], v_new[:, hs(h)], start=True, stop=True)
                    mm.then_inc(step_done.sem, 1)

        @block.sync
        def _(sp):
            with sp.Fori(0, n_it) as it:
                for s in range(2):
                    sp.wait_ge(o_ready.sem, o_ready.at(it * 2))
                    sp.wait_ge(state_ready.sem, state_ready.at(it * 2))
                    sp.dma_start(heads(k_cur[s][:]), qk[:, 4:8, bass.ds(it * 256 + s * P, P)])\
                      .then_inc(block_loaded[s].sem, 16)
                    sp.dma_start(heads(v_cur[s][:]), vv[:, 0:4, bass.ds(it * 256 + s * P, P)])\
                      .then_inc(block_loaded[s].sem, 16)
    st.close()

    norm_units([dict(src=z[:, hf * HALF:(hf + 1) * HALF], out=z[:, hf * HALF:(hf + 1) * HALF], scale=1.0 / 128,
                     gain=param("dn_onorm"), times=gate[:, t, hf * HALF:(hf + 1) * HALF])
                for t in range(HEADS) for z in [qk[:, t]] for hf in range(2)], ones[:], vv[:, 0:2])
    y_stack = main.enter_context(ExitStack())
    y = (sb(y_stack, "y1_hi", [P, KT, SEQ], F32R), sb(y_stack, "y1_lo", [P, KT, SEQ], F32R))
    halves = [slice(0, HALF), slice(HALF, SEQ)]

    def reload_x(src):
        def start(sp):
            sp.wait_ge(lo_done.sem, lo_done.at(KT))
            for k in range(KT):
                sp.dma_start(xr[:, k, :], src[:, k, :]).then_inc(loaded.sem, 16)

        def wait(dve):
            dve.wait_ge(loaded.sem, loaded.at(16 * KT))
        return start, wait

    start, wait = reload_x(x_t)
    dense(y, [dict(n=4, dst=xr, add=True, wait=wait)], before=start,
          feed=Feed(y, [(ya if t < 4 else qk)[:, t % 4] for t in range(KT)]))
    loaded.advance(16 * KT)
    y_stack.close()
    mix_stack.close()

    def scope():
        return main.enter_context(ExitStack())

    xa = scope()
    q_t = sb(xa, "xa_q", [P, KT, SEQ])
    k_t = sb(xa, "xa_k", [P, KT, MEM])
    v_m = sb(xa, "xa_v", [P, 2, D])
    mem = scope()
    mem_x = sb(mem, "mem_x", [P, KT, MEM])
    m = (sb(mem, "mem_hi", [P, KT, MEM], F32R), sb(mem, "mem_lo", [P, KT, MEM], F32R))
    with nc.Block() as block:
        @block.sync
        def _(sp):
            sp.dma_start(mem_x[:], mem_t).then_inc(loaded.sem, 16)
            sp.wait_ge(loaded.sem, loaded.at(16))
    loaded.advance(16)
    mem_rstd = sb(mem, "mem_rstd", [P, MEM])
    mem_rcol = sb(mem, "mem_rcol", [P, 2])
    dense(m, [dict(n=4, dst=k_t), dict(n=4, dst=v_m, token_major=True)], tokens=MEM,
          feed=Feed(m, [mem_x[:, k] for k in range(KT)], param("norm_mem"),
                    dict(squares=q_t[:, 6:8, 0:MEM], sum=q_t[:, 5, 0:MEM], rstd=mem_rstd[:], rcol=mem_rcol[:]),
                    tokens=MEM))
    mem.close()

    h_stack = scope()
    h = (sb(h_stack, "h2_hi", [P, KT, SEQ], F32R), sb(h_stack, "h2_lo", [P, KT, SEQ], F32R))
    rstd = sb(h_stack, "h2_rstd", [P, SEQ])
    dense(h, [dict(n=4, dst=q_t)],
          feed=Feed(h, x_tiles, param("norm_xa"),
                    dict(squares=q_t[:, 6:8], sum=q_t[:, 5], rstd=rstd[:], rcol=None)))
    h_stack.close()

    at = scope()
    q_h = sb(at, "q_h", [P, 2, 2, SEQ])
    k_h = sb(at, "k_h", [P, 2, 2, MEM])
    v_h = sb(at, "v_h", [P, 2, 2, XA_D])
    prob = sb(at, "prob", [P, 2, MEM])
    prob_t = sb(at, "prob_t", [P, 2, 2, HALF])
    stat = sb(at, "stat", [P, 2, 4])

    scale = XA_D ** -0.5
    with nc.Block() as block:
        @block.sync
        def _(sp):
            with sp.Fori(0, 2) as it:
                for s in range(2):
                    sp.wait_ge(xa_o_copied.sem, xa_o_copied.at(it * 8))
                    sp.dma_start(q_h[:, s], q_t[:, bass.ds(it * 4 + s * 2, 2), :]).then_inc(xa_head_loaded[s].sem, 16)
                    sp.dma_start(k_h[:, s], k_t[:, bass.ds(it * 4 + s * 2, 2), :]).then_inc(xa_head_loaded[s].sem, 16)
                    sp.dma_start(v_h[:, s], v_m[:, :, bass.ds(it * 512 + s * 256, 256)])\
                      .then_inc(xa_head_loaded[s].sem, 16)

        @block.tensor
        def _(pe):
            with pe.Fori(0, 2) as it:
                for s in range(2):
                    pe.wait_ge(xa_head_loaded[s].sem, xa_head_loaded[s].at(it * 48 + 48))
                    n0 = it * 16 + s * 8

                    def scores(u):
                        pe.wait_ge(xa_exp_done.sem, xa_exp_done.at(n0 + u - 1 if u >= 1 else n0))
                        for t in range(2):
                            mm = pe.matmul(ps[:, u % 2, 0:MEM], q_h[:, s, t, u * P:(u + 1) * P], k_h[:, s, t, :],
                                           start=(t == 0), stop=(t == 1))
                        mm.then_inc(xa_score_done.sem, 1)

                    def outputs(hf):
                        pe.wait_ge(xa_pt_ready.sem, xa_pt_ready.at(n0 + hf * 4 + 4))
                        pe.wait_ge(xa_o_copied.sem, xa_o_copied.at(it * 8 + s * 4))
                        for dt in range(2):
                            for t in range(2):
                                mm = pe.matmul(ps[:, 4 + 2 * hf + dt, :], v_h[:, s, t, dt * P:(dt + 1) * P],
                                               prob_t[:, hf, t, :], start=(t == 0), stop=(t == 1))
                            mm.then_inc(xa_o_done.sem, 1)

                    scores(0)
                    for u in range(8):
                        if u < 7:
                            scores(u + 1)
                        if u == 4:
                            outputs(0)
                        pe.wait_ge(xa_p_ready.sem, xa_p_ready.at(n0 + u + 1))
                        pe.wait_ge(xa_pt_ready.sem, xa_pt_ready.at(n0 + u - 1 if u >= 1 else n0))
                        for t in range(2):
                            mm = pe.transpose(ps[:, 2 + u % 2, t * P:(t + 1) * P], prob[:, u % 2, t * P:(t + 1) * P],
                                              ident[:])
                        mm.then_inc(xa_pt_done.sem, 1)
                    outputs(1)

        @block.vector
        def _(dve):
            with dve.Fori(0, 2) as it:
                for s in range(2):
                    def soft(u):
                        n = it * 16 + s * 8 + u
                        st = stat[:, u % 2]
                        dve.wait_ge(xa_score_done.sem, xa_score_done.at(n + 1))
                        dve.tensor_reduce(st[:, 0:1], ps[:, u % 2, 0:MEM], AX.X, ALU.max)\
                           .then_inc(xa_max_done.sem, 1)
                        dve.wait_ge(xa_max_done.sem, xa_max_done.at(n + 1))
                        dve.tensor_scalar(st[:, 1:2], st[:, 0:1], -scale, None, ALU.mult)\
                           .then_inc(xa_bias_done.sem, 1)

                    def combine(u):
                        n = it * 16 + s * 8 + u
                        st = stat[:, u % 2]
                        dve.wait_ge(xa_exp_done.sem, xa_exp_done.at(n + 1))
                        dve.reciprocal(st[:, 3:4], st[:, 2:3]).then_inc(xa_inv_done.sem, 1)
                        dve.wait_ge(xa_inv_done.sem, xa_inv_done.at(n + 1))
                        dve.tensor_scalar(prob[:, u % 2], prob[:, u % 2], st[:, 3:4], None, ALU.mult)\
                           .then_inc(xa_p_ready.sem, 1)

                    def store(hf):
                        for dt in range(2):
                            dve.wait_ge(xa_o_done.sem, xa_o_done.at(it * 8 + s * 4 + 2 * hf + dt + 1))
                            dve.tensor_copy(q_t[:, bass.ds(it * 4 + s * 2 + dt, 1), halves[hf]]
                                            .rearrange("p o n -> p (o n)"), ps[:, 4 + 2 * hf + dt, :])\
                               .then_inc(xa_o_copied.sem, 1)

                    soft(0)
                    for u in range(8):
                        combine(u)
                        if u < 7:
                            soft(u + 1)
                        if u == 4:
                            store(0)
                    store(1)

        @block.scalar
        def _(act):
            with act.Fori(0, 2) as it:
                for s in range(2):
                    def exps(u):
                        n = it * 16 + s * 8 + u
                        st = stat[:, u % 2]
                        act.wait_ge(xa_bias_done.sem, xa_bias_done.at(n + 1))
                        act.wait_ge(xa_pt_done.sem, xa_pt_done.at(n - 1 if u >= 1 else it * 16 + s * 8))
                        act.activation(prob[:, u % 2], ps[:, u % 2, 0:MEM], ACT.Exp, bias=st[:, 1:2], scale=scale,
                                       accum_out=st[:, 2:3]).then_inc(xa_exp_done.sem, 1)

                    exps(0)
                    for u in range(8):
                        n = it * 16 + s * 8 + u
                        if u < 7:
                            exps(u + 1)
                        act.wait_ge(xa_pt_done.sem, xa_pt_done.at(n + 1))
                        if u % 4 == 0:
                            act.wait_ge(xa_o_done.sem, xa_o_done.at(it * 8 + s * 4))
                        act.activation(prob_t[:, u // 4, :, (u % 4) * P:(u % 4 + 1) * P],
                                       ps[:, 2 + u % 2, 0:MEM].rearrange("p (t n) -> p t n", t=2), ACT.Copy)\
                           .then_inc(xa_pt_ready.sem, 1)
    at.close()
    y_stack = scope()
    y = (sb(y_stack, "y2_hi", [P, KT, SEQ], F32R), sb(y_stack, "y2_lo", [P, KT, SEQ], F32R))
    dense(y, [dict(n=4, dst=xr, add=True)], feed=Feed(y, [q_t[:, t] for t in range(KT)]))
    y_stack.close()
    xa.close()


    def mlp(gain, n_chunks, gated, name):
        st = scope()
        h = (sb(st, name + "_hi", [P, KT, SEQ], F32R), sb(st, name + "_lo", [P, KT, SEQ], F32R))
        rstd = sb(st, name + "_rstd", [P, SEQ])
        hid = [[sb(st, f"{name}_hid{p}{c}", [P, 2, SEQ], F32R) for c in range(2)] for p in range(2)]
        val = sb(st, f"{name}_val", [P, 4, HALF])
        feed = Feed(h, x_tiles, gain, dict(squares=val[:].rearrange("p (a b) n -> p a (b n)", a=2), sum=rstd[:],
                                           rstd=rstd[:], rcol=None))
        per = 3 if gated else 2
        base = slab_at[0]
        total = per * n_chunks
        ends = base + total == n_slabs
        loops = (n_chunks - 1) // 2 - (1 if ends and (n_chunks - 1) % 2 == 0 else 0)

        def sequence(eng, step):
            def chunk(c0, s0, it, kc, ks):
                for n, (op, dc) in enumerate(([("gate", 0)] if gated else []) + [("up", 0), ("down", -1)]):
                    step(eng, op, kc * it + (c0 + dc), ks * it + (s0 + n), c0 + dc, s0 + n, it)
            if gated:
                step(eng, "gate", 0, 0, 0, 0, 0)
            step(eng, "up", 0, per - 2, 0, per - 2, 0)
            with eng.Fori(0, loops) as it:
                for cc in range(2):
                    chunk(1 + cc, per - 1 + cc * per, it, 2, 2 * per)
            for c in range(1 + 2 * loops, n_chunks):
                chunk(c, per - 1 + (c - 1) * per, 0, 0, 0)
            step(eng, "down", n_chunks - 1, total - 1, n_chunks - 1, total - 1, 0)

        def wait_group(eng, op, c, j):
            sem, n = {"gate": (gate_done, 4), "up": (up_done, 4), "down": (down_done, 16)}[op]
            eng.wait_ge(sem.sem, sem.at(c * n + j + 1))

        def hidden(part, cf, j):
            return hid[part][cf % 2][:, j // 2, halves[j % 2]]

        def act_step(act, op, c, s, cf, sf, it):
            if sf == 0:
                feed.act_split(act)
                feed.act_root(act)
            if op == "gate":
                for j in range(4):
                    act.wait_ge(gate_read.sem, gate_read.at(c * 4 + j + 1))
                    act.activation(val[:, j], val[:, j], ACT.Silu).then_inc(silu_done.sem, 1)
            if op == "up":
                if not gated:
                    for j in range(4):
                        act.wait_ge(relu_done.sem, relu_done.at(c * 4 + j + 1))
                        act.activation(val[:, j], val[:, j], ACT.Square).then_inc(square_done.sem, 1)
                for j in range(4):
                    act.wait_ge(square_done.sem, square_done.at(c * 4 + j + 1))
                    act.activation(hidden(0, cf, j), val[:, j], ACT.Copy).then_inc(hid_hi.sem, 1)
            if sf + base + 2 < n_slabs:
                wait_group(act, op, c, 15 if op == "down" else 3)
                g = base + sf + 2
                split_hi(act, base + 2 + s, it * per + g // 2, g % 2)

        def dve_step(dve, op, c, s, cf, sf, it):
            if sf == 0:
                feed.dve_split(dve)
                feed.dve_wait_root(dve)
            if op == ("gate" if gated else "up"):
                dve.wait_ge(hid_ready.sem, hid_ready.at(c * 4))
            if op == "gate":
                for j in range(4):
                    wait_group(dve, op, c, j)
                    dve.tensor_tensor(val[:, j], ps[:, j, :], rstd[:, halves[j % 2]], ALU.mult)\
                       .then_inc(gate_read.sem, 1)
            if op == "up":
                for j in range(4):
                    wait_group(dve, op, c, j)
                    if gated:
                        dve.wait_ge(silu_scaled.sem, silu_scaled.at(c * 4 + j + 1))
                        dve.tensor_tensor(val[:, j], ps[:, j, :], val[:, j], ALU.mult).then_inc(square_done.sem, 1)
                    else:
                        dve.scalar_tensor_tensor(out=val[:, j], in0=ps[:, j, :], scalar=0.0,
                                                 in1=rstd[:, halves[j % 2]], op0=ALU.max, op1=ALU.mult)\
                           .then_inc(relu_done.sem, 1)
                for j in range(4):
                    dve.wait_ge(hid_hi.sem, hid_hi.at(c * 4 + j + 1))
                    dve.tensor_tensor(hidden(1, cf, j), val[:, j], hidden(0, cf, j).bitcast(F32), ALU.subtract)\
                       .then_inc(hid_ready.sem, 1)
            if op == "down":
                for j in range(16):
                    wait_group(dve, op, c, j)
                    t = xr[:, j // 2, halves[j % 2]]
                    dve.tensor_tensor(t, ps[:, 4 + j % 4, :], t, ALU.add).then_inc(bank_free.sem, 1)

        def pe_step(pe, op, c, s, cf, sf, it):
            slot = (base + sf) % 2
            pe.wait_ge(slab_split.sem, base + 1 + s)
            if sf == 0:
                feed.pe_first(pe, slot, [(ps[:, j, :], j // 2, j % 2) for j in range(4)],
                              gate_done if gated else up_done)
                feed.pe_sums(pe)
            elif op != "down":
                done = gate_done if op == "gate" else up_done
                for j in range(4):
                    if op == "up" and gated:
                        pe.wait_ge(gate_read.sem, gate_read.at(c * 4 + j + 1))
                    elif cf > 0:
                        last = square_done if gated else relu_done
                        pe.wait_ge(last.sem, last.at(c * 4 + j - 3))
                    m, hf = j // 2, j % 2
                    for i, (wp, ap) in enumerate(((0, 0), (0, 1), (1, 0))):
                        for k in range(KT):
                            mm = pe.matmul(ps[:, j, :], slab_of(wp, slot)[:, k * CB + m * P:k * CB + (m + 1) * P],
                                           h[ap][:, k, halves[hf]],
                                           start=(i == 0 and k == 0), stop=(i == 2 and k == KT - 1))
                    mm.then_inc(done.sem, 1)
            else:
                pe.wait_ge(hid_ready.sem, hid_ready.at(c * 4 + 4))
                if cf == 0:
                    feed.pe_wait_sums_read(pe)
                for j in range(16):
                    pe.wait_ge(bank_free.sem, bank_free.at(c * 16 + j - 3))
                    m, hf = j // 2, j % 2
                    for i, (wp, ap) in enumerate(((0, 0), (0, 1), (1, 0))):
                        for k in range(2):
                            mm = pe.matmul(ps[:, 4 + j % 4, :], slab_of(wp, slot)[:, k * D + m * P:k * D + (m + 1) * P],
                                           hid[ap][cf % 2][:, k, halves[hf]],
                                           start=(i == 0 and k == 0), stop=(i == 2 and k == 1))
                    mm.then_inc(down_done.sem, 1)

        def pool_step(pool, op, c, s, cf, sf, it):
            if op == "gate":
                for j in range(4):
                    pool.wait_ge(silu_done.sem, silu_done.at(c * 4 + j + 1))
                    pool.tensor_tensor(val[:, j], val[:, j], rstd[:, halves[j % 2]], ALU.mult)\
                        .then_inc(silu_scaled.sem, 1)
            if sf + base + 2 < n_slabs:
                split_lo(pool, base + 2 + s, (base + sf) % 2)

        def sync_step(sp, op, c, s, cf, sf, it):
            if sf + base + 4 < n_slabs:
                load_slab(sp, base + 4 + s, (base + sf) % 2)

        with nc.Block() as block:
            for eng, step in ((block.scalar, act_step), (block.vector, dve_step), (block.tensor, pe_step),
                              (block.gpsimd, pool_step), (block.sync, sync_step)):
                eng(lambda x, step=step: sequence(x, step))
        feed.advance()
        for c, n in ((gate_done, 4 if gated else 0), (gate_read, 4 if gated else 0),
                     (silu_done, 4 if gated else 0), (silu_scaled, 4 if gated else 0), (up_done, 4), (down_done, 16),
                     (relu_done, 0 if gated else 4), (square_done, 4), (hid_hi, 4), (hid_ready, 4), (bank_free, 16)):
            c.advance(n * n_chunks)
        slab_at[0] += total
        st.close()

    mlp(param("norm_ffn"), FF1_CHUNKS, False, "ff1")

    st = scope()
    final = sb(st, "final", [P, 4, SEQ])
    feed = Feed(None, x_tiles, None, dict(squares=final[:, 0:2], sum=final[:, 2], rstd=final[:, 3], rcol=None))
    with nc.Block() as block:
        @block.scalar
        def _(act):
            feed.act_squares(act)
            feed.act_root(act)

        @block.tensor
        def _(pe):
            feed.pe_sums(pe)

        @block.vector
        def _(dve):
            feed.dve_add_squares(dve)
            feed.dve_wait_root(dve)
            for k in range(KT):
                dve.scalar_tensor_tensor(out=xr[:, k], in0=xr[:, k], scalar=param("norm_final")[:, k:k + 1],
                                         in1=final[:, 3], op0=ALU.mult, op1=ALU.mult)
    feed.advance()
    st.close()
    m2 = scope()
    mix = sb(m2, "mix2", [P, 13, SEQ])
    zq, zk, c_a, c_g = mix[:, 0:2], mix[:, 2:4], mix[:, 6:8], mix[:, 8:10]
    zv = mix[:, 4:6].rearrange("p a n -> p (a n)").rearrange("p (t c) -> p t c", t=NB)
    attn_out = c_g
    st = scope()
    h = (sb(st, "h5_hi", [P, KT, SEQ], F32R), sb(st, "h5_lo", [P, KT, SEQ], F32R))
    rstd = sb(st, "h5_rstd", [P, SEQ])
    rcol = sb(st, "h5_rcol", [P, NB])

    def spill(sp):
        for k in range(KT):
            sp.dma_start(x_spill[:, k, :], xr[:, k, :]).then_inc(stored.sem, 16)

    dense(h, [dict(n=2, dst=mix[:, 0:4]), dict(n=1, dst=zv, token_major=True), dict(n=2, dst=mix[:, 6:10]),
              dict(n=4, dst=xr, wait=lambda dve: dve.wait_ge(stored.sem, stored.at(16 * KT)))],
          before=spill,
          feed=Feed(h, x_tiles, param("norm1_2"),
                    dict(squares=mix[:, 10:12], sum=mix[:, 12], rstd=rstd[:], rcol=rcol[:])))
    stored.advance(16 * KT)
    st.close()
    s_b, s_c, s_h = xr[:, 2:4], xr[:, 4:6], xr[:, 6:8]

    st = scope()
    tmp = sb(st, "m2_tmp", [P, 6, SEQ])
    edge = sb(st, "edge", [P, 2, 16])
    pw = sb(st, "pw", [P, 2, P])
    with nc.Block() as block:
        @block.sync
        def _(sp):
            sp.dma_start(edge[:].rearrange("p a n -> p (a n)"), const("pool_edge")).then_inc(loaded.sem, 16)
            sp.dma_start(pw[:].rearrange("p a n -> p (a n)"), pool_w).then_inc(loaded.sem, 16)
            sp.wait_ge(loaded.sem, loaded.at(32))

        @block.scalar
        def _(act):
            act.activation(c_g, c_g, ACT.Sigmoid).then_inc(a_step.sem, 1)
            for t in range(2):
                for hf in range(2):
                    act.wait_ge(p_step.sem, p_step.at(2 * t + hf + 1))
                    act.activation(xr[:, t, halves[hf]], ps[:, 2 * t + hf, :], ACT.Copy,
                                   scale=param("pool_scale")[:, t:t + 1])

        @block.gpsimd
        def _(pool):
            pool.tensor_tensor(s_c, s_c, s_h, ALU.mult)
            pool.wait_ge(a_step.sem, a_step.at(1))
            pool.tensor_tensor(c_a, c_a, c_g, ALU.mult)

        @block.vector
        def _(dve):
            n = [0]

            def then(ins):
                n[0] += 1
                ins.then_inc(v_step.sem, 1)
                dve.wait_ge(v_step.sem, v_step.at(n[0]))

            dve.wait_ge(loaded.sem, loaded.at(32))
            for t in range(2):
                u = xr[:, t]
                src, bufs = u, [tmp[:, 0], tmp[:, 1]]
                for d in range(4 if t else 2):
                    w, o = 2 ** d, bufs[d % 2]
                    then(dve.tensor_copy(o[:, 0:w], src[:, 0:w]))
                    then(dve.tensor_tensor(o[:, w:SEQ], src[:, w:SEQ], src[:, 0:SEQ - w], ALU.add))
                    src = o
                for half in range(2):
                    c = slice(64 * half, 64 * half + 64)
                    s = bufs[half]
                    then(dve.scalar_tensor_tensor(out=tmp[c, 2 + t, :], in0=s[c], scalar=edge[c, t, 15:16], in1=u[c],
                                                  op0=ALU.mult, op1=ALU.subtract))
                    then(dve.tensor_tensor(s[c, 0:16], s[c, 0:16], edge[c, t, :], ALU.mult))
                    then(dve.tensor_tensor(tmp[c, 2 + t, 0:16], s[c, 0:16], u[c, 0:16], ALU.subtract))

        @block.tensor
        def _(pe):
            for t in range(2):
                pe.wait_ge(v_step.sem, v_step.at(10 if t == 0 else 24))
                for hf in range(2):
                    pe.matmul(ps[:, 2 * t + hf, :], pw[:, t, :], tmp[:, 2 + t, halves[hf]], start=True, stop=True)\
                      .then_inc(p_step.sem, 1)
    loaded.advance(32)
    a_step.advance(1)
    v_step.advance(24)
    p_step.advance(4)
    conv(s_c, 2, param("sconv_w"), 3, tmp[:, 0:2], ACT.Copy)
    conv(c_a, 2, param("conf_dw_w"), CONF_K, tmp[:, 0:2], ACT.Identity, bias=param("conf_dw_b"))

    with nc.Block() as block:
        @block.gpsimd
        def _(pool):
            for hf in range(2):
                for t in range(2):
                    pool.wait_ge(v_step.sem, v_step.at(4 * hf + t + 1))
                    pool.tensor_tensor(tmp[:, t, halves[hf]], c_a[:, t, halves[hf]], c_a[:, t, halves[hf]],
                                       ALU.mult).then_inc(g_step.sem, 1)
            pool.tensor_tensor(s_c, s_c, s_b, ALU.mult)

        @block.tensor
        def _(pe):
            for hf in range(2):
                for t in range(2):
                    mm = pe.matmul(ps[:, hf, :], ones[:], c_a[:, t, halves[hf]], start=(t == 0), stop=(t == 1))
                mm.then_inc(p_step.sem, 1)
            for hf in range(2):
                for t in range(2):
                    pe.wait_ge(g_step.sem, g_step.at(2 * hf + t + 1))
                    mm = pe.matmul(ps[:, 2 + hf, :], ones[:], tmp[:, t, halves[hf]], start=(t == 0), stop=(t == 1))
                mm.then_inc(p_step.sem, 1)

        @block.vector
        def _(dve):
            for hf in range(2):
                dve.wait_ge(p_step.sem, p_step.at(hf + 1))
                for t in range(2):
                    dve.scalar_tensor_tensor(out=c_a[:, t, halves[hf]], in0=ps[:, hf, :], scalar=-1.0 / 256,
                                             in1=c_a[:, t, halves[hf]], op0=ALU.mult, op1=ALU.add)\
                       .then_inc(v_step.sem, 1)
                dve.wait_ge(rstd_done.sem, rstd_done.at(hf + 1))
                for t in range(2):
                    dve.scalar_tensor_tensor(out=c_a[:, t, halves[hf]], in0=c_a[:, t, halves[hf]],
                                             scalar=param("conf_ln_g")[:, t:t + 1], in1=tmp[:, 2, halves[hf]],
                                             op0=ALU.mult, op1=ALU.mult).then_inc(v_step.sem, 1)

        @block.scalar
        def _(act):
            for hf in range(2):
                r = tmp[:, 2, halves[hf]]
                act.wait_ge(p_step.sem, p_step.at(3 + hf))
                act.activation(r, ps[:, 2 + hf, :], ACT.Ln, scale=1.0 / 256, bias=eps_col).then_inc(log_done.sem, 1)
                act.wait_ge(log_done.sem, log_done.at(hf + 1))
                act.activation(r, r, ACT.Exp, scale=-0.5).then_inc(rstd_done.sem, 1)
            for hf in range(2):
                act.wait_ge(v_step.sem, v_step.at(4 * hf + 4))
                for t in range(2):
                    z = c_a[:, t, halves[hf]]
                    act.activation(z, z, ACT.Silu, bias=param("conf_ln_b")[:, t:t + 1])
    g_step.advance(4)
    p_step.advance(4)
    v_step.advance(8)
    log_done.advance(2)
    rstd_done.advance(2)
    st.close()

    st = scope()
    tmp = sb(st, "at_tmp", [P, 2, SEQ])
    causal = sb(st, "causal", [P, P])
    hot = sb(st, "hot", [P, 384])
    rel = sb(st, "rel", [P, HEADS, P])
    table = sb(st, "table", [P, HEADS, 400])
    bias = sb(st, "bias", [P, HEADS, 256])
    ones32 = sb(st, "ones32", [P, P])
    ones64 = sb(st, "ones64", [P, P])
    lam = sb(st, "lam", [P, 80])
    neg_lam, q_gain, o_gain = lam[:, 70:71], lam[:, 71:72], lam[:, 72:73]
    with nc.Block() as block:
        @block.sync
        def _(sp):
            for dst, name in ((causal, "causal"), (hot, "onehot"), (ones32, "ones32"), (ones64, "ones64")):
                sp.dma_start(dst[:], const(name)).then_inc(loaded.sem, 16)
            sp.wait_ge(v_step.sem, v_step.at(3))
            sp.dma_start(bias_skew.rearrange("h p n -> p h n"), table[:]).then_inc(stored.sem, 16)
            sp.wait_ge(stored.sem, stored.at(16))
            for hd in range(HEADS):
                skewed = bias_skew[hd].rearrange("p n -> (p n)")[127:127 + P * 399]\
                    .rearrange("(p n) -> p n", n=399)[:, 0:256]
                sp.dma_start(bias[:, hd, :], skewed).then_inc(loaded.sem, 16)
            sp.wait_ge(loaded.sem, loaded.at(16 * 8))

        @block.vector
        def _(dve):
            lam_v = param("lam").rearrange("p (a b n) -> p a b n", a=2, b=2)
            prod = lam[:, 0:64].rearrange("p (a n) -> p a n", a=2)
            dve.memset(table[:], 0.0).then_inc(v_step.sem, 1)
            dve.wait_ge(v_step.sem, v_step.at(1))
            dve.tensor_copy(rel[0:32], param("rel_bias")[0:32].unsqueeze(2).to_broadcast([32, HEADS, P]))\
               .then_inc(v_step.sem, 1)
            for hd in range(HEADS):
                dve.wait_ge(p_step.sem, p_step.at(hd + 1))
                dve.tensor_copy(lam[:, 74 + hd:75 + hd], ps[:, hd, 0:1]).then_inc(value_done.sem, 1)
                dve.wait_ge(value_done.sem, value_done.at(hd + 1))
                last = dve.tensor_scalar(table[:, hd, 0:384], ps[:, hd, 0:384], lam[:, 74 + hd:75 + hd], None,
                                         ALU.subtract)
            last.then_inc(v_step.sem, 1)
            dve.tensor_tensor(prod, lam_v[:, :, 0], lam_v[:, :, 1], ALU.mult).then_inc(v_step.sem, 1)
            dve.wait_ge(v_step.sem, v_step.at(4))
            dve.tensor_reduce(lam[:, 64:66], prod, AX.X, ALU.add).then_inc(v_step.sem, 1)
            dve.tensor_scalar(q_gain, param("q_norm"), QK2 ** -0.5, None, ALU.mult)
            dve.tensor_scalar(o_gain, param("subln"), 1.0 - LAM_INIT, None, ALU.mult)
            dve.wait_ge(a_step.sem, a_step.at(1))
            dve.tensor_tensor(lam[:, 68:69], lam[:, 67:68], lam[:, 66:67], ALU.subtract).then_inc(v_step.sem, 1)
            dve.wait_ge(v_step.sem, v_step.at(6))
            dve.tensor_scalar(neg_lam, lam[:, 68:69], -LAM_INIT, None, ALU.add)
            dve.wait_ge(loaded.sem, loaded.at(16 * 8))
            d = bias[:, :, P:2 * P]
            dve.tensor_tensor(d, d, causal[:].unsqueeze(1).to_broadcast([P, HEADS, P]), ALU.add)

        @block.scalar
        def _(act):
            act.wait_ge(v_step.sem, v_step.at(5))
            act.activation(lam[:, 66:68], lam[:, 64:66], ACT.Exp).then_inc(a_step.sem, 1)

        @block.tensor
        def _(pe):
            pe.wait_ge(loaded.sem, loaded.at(64))
            pe.wait_ge(v_step.sem, v_step.at(2))
            for hd in range(HEADS):
                pe.matmul(ps[:, hd, 0:384], rel[0:32, hd, :], hot[0:32, :], start=True, stop=True)\
                  .then_inc(p_step.sem, 1)
    loaded.advance(16 * 8)
    stored.advance(16)
    v_step.advance(6)
    value_done.advance(4)
    a_step.advance(1)
    p_step.advance(4)
    norm_units([dict(src=z[:, t, c], out=z[:, t, c], scale=1.0 / QK2, gain=g)
                for z, g in ((zq, q_gain), (zk, param("k_norm"))) for t in range(2) for c in halves],
               ones32[:], tmp)

    q_p = sb(st, "q_p", [P, SEQ])
    k_p = sb(st, "k_p", [P, SEQ])
    v_p = sb(st, "v_p", [P, NB, P])
    bias_p = sb(st, "bias_p", [P, 2, 256])
    prob = [sb(st, f"diff_prob{b}", [P, 2, SEQ]) for b in range(2)]
    a_t = sb(st, "a_t", [P, 2, NB, P])
    stat = sb(st, "diff_stat", [P, 2, 2, 4])
    units = [(hd, qb) for hd in range(2) for qb in range(NB)]
    NU = len(units)
    turn_groups = [(qb + 4) // 4 for _, qb in units]
    turns_before = [sum(turn_groups[:u]) for u in range(NU + 1)]
    NT = turns_before[-1]
    with nc.Block() as block:
        @block.sync
        def _(sp):
            with sp.Fori(0, 2) as it:
                sp.wait_ge(d_stored.sem, d_stored.at(it * NU))
                for dst, src in ((q_p[:], zq[:, bass.ds(it, 1), :].rearrange("p o n -> p (o n)")),
                                 (k_p[:], zk[:, bass.ds(it, 1), :].rearrange("p o n -> p (o n)")),
                                 (v_p[:], zv[:, :, bass.ds(it * P, P)]),
                                 (bias_p[:], bias[:, bass.ds(it * 2, 2), :])):
                    sp.dma_start(dst, src).then_inc(pair_loaded.sem, 16)

        @block.tensor
        def _(pe):
            with pe.Fori(0, 2) as it:
                pe.wait_ge(pair_loaded.sem, pair_loaded.at(it * 64 + 64))

                def scores(u):
                    hd, qb = units[u]
                    w = (qb + 1) * P
                    for m in range(2):
                        pe.wait_ge(d_exp.sem, d_exp.at(it * 2 * NU + (2 * (u - 1) + m + 1 if u else 0)))
                        r = slice(64 * hd + 32 * m, 64 * hd + 32 * m + 32)
                        for a in range(0, w, HALF):
                            b = min(w, a + HALF)
                            mm = pe.matmul(ps[:, 2 * m + a // HALF, 0:b - a], q_p[r, qb * P:(qb + 1) * P],
                                           k_p[r, a:b], start=True, stop=True)
                        mm.then_inc(d_scores.sem, 1)

                def outputs(u):
                    hd, qb = units[u]
                    pe.wait_ge(d_copied.sem, d_copied.at(it * NT + turns_before[u + 1]))
                    pe.wait_ge(d_stored.sem, d_stored.at(it * NU + max(u - 1, 0)))
                    for kb in range(qb + 1):
                        mm = pe.matmul(ps[64 * hd:64 * hd + 64, 6 + u % 2, 0:P], v_p[:, kb, 64 * hd:64 * hd + 64],
                                       a_t[:, u % 2, kb, :], start=(kb == 0), stop=(kb == qb))
                    mm.then_inc(d_out.sem, 1)

                scores(0)
                for u, (hd, qb) in enumerate(units):
                    if u + 1 < NU:
                        scores(u + 1)
                    pe.wait_ge(d_diff.sem, d_diff.at(it * NU + u + 1))
                    for a in range(0, qb + 1, 4):
                        n = turns_before[u] + a // 4
                        pe.wait_ge(d_copied.sem, d_copied.at(it * NT + max(n - 1, 0)))
                        for kb in range(a, min(a + 4, qb + 1)):
                            mm = pe.transpose(ps[:, 4 + n % 2, (kb - a) * P:(kb - a + 1) * P],
                                              prob[u % 2][:, 0, kb * P:(kb + 1) * P], ident[:])
                        mm.then_inc(d_turned.sem, 1)
                    if u:
                        outputs(u - 1)
                outputs(NU - 1)

        @block.vector
        def _(dve):
            with dve.Fori(0, 2) as it:
                def soft(u):
                    hd, qb = units[u]
                    w, near = (qb + 1) * P, min(qb + 1, 2) * P
                    for m in range(2):
                        n = it * 2 * NU + 2 * u + m + 1
                        sc = ps[:, 2 * m:2 * m + 2, :].rearrange("p a n -> p (a n)")
                        dve.wait_ge(d_scores.sem, d_scores.at(n))
                        dve.wait_ge(pair_loaded.sem, pair_loaded.at(it * 64 + 64))
                        dve.tensor_tensor(sc[:, w - near:w], sc[:, w - near:w], bias_p[:, hd, 256 - near:256],
                                          ALU.add).then_inc(d_biased.sem, 1)
                        dve.wait_ge(d_biased.sem, d_biased.at(n))
                        dve.tensor_reduce(stat[:, u % 2, m, 0:1], sc[:, 0:w], AX.X, ALU.max, negate=True)\
                           .then_inc(d_max.sem, 1)

                def combine(u):
                    hd, qb = units[u]
                    w = (qb + 1) * P
                    s = stat[:, u % 2]
                    dve.wait_ge(d_exp.sem, d_exp.at(it * 2 * NU + 2 * u + 2))
                    dve.reciprocal(s[:, :, 2:3], s[:, :, 1:2]).then_inc(d_inv.sem, 1)
                    dve.wait_ge(d_inv.sem, d_inv.at(it * NU + u + 1))
                    dve.tensor_scalar(s[:, 1, 3:4], s[:, 1, 2:3], neg_lam, None, ALU.mult).then_inc(d_inv2.sem, 1)
                    dve.wait_ge(d_inv2.sem, d_inv2.at(it * NU + u + 1))
                    dve.tensor_scalar(prob[u % 2][:, 1, 0:w], prob[u % 2][:, 1, 0:w], s[:, 1, 3:4], None, ALU.mult)\
                       .then_inc(d_scaled.sem, 1)
                    dve.wait_ge(d_scaled.sem, d_scaled.at(it * NU + u + 1))
                    dve.scalar_tensor_tensor(out=prob[u % 2][:, 0, 0:w], in0=prob[u % 2][:, 0, 0:w],
                                             scalar=s[:, 0, 2:3], in1=prob[u % 2][:, 1, 0:w],
                                             op0=ALU.mult, op1=ALU.add).then_inc(d_diff.sem, 1)

                def store(u):
                    hd, qb = units[u]
                    r = slice(64 * hd, 64 * hd + 64)
                    dve.wait_ge(d_out.sem, d_out.at(it * NU + u + 1))
                    dve.tensor_copy(attn_out[r, bass.ds(it, 1), qb * P:(qb + 1) * P].rearrange("p o n -> p (o n)"),
                                    ps[r, 6 + u % 2, 0:P]).then_inc(d_stored.sem, 1)

                soft(0)
                for u in range(NU):
                    combine(u)
                    if u + 1 < NU:
                        soft(u + 1)
                    if u >= 2:
                        store(u - 2)
                store(NU - 2)
                store(NU - 1)

        @block.scalar
        def _(act):
            with act.Fori(0, 2) as it:
                def exps(u):
                    hd, qb = units[u]
                    w = (qb + 1) * P
                    for m in range(2):
                        sc = ps[:, 2 * m:2 * m + 2, :].rearrange("p a n -> p (a n)")
                        act.wait_ge(d_max.sem, d_max.at(it * 2 * NU + 2 * u + m + 1))
                        act.wait_ge(d_turned.sem, d_turned.at(it * NT + (turns_before[u - 1] if u >= 2 else 0)))
                        act.activation(prob[u % 2][:, m, 0:w], sc[:, 0:w], ACT.Exp, bias=stat[:, u % 2, m, 0:1],
                                       accum_out=stat[:, u % 2, m, 1:2]).then_inc(d_exp.sem, 1)

                exps(0)
                for u, (hd, qb) in enumerate(units):
                    if u + 1 < NU:
                        exps(u + 1)
                    act.wait_ge(d_out.sem, d_out.at(it * NU + max(u - 1, 0)))
                    for a in range(0, qb + 1, 4):
                        n = turns_before[u] + a // 4
                        b = min(a + 4, qb + 1)
                        act.wait_ge(d_turned.sem, d_turned.at(it * NT + n + 1))
                        act.activation(a_t[:, u % 2, a:b, :].rearrange("p a n -> p (a n)"),
                                       ps[:, 4 + n % 2, 0:(b - a) * P], ACT.Copy).then_inc(d_copied.sem, 1)
    norm_units([dict(src=attn_out[:, t, c], out=attn_out[:, t, c], scale=1.0 / HV2, gain=o_gain)
                for t in range(2) for c in halves], ones64[:], tmp, wide=True)
    st.close()

    y_stack = scope()
    y = (sb(y_stack, "y3_hi", [P, KT, SEQ], F32R), sb(y_stack, "y3_lo", [P, KT, SEQ], F32R))
    parts = [xr[:, 0], xr[:, 1], s_c[:, 0], s_c[:, 1], c_a[:, 0], c_a[:, 1], attn_out[:, 0], attn_out[:, 1]]
    start, wait = reload_x(x_spill)
    dense(y, [dict(n=4, dst=xr, add=True, wait=wait)], before=start, feed=Feed(y, parts))
    loaded.advance(16 * KT)
    y_stack.close()
    m2.close()

    mlp(param("norm2_2"), FF2_CHUNKS, True, "ff2")
    with nc.Block() as block:
        @block.sync
        def _(sp):
            for k in range(KT):
                sp.dma_start(out_t[:, k, :], xr[:, k, :]).then_inc(stored.sem, 16)
            sp.wait_ge(stored.sem, stored.at(16 * KT))


def slab_up(w, c):
    return w[:, c:c + CB].reshape(KT, P, CB).transpose(1, 0, 2).reshape(P, SLAB)


def slab_down(w, r):
    return w[r:r + CB].reshape(2, P, D).transpose(1, 0, 2).reshape(P, SLAB)


def feature_columns(v, n):
    return np.reshape(v, (n, P)).T


def lay_out(a):
    a = {k: np.asarray(v) for k, v in a.items()}
    m = {k: (v[0] if v.ndim > 1 and v.shape[0] == 1 else v) for k, v in a.items()}

    def ups(w, c0=0, c1=None):
        return [slab_up(w, c) for c in range(c0, w.shape[1] if c1 is None else c1, CB)]

    slabs = ups(m["w_in"], 0, 3072)
    for name in ("w_out", "xa_wk", "xa_wv", "xa_wq", "xa_wo"):
        slabs += ups(m[name])
    up, down = ups(m["ffn_w1"]), [slab_down(m["ffn_w2"], r) for r in range(0, 4096, CB)]
    slabs.append(up[0])
    for c in range(1, FF1_CHUNKS):
        slabs += [up[c], down[c - 1]]
    slabs.append(down[-1])
    pool, s_b, s_c, s_h, c_a, c_g, zq, zk, zv = ups(m["w_in_2"])
    slabs += [zq, zk, zv, c_a, c_g, pool, s_b, s_c, s_h] + ups(m["w_out_2"])
    gate, up = ups(m["w_gate_2"]), ups(m["w_up_2"])
    down = [slab_down(m["w_down_2"], r) for r in range(0, 2816, CB)]
    slabs += [gate[0], up[0]]
    for c in range(1, FF2_CHUNKS):
        slabs += [gate[c], up[c], down[c - 1]]
    slabs.append(down[-1])

    params = np.zeros((P, N_PARAMS), np.float32)

    def put(name, v):
        lo, hi = PARAM_COLS[name]
        params[:v.shape[0], lo:hi] = v

    for name, src in (("norm_mix", "norm_mix"), ("norm_xa", "norm_xa"), ("norm_mem", "norm_mem"),
                      ("norm_ffn", "norm_ffn"), ("norm_final", "norm_final"), ("norm1_2", "norm1_g_2"),
                      ("norm2_2", "norm2_g_2")):
        put(name, feature_columns(m[src], 8))
    put("gm_ln_g", m["gm_ln_g"].T)
    put("dn_conv", m["dn_conv"].reshape(CONV_W, 12, P).transpose(2, 1, 0).reshape(P, 48))
    put("dn_a_log", np.tile(np.reshape(m["dn_a_log"], (1, 4)), (P, 1)))
    put("dn_dt_bias", np.tile(np.reshape(m["dn_dt_bias"], (1, 4)), (P, 1)))
    put("dn_onorm", np.reshape(m["dn_onorm"], (P, 1)))
    put("w_logits", m["w_in"][:, 3072:3080].reshape(KT, P, 8).transpose(1, 0, 2).reshape(P, 64))
    put("pool_scale", feature_columns(m["pool_scale_2"], 2))
    put("sconv_w", m["sconv_w_2"].reshape(3, 2, P).transpose(2, 1, 0).reshape(P, 6))
    put("conf_dw_w", m["conf_dw_w_2"].reshape(CONF_K, 2, P).transpose(2, 1, 0).reshape(P, 62))
    put("conf_dw_b", feature_columns(m["conf_dw_b_2"], 2))
    put("conf_ln_g", feature_columns(m["conf_ln_g_2"], 2))
    put("conf_ln_b", feature_columns(m["conf_ln_b_2"], 2))
    put("q_norm", np.tile(np.reshape(m["q_norm_g_2"], (QK2, 1)), (4, 1)))
    put("k_norm", np.tile(np.reshape(m["k_norm_g_2"], (QK2, 1)), (4, 1)))
    put("subln", np.tile(np.reshape(m["subln_g_2"], (HV2, 1)), (2, 1)))
    put("lam", np.tile(np.concatenate([np.reshape(m[n], (1, QK2)) for n in
                                       ("lam_q1_2", "lam_k1_2", "lam_q2_2", "lam_k2_2")], 1), (P, 1)))
    put("rel_bias", m["rel_bias_2"])

    pool_w = np.zeros((P, 2, P), np.float32)
    for g in range(4):
        o = (g % 2) * 64
        pool_w[o:o + 64, g // 2, o:o + 64] = m["pool_w_2"][g]
    return {
        "x_t": m["x"].T.reshape(KT, P, SEQ).transpose(1, 0, 2),
        "mem_t": m["mem"].T.reshape(KT, P, MEM).transpose(1, 0, 2),
        "slabs": np.stack(slabs),
        "params": params,
        "row_params": np.concatenate([m["gm_ln_b"].reshape(1, 512), m["gm_bs"].reshape(1, 512)], 1),
        "gm_ws_t": m["gm_ws"].transpose(2, 0, 1).reshape(P, 512),
        "pool_w": pool_w.reshape(P, 2 * P),
        "consts": constant_tables(),
    }


def kernel(**inputs):
    import concourse.bacc as bacc
    from concourse.bass_utils import run_bass_kernel_spmd

    arrays = {f"in_{k}_dram": np.ascontiguousarray(v) for k, v in lay_out(inputs).items()}
    nc = bacc.Bacc("TRN2", target_bir_lowering=False, num_devices=1)
    ins = {k[3:-5]: nc.dram_tensor(k, v.shape, F32, kind="ExternalInput").ap() for k, v in arrays.items()}
    out_t = nc.dram_tensor("out_0_dram", (P, KT, SEQ), F32, kind="ExternalOutput").ap()
    x_spill = nc.dram_tensor("x_spill", (P, KT, SEQ), F32, kind="Internal").ap()
    bias_skew = nc.dram_tensor("bias_skew", (HEADS, P, 400), F32, kind="Internal").ap()
    with ExitStack() as main:
        build(nc, main, **ins, x_spill=x_spill, bias_skew=bias_skew, out_t=out_t)
    r = run_bass_kernel_spmd(nc, [arrays], core_ids=[0])
    return np.ascontiguousarray(r.results[0]["out_0_dram"].transpose(2, 1, 0).reshape(1, SEQ, D))
```

```python
from contextlib import ExitStack

import numpy as np

import concourse.bass as bass
from concourse import mybir

F32 = mybir.dt.float32
F32R = mybir.dt.float32r
ALU = mybir.AluOpType
ACT = mybir.ActivationFunctionType
AX = mybir.AxisListType

P = 128
D = 1024
KT = D // P
SEQ = 1024
HALF = 512
NB = SEQ // P
MEM = 256
EPS = 1e-6
CB = 256
SLAB = KT * CB
HEADS = 4
CONV_W = 4
FF1_CHUNKS = 4096 // CB
FF2_CHUNKS = 2816 // CB
XA_D = 256
LAM_INIT = 0.2
POOL_WINDOWS = (2, 4, 8, 16)
CONF_K = 31
QK2 = 32
HV2 = 64

PARAM_COLS = {}
_at = 0
for _name, _n in [("norm_mix", 8), ("norm_xa", 8), ("norm_mem", 8), ("norm_ffn", 8), ("norm_final", 8),
                  ("norm1_2", 8), ("norm2_2", 8), ("gm_ln_g", 4), ("dn_conv", 48), ("dn_a_log", 4),
                  ("dn_dt_bias", 4), ("dn_onorm", 1), ("w_logits", 64), ("pool_scale", 2), ("sconv_w", 6),
                  ("conf_dw_w", 62), ("conf_dw_b", 2), ("conf_ln_g", 2), ("conf_ln_b", 2), ("q_norm", 1),
                  ("k_norm", 1), ("subln", 1), ("lam", 128), ("rel_bias", 4)]:
    PARAM_COLS[_name] = (_at, _at + _n)
    _at += _n
N_PARAMS = _at

CONST_COLS = {}
_at = 0
for _name, _n in [("ident", 128), ("tri", 128), ("strict", 128), ("levels", 7 * 128), ("ones32", 128),
                  ("ones64", 128), ("pool_edge", 32), ("onehot", 384), ("causal", 128)]:
    CONST_COLS[_name] = (_at, _at + _n)
    _at += _n
N_CONSTS = _at


def constant_tables():
    c = np.zeros((P, N_CONSTS), np.float32)
    i = np.arange(P)

    def put(name, a):
        lo, hi = CONST_COLS[name]
        c[:a.shape[0], lo:hi] = a

    put("ident", np.eye(P))
    put("tri", (i[:, None] <= i[None, :]) * 1.0)
    put("strict", (i[:, None] < i[None, :]) * 1.0)
    lev = [((i[None, :] >> (l + 1)) == (i[:, None] >> (l + 1))) & ((i[None, :] >> l & 1) == 1)
           & ((i[:, None] >> l & 1) == 0) for l in range(7)]
    put("levels", np.stack(lev, 1).reshape(P, 7 * P) * 1.0)
    put("ones32", (i[:, None] // 32 == i[None, :] // 32) * 1.0)
    put("ones64", (i[:, None] // 64 == i[None, :] // 64) * 1.0)
    edge = np.zeros((P, 2, 16))
    for g, win in enumerate(POOL_WINDOWS):
        for t in range(16):
            edge[(g % 2) * 64:(g % 2) * 64 + 64, g // 2, t] = 1.0 / min(t + 1, win)
    put("pool_edge", edge.reshape(P, 32))
    n = np.maximum(255 - np.arange(384), 0)
    large = 16 + (np.log(np.maximum(n, 1).astype(np.float32) / np.float32(16)) / np.float32(np.log(8.0))
                  * np.float32(16)).astype(np.int32)
    bucket = np.where(n < 16, n, np.minimum(large, 31))
    put("onehot", (np.arange(32)[:, None] == bucket[None, :]) * 1.0)
    put("causal", np.where(i[:, None] >= i[None, :], 0.0, -1e30))
    return c


class Count:

    def __init__(self, sem, base=0):
        self.sem, self.base = sem, base

    def at(self, n):
        return self.base + n

    def advance(self, n):
        self.base += n


def build(nc, main, x_t, mem_t, slabs, params, row_params, gm_ws_t, pool_w, consts, x_spill, bias_skew, out_t):
    def sb(stack, name, shape, dt=F32):
        return stack.enter_context(nc.sbuf_tensor(name, shape, dt))

    counters = []

    def counter(name, start=1):
        counters.append(Count(main.enter_context(nc.semaphore(name)), start))
        return counters[-1]

    slab_raw = sb(main, "slab_raw", [P, 2, SLAB])
    slab_hi = sb(main, "slab_hi", [P, 2, SLAB], F32R)
    slab_lo = sb(main, "slab_lo", [P, 2, SLAB], F32R)
    ident = sb(main, "ident", [P, P])
    ones = sb(main, "ones", [P, P])
    par = sb(main, "par", [P, N_PARAMS])
    eps_tile = sb(main, "eps_tile", [P, 1])
    eps_col = eps_tile[:]
    xr = sb(main, "xr", [P, KT, SEQ])

    ps = main.enter_context(nc.psum_tensor("ps", [P, 8, HALF], F32))

    def param(name):
        a, b = PARAM_COLS[name]
        return par[:, a:b]

    def const(name):
        a, b = CONST_COLS[name]
        return consts[:, a:b]

    slab_loaded = [counter("slab_loaded0", 0), counter("slab_loaded1", 0)]
    slab_hi_done = counter("slab_hi_done", 0)
    slab_split = counter("slab_split", 0)
    group_done = counter("group_done")
    bank_free = counter("bank_free", 9)
    loaded = counter("loaded", 0)
    stored = counter("stored")
    sq_ready = counter("sq_ready")
    sum_done = counter("sum_done")
    log_done = counter("log_done")
    rstd_done = counter("rstd_done")
    value_done = counter("value_done")
    hi_done = counter("hi_done")
    lo_done = counter("lo_done")
    a_step = counter("a_step")
    v_step = counter("v_step")
    g_step = counter("g_step")
    p_step = counter("p_step")
    bias_step = counter("bias_step")
    conv_started = counter("conv_started")
    tap_done = counter("tap_done")
    conv_done = counter("conv_done")

    def pair(name):
        return [counter(f"{name}{s}") for s in range(2)]

    block_loaded = pair("block_loaded")
    gtri_ready = pair("gtri_ready")
    rows_done = pair("rows_done")
    grams_done = pair("grams_done")
    arg_ready = pair("arg_ready")
    exp_done = pair("exp_done")
    raw_done = pair("raw_done")
    masked = pair("masked")
    turned = pair("turned")
    by_token = pair("by_token")
    level_ready = pair("level_ready")
    tt_ready = pair("tt_ready")
    first_turned = pair("first_turned")
    t_ready = pair("t_ready")
    x_done = pair("x_done")
    x_ready = pair("x_ready")
    prod_done = pair("prod_done")
    ks_done, resid_ready, tr_done, vnew_ready, step_done, state_ready, o_done, o_ready = (
        counter(n) for n in
        ("ks_done", "resid_ready", "tr_done", "vnew_ready", "step_done", "state_ready", "o_done", "o_ready"))
    xa_head_loaded = pair("xa_head_loaded")
    xa_v_loaded = pair("xa_v_loaded")
    (xa_score_done, xa_max_done, xa_bias_done, xa_exp_done, xa_inv_done, xa_p_ready, xa_pt_done, xa_pt_ready,
     xa_o_done) = (
        counter(n) for n in ("xa_score_done", "xa_max_done", "xa_bias_done", "xa_exp_done", "xa_inv_done",
                             "xa_p_ready", "xa_pt_done", "xa_pt_ready", "xa_o_done"))
    xa_o_copied = counter("xa_o_copied", 5)
    d_head_loaded = [counter("d_head_loaded0"), counter("d_head_loaded1")]
    d_scores = counter("d_scores", 1 + 2 * NB)
    (pair_loaded, pair_v_loaded, d_biased, d_max, d_exp, d_inv, d_inv2, d_diff, d_turned,
     d_copied, d_out, d_stored) = (
        counter(n) for n in ("pair_loaded", "pair_v_loaded", "d_biased", "d_max", "d_exp", "d_inv",
                             "d_inv2", "d_diff", "d_turned", "d_copied", "d_out", "d_stored"))
    (gate_done, up_done, down_done, gate_read, silu_done, silu_scaled, relu_done, square_done, hid_hi, hid_ready) = (
        counter(n) for n in ("gate_done", "up_done", "down_done", "gate_read", "silu_done", "silu_scaled",
                             "relu_done", "square_done", "hid_hi", "hid_ready"))
    final_squared, final_added, final_summed, final_log, final_rooted, final_written = (
        counter(n) for n in ("final_squared", "final_added", "final_summed", "final_log", "final_rooted",
                             "final_written"))
    n_slabs = slabs.shape[0]

    def load_slab(sp, g, slot, check=True):
        if check:
            sp.wait_ge(slab_split.sem, g - 1)
        sp.dma_start(slab_raw[:, slot, :], slabs[bass.ds(g, 1)].rearrange("o p n -> p (o n)"))\
          .then_inc(slab_loaded[slot].sem, 16)

    def split_hi(act, g, g_half, slot):
        act.wait_ge(slab_loaded[slot].sem, 16 * g_half + 16)
        act.activation(slab_hi[:, slot, :], slab_raw[:, slot, :], ACT.Copy).then_inc(slab_hi_done.sem, 1)

    def split_lo(pool, g, slot):
        pool.wait_ge(slab_hi_done.sem, g + 1)
        pool.tensor_tensor(slab_lo[:, slot, :], slab_raw[:, slot, :], slab_hi[:, slot, :].bitcast(F32),
                           ALU.subtract).then_inc(slab_split.sem, 1)

    PASSES = ((0, 0), (0, 1), (1, 0))

    def slab_of(part, slot):
        return (slab_hi, slab_lo)[part][:, slot, :]

    halves = [slice(0, HALF), slice(HALF, SEQ)]

    starts = [(c, c.base) for c in counters]

    with nc.Block() as block:
        @block.sync
        def _(sp):
            sp.dma_start(ident[:], const("ident")).then_inc(loaded.sem, 16)
            sp.dma_start(par[:], params).then_inc(loaded.sem, 16)
            load_slab(sp, 0, 0, check=False)
            for k in range(KT):
                sp.dma_start(xr[:, k, :], x_t[:, k, :]).then_inc(loaded.sem, 16)
            for g in (1, 2):
                load_slab(sp, g, g % 2, check=g >= 2)
            sp.wait_ge(loaded.sem, 16 * (2 + KT))

        @block.scalar
        def _(act):
            split_hi(act, 0, 0, 0)

        @block.gpsimd
        def _(pool):
            pool.memset(ones[:], 1.0)
            pool.memset(eps_tile[:], EPS)
            split_lo(pool, 0, 0)

        @block.tensor
        def _(pe):
            for c, start in starts:
                if start:
                    pe.sem_inc(c.sem, start)
    loaded.advance(16 * (2 + KT))

    class Feed:

        def __init__(self, dst, src, gain=None, norm=None, tokens=SEQ, late=None):
            self.dst, self.src, self.gain, self.norm, self.tokens, self.late = dst, src, gain, norm, tokens, late
            self.w = min(tokens, HALF)
            self.n_half = tokens // self.w
            self.parts = self.n_half + (1 if norm and norm["rcol"] is not None else 0)

        def when_late(self, eng, name, k):
            if self.late:
                if k == self.late["first"]:
                    self.late[name](eng)
                if k >= self.late["first"]:
                    self.late["ready"](eng, k)

        def act_split(self, act):
            for k in range(KT):
                self.when_late(act, "act", k)
                act.activation(self.dst[0][:, k, :], self.src[k], ACT.Copy,
                               scale=1.0 if self.gain is None else self.gain[:, k:k + 1]).then_inc(hi_done.sem, 1)

        def act_squares(self, act):
            for k in range(KT):
                if k >= 2:
                    act.wait_ge(value_done.sem, value_done.at(max(k - 2, 1)))
                act.activation(self.norm["squares"][:, k % 2, :], self.src[k], ACT.Square).then_inc(sq_ready.sem, 1)

        def act_root(self, act):
            rstd, rcol = self.norm["rstd"], self.norm["rcol"]
            for hf in range(self.n_half):
                act.wait_ge(sum_done.sem, sum_done.at(hf + 1))
                act.activation(rstd[:, hf * self.w:(hf + 1) * self.w], ps[:, 6 + hf, 0:self.w], ACT.Ln,
                               scale=1.0 / D, bias=eps_col).then_inc(log_done.sem, 1)
            if rcol is not None:
                act.wait_ge(sum_done.sem, sum_done.at(self.parts))
                act.activation(rcol, ps[:, 5, 0:self.tokens // P], ACT.Ln, scale=1.0 / D, bias=eps_col)\
                   .then_inc(log_done.sem, 1)
            act.wait_ge(log_done.sem, log_done.at(self.parts))
            act.activation(rstd, rstd, ACT.Exp, scale=-0.5).then_inc(rstd_done.sem, 1)
            if rcol is not None:
                act.activation(rcol, rcol, ACT.Exp, scale=-0.5).then_inc(rstd_done.sem, 1)

        def dve_split(self, dve):
            for k in range(KT):
                self.when_late(dve, "dve", k)
                dve.wait_ge(hi_done.sem, hi_done.at(k + 1))
                lo, hi = self.dst[1][:, k, :], self.dst[0][:, k, :].bitcast(F32)
                if self.gain is None:
                    dve.tensor_tensor(lo, self.src[k], hi, ALU.subtract).then_inc(lo_done.sem, 1)
                else:
                    dve.scalar_tensor_tensor(out=lo, in0=self.src[k], scalar=self.gain[:, k:k + 1], in1=hi,
                                             op0=ALU.mult, op1=ALU.subtract).then_inc(lo_done.sem, 1)
            if self.norm:
                self.dve_add_squares(dve)

        def dve_add_squares(self, dve):
            sq, total = self.norm["squares"], self.norm["sum"]
            for k in range(1, KT):
                dve.wait_ge(sq_ready.sem, sq_ready.at(k + 1))
                if k > 1:
                    dve.wait_ge(value_done.sem, value_done.at(k - 1))
                dve.tensor_tensor(total, sq[:, 0, :] if k == 1 else total, sq[:, k % 2, :], ALU.add)\
                   .then_inc(value_done.sem, 1)

        def dve_wait_root(self, dve):
            if self.norm:
                dve.wait_ge(rstd_done.sem, rstd_done.at(1 if self.norm["rcol"] is None else 2))

        def pe_sums(self, pe):
            total = self.norm["sum"]
            pe.wait_ge(value_done.sem, value_done.at(KT - 1))
            for hf in range(self.n_half):
                pe.matmul(ps[:, 6 + hf, 0:self.w], ones[:], total[:, hf * self.w:(hf + 1) * self.w],
                          start=True, stop=True).then_inc(sum_done.sem, 1)
            if self.norm["rcol"] is not None:
                for t in range(self.tokens // P):
                    mm = pe.matmul(ps[:, 5, t:t + 1], total[:, t * P:(t + 1) * P], ones[:, 0:1], start=True, stop=True)
                mm.then_inc(sum_done.sem, 1)

        def pe_wait_sums_read(self, pe):
            if self.norm:
                pe.wait_ge(log_done.sem, log_done.at(self.parts))

        def pe_first(self, pe, slot, outputs, done):
            cuts = [0, self.late["pe_after"], self.late["first"], KT] if self.late else [0, KT]
            for n, (a, b) in enumerate(zip(cuts, cuts[1:])):
                for i, (wp, ap) in enumerate(((0, 0), (1, 0), (0, 1))):
                    for k in range(a, b):
                        if i == 0:
                            pe.wait_ge(hi_done.sem, hi_done.at(k + 1))
                        if i == 2:
                            pe.wait_ge(lo_done.sem, lo_done.at(k + 1))
                        for o, m, h in outputs:
                            mm = pe.matmul(o, slab_of(wp, slot)[:, k * CB + m * P:k * CB + (m + 1) * P],
                                           self.dst[ap][:, k, h * self.w:(h + 1) * self.w],
                                           start=(i == 0 and k == 0), stop=(i == 2 and k == KT - 1))
                            if i == 2 and k == KT - 1:
                                mm.then_inc(done.sem, 1)
                if self.late and n == 0:
                    self.late["pe"](pe)

        def advance(self):
            if self.dst:
                hi_done.advance(KT)
                lo_done.advance(KT)
            if self.norm:
                sq_ready.advance(KT)
                value_done.advance(KT - 1)
                sum_done.advance(self.parts)
                log_done.advance(self.parts)
                rstd_done.advance(1 if self.norm["rcol"] is None else 2)

    slab_at = [0]

    def dense(act_in, segments, feed=None, rstd=None, tokens=SEQ, before=None, beside=None):
        if feed and feed.norm:
            rstd = (feed.norm["rstd"], feed.norm["rcol"])
        first_slab = slab_at[0]
        plan = []
        at, done = first_slab, 0
        for seg in segments:
            token_major = seg.get("token_major", False)
            w = CB if token_major else min(tokens, HALF)
            groups = [(t, None) for t in range(tokens // P)] if token_major else \
                     [(m, h) for m in range(2) for h in range(tokens // w)]
            plan.append(dict(seg, base=at, done=done, w=w, groups=groups, token_major=token_major))
            at, done = at + seg["n"], done + seg["n"] * len(groups)
        n_all = at - first_slab
        depth = 4 if tokens < SEQ or beside else 8

        def passes(step, work=None):
            def run(eng):
                for p in plan:
                    n = p["n"]
                    head = n if beside else min(n, 2) if p is plan[0] else 0
                    for s in range(head):
                        step(eng, p, s, s // 2, s % 2)
                        if work:
                            work(eng, p["base"] - first_slab + s)
                    loops = (n - head) // 2
                    if loops:
                        with eng.Fori(0, loops) as it:
                            for parity in range(2):
                                step(eng, p, it * 2 + (head + parity), it + head // 2, parity)
                    if (n - head) % 2:
                        step(eng, p, n - 1, (n - 1) // 2, (n - 1) % 2)
            return run

        def slot_of(p, parity):
            return (p["base"] + parity) % 2

        def bank(p, parity, j):
            return (p["done"] + parity * len(p["groups"]) + j) % depth

        def count(p, s, j):
            return s * len(p["groups"]) + (p["done"] + j + 1)

        def destination(p, s, j):
            a, h = p["groups"][j]
            if p["token_major"]:
                return p["dst"][:, a, bass.ds(s * CB, CB)]
            return p["dst"][:, bass.ds(s * 2 + a, 1), h * p["w"]:(h + 1) * p["w"]].rearrange("p o n -> p (o n)")

        def is_first(p, s):
            return feed and p is plan[0] and isinstance(s, int) and s == 0

        def sync_step(sp, p, s, pair, parity):
            load_slab(sp, s + (p["base"] + 3), slot_of(p, parity + 1))

        def act_step(act, p, s, pair, parity):
            G = len(p["groups"])
            if is_first(p, s):
                feed.act_split(act)
            act.wait_ge(group_done.sem, group_done.at(count(p, s, -1)))
            split_hi(act, s + (p["base"] + 1), pair + (p["base"] + parity + 1) // 2, slot_of(p, parity + 1))
            if is_first(p, s) and feed.norm:
                feed.act_squares(act)
                feed.act_root(act)
            if p.get("func"):
                for j in range(G):
                    act.wait_ge(bank_free.sem, bank_free.at(count(p, s, j)))
                    o = destination(p, s, j)
                    act.activation(o, o, p["func"])

        def dve_step(dve, p, s, pair, parity):
            if is_first(p, s):
                feed.dve_split(dve)
                feed.dve_wait_root(dve)
            if p.get("wait") and (not isinstance(s, int) or s == 0) and parity == 0:
                p["wait"](dve)
            for j, (a, h) in enumerate(p["groups"]):
                dve.wait_ge(group_done.sem, group_done.at(count(p, s, j)))
                o, psum = destination(p, s, j), ps[:, bank(p, parity, j), 0:p["w"]]
                if p.get("add"):
                    ins = dve.tensor_tensor(o, psum, o, ALU.add)
                elif p["token_major"]:
                    ins = dve.tensor_scalar(o, psum, rstd[1][:, a:a + 1], None, ALU.mult)
                else:
                    ins = dve.tensor_tensor(o, psum, rstd[0][:, h * p["w"]:(h + 1) * p["w"]], ALU.mult)
                ins.then_inc(bank_free.sem, 1)

        def pool_step(pool, p, s, pair, parity):
            if is_first(p, s) and feed.late:
                feed.late["pool"](pool)
            split_lo(pool, s + (p["base"] + 1), slot_of(p, parity + 1))

        def pe_step(pe, p, s, pair, parity):
            slot, w = slot_of(p, parity), p["w"]
            pe.wait_ge(slab_split.sem, s + (p["base"] + 1))
            if is_first(p, s):
                feed.pe_first(pe, slot, [(ps[:, bank(p, 0, j), 0:w], m, h) for j, (m, h) in enumerate(p["groups"])],
                              group_done)
                if feed.norm:
                    feed.pe_sums(pe)
                return
            for j, (a, h) in enumerate(p["groups"]):
                if feed and p is plan[0] and isinstance(s, int) and s == 1 and j == 1:
                    feed.pe_wait_sums_read(pe)
                pe.wait_ge(bank_free.sem, bank_free.at(count(p, s, j) - depth))
                o = ps[:, bank(p, parity, j), 0:w]
                for i, (wp, ap) in enumerate(PASSES):
                    for k in range(KT):
                        flags = dict(start=(i == 0 and k == 0), stop=(i == 2 and k == KT - 1))
                        if p["token_major"]:
                            mm = pe.matmul(o, act_in[ap][:, k, a * P:(a + 1) * P],
                                           slab_of(wp, slot)[:, k * CB:(k + 1) * CB], **flags)
                        else:
                            mm = pe.matmul(o, slab_of(wp, slot)[:, k * CB + a * P:k * CB + (a + 1) * P],
                                           act_in[ap][:, k, h * w:(h + 1) * w], **flags)
                mm.then_inc(group_done.sem, 1)

        work = beside or {}
        with nc.Block() as block:
            @block.sync
            def _(sp):
                if before:
                    before(sp)
                passes(sync_step, work.get("sp"))(sp)

            block.scalar(passes(act_step, work.get("act")))
            block.vector(passes(dve_step, work.get("dve")))
            block.gpsimd(passes(pool_step, work.get("pool")))
            block.tensor(passes(pe_step, work.get("pe")))
        group_done.advance(done)
        bank_free.advance(done)
        if feed:
            feed.advance()
        slab_at[0] += n_all

    mix_stack = main.enter_context(ExitStack())
    mix = sb(mix_stack, "mix", [P, 13, SEQ])
    qk = xr
    vv = mix[:, 0:4]
    gate = mix[:, 4:8]
    ya = mix[:, 8:12]
    small = mix[:, 12]

    h_stack = main.enter_context(ExitStack())
    act_hi = sb(h_stack, "h1_hi", [P, KT, SEQ], F32R)
    act_lo = sb(h_stack, "h1_lo", [P, KT, SEQ], F32R)
    h = (act_hi, act_lo)
    rstd = sb(h_stack, "h1_rstd", [P, SEQ])
    rcol = sb(h_stack, "h1_rcol", [P, NB])
    x_tiles = [xr[:, k] for k in range(KT)]

    gv = mix[:, 0:4].rearrange("p a n -> p (a n)").rearrange("p (t c) -> p t c", t=NB)
    dense(h, [dict(n=2, dst=ya, func=ACT.Gelu_apprx_tanh),
              dict(n=2, dst=gv, token_major=True, func=ACT.Gelu_apprx_tanh)],
          feed=Feed(h, x_tiles, param("norm_mix"),
                    dict(squares=mix[:, 4:6], sum=mix[:, 6], rstd=rstd[:], rcol=rcol[:])))

    gvn = gv.rearrange("p t (g d) -> p (t g) d", g=4)
    gsq = qk[:, 0:4].rearrange("p a n -> p (a n)").rearrange("p (m d) -> p m d", m=32)
    wT = qk[:, 4, 0:512]
    tri_s = qk[:, 4, 512:640]
    gstat = qk[:, 4, 640:1024]
    rows = qk[:, 5:7].rearrange("p a n -> p (a n)")
    R = qk[:, 7, 0:512]
    gmix = qk[:, 7, 512:1024]
    with nc.Block() as block:
        gsum, gmean, gvar, grstd = (gstat[:, 32 * n:32 * n + 32] for n in range(4))

        @block.sync
        def _(sp):
            sp.dma_start(wT, gm_ws_t).then_inc(loaded.sem, 16)
            sp.dma_start(tri_s, const("tri")).then_inc(loaded.sem, 16)
            sp.dma_start(rows[0:1, 0:1024], row_params).then_inc(loaded.sem, 16)
            sp.wait_ge(loaded.sem, loaded.at(48))

        @block.vector
        def _(dve):
            n = [0]

            def then(ins):
                n[0] += 1
                ins.then_inc(v_step.sem, 1)
                dve.wait_ge(v_step.sem, v_step.at(n[0]))

            then(dve.tensor_reduce(gsum, gvn, AX.X, ALU.add))
            then(dve.tensor_scalar(gmean, gsum, 1.0 / 128, None, ALU.mult))
            then(dve.tensor_tensor(gvn, gvn, gmean.unsqueeze(2).to_broadcast([P, 32, P]), ALU.subtract))
            dve.wait_ge(loaded.sem, loaded.at(48))
            then(dve.tensor_tensor(wT.rearrange("p (g t) -> p g t", g=4), wT.rearrange("p (g t) -> p g t", g=4),
                                   tri_s.unsqueeze(1).to_broadcast([P, 4, P]), ALU.mult))
            dve.wait_ge(a_step.sem, a_step.at(1))
            then(dve.tensor_reduce(gvar, gsq, AX.X, ALU.add))
            then(dve.tensor_scalar(gvar, gvar, 1.0 / 128, EPS, ALU.mult, ALU.add))
            dve.wait_ge(a_step.sem, a_step.at(2))
            then(dve.reciprocal(grstd, grstd))
            then(dve.tensor_tensor(gvn, gvn, grstd.unsqueeze(2).to_broadcast([P, 32, P]), ALU.mult))
            dve.wait_ge(p_step.sem, p_step.at(1))
            then(dve.tensor_copy(rows[0:1, 1024:1536], ps[0:1, 0, 0:512]))
            dve.wait_ge(p_step.sem, p_step.at(2))
            then(dve.tensor_copy(R, ps[:, 1, 0:512]))
            for t in range(NB):
                dve.wait_ge(p_step.sem, p_step.at(3 + t))
                for g in range(4):
                    last = dve.scalar_tensor_tensor(
                        out=gmix[:, g * P:(g + 1) * P], in0=ps[:, 2 + t % 4, g * P:(g + 1) * P],
                        scalar=param("gm_ln_g")[:, g:g + 1], in1=R[:, g * P:(g + 1) * P],
                        op0=ALU.mult, op1=ALU.add)
                then(last)
                u = ya[:, :, t * P:(t + 1) * P]
                then(dve.tensor_tensor(u, u, gmix.rearrange("p (g t) -> p g t", g=4), ALU.mult))

        @block.scalar
        def _(act):
            act.wait_ge(v_step.sem, v_step.at(3))
            act.activation(gsq, gvn, ACT.Square).then_inc(a_step.sem, 1)
            act.wait_ge(v_step.sem, v_step.at(6))
            act.activation(grstd, gvar, ACT.Sqrt).then_inc(a_step.sem, 1)

        @block.tensor
        def _(pe):
            pe.wait_ge(v_step.sem, v_step.at(4))
            pe.matmul(ps[0:1, 0, 0:512], ones[:, 0:1], wT, start=True, stop=True).then_inc(p_step.sem, 1)
            pe.wait_ge(v_step.sem, v_step.at(9))
            for g in range(4):
                c = slice(g * P, (g + 1) * P)
                pe.matmul(ps[:, 1, c], rows[0:1, c], rows[0:1, 1024 + g * P:1024 + (g + 1) * P],
                          start=True, stop=False)
                mm = pe.matmul(ps[:, 1, c], ones[0:1, :], rows[0:1, 512 + g * P:512 + (g + 1) * P],
                               start=False, stop=True)
            mm.then_inc(p_step.sem, 1)
            for t in range(NB):
                if t >= 4:
                    pe.wait_ge(v_step.sem, v_step.at(10 + 2 * (t - 4) + 1))
                for g in range(4):
                    mm = pe.matmul(ps[:, 2 + t % 4, g * P:(g + 1) * P], gv[:, t, g * P:(g + 1) * P],
                                   wT[:, g * P:(g + 1) * P], start=True, stop=True)
                mm.then_inc(p_step.sem, 1)
    loaded.advance(48)
    v_step.advance(10 + 2 * NB)
    a_step.advance(2)
    p_step.advance(2 + NB)

    temp = [gate[:, 0:2], gate[:, 2:4]]
    wl_hi = sb(h_stack, "wl_hi", [P, 64], F32R)
    wl_lo = sb(h_stack, "wl_lo", [P, 64], F32R)
    logits = small[:, 0:64]
    N_PAIRS, N_NORMED, TAPS = 6, 4, 2 * (CONV_W - 1)

    def tile_of(t):
        return qk[:, t] if t < 8 else vv[:, t - 8]

    def act_beside(act, s):
        if s == 0:
            act.activation(wl_hi[:], param("w_logits"), ACT.Copy).then_inc(a_step.sem, 1)
        if s < N_PAIRS:
            act.wait_ge(bank_free.sem, bank_free.at(4 * s + 4))
            if s >= 2:
                act.wait_ge(v_step.sem, v_step.at(2 * (s - 2) + 3))
            for b in range(2):
                t = 2 * s + b
                act.activation(temp[s % 2][:, b], tile_of(t), ACT.Copy,
                               scale=param("dn_conv")[:, (t + 1) * CONV_W - 1:(t + 1) * CONV_W])\
                   .then_inc(conv_started.sem, 1)
        n = s - 1
        if 0 <= n < N_NORMED:
            root = temp[n % 2]
            for u in range(4):
                act.wait_ge(sum_done.sem, sum_done.at(4 * n + u + 1))
                act.activation(root[:, u // 2, halves[u % 2]], ps[:, 4 + u, :], ACT.Ln, bias=eps_col)\
                   .then_inc(log_done.sem, 1)
            act.wait_ge(log_done.sem, log_done.at(4 * n + 4))
            act.activation(root, root, ACT.Exp, scale=-0.5).then_inc(rstd_done.sem, 1)
        if s < N_PAIRS:
            for b in range(2):
                act.wait_ge(tap_done.sem, tap_done.at(TAPS * s + TAPS - 1 + b))
                act.activation(tile_of(2 * s + b), temp[s % 2][:, b], ACT.Silu).then_inc(conv_done.sem, 1)

    def dve_beside(dve, s):
        if s == 0:
            dve.wait_ge(a_step.sem, a_step.at(1))
            dve.tensor_tensor(wl_lo[:], param("w_logits"), wl_hi[:].bitcast(F32), ALU.subtract)\
               .then_inc(v_step.sem, 1)
        if s < N_PAIRS:
            for back in range(1, CONV_W):
                for b in range(2):
                    t = 2 * s + b
                    if back == 1:
                        dve.wait_ge(conv_started.sem, conv_started.at(2 * s + b + 1))
                    else:
                        dve.wait_ge(tap_done.sem, tap_done.at(TAPS * s + 2 * (back - 2) + b + 1))
                    dve.scalar_tensor_tensor(
                        out=temp[s % 2][:, b, back:SEQ], in0=tile_of(t)[:, 0:SEQ - back],
                        scalar=param("dn_conv")[:, (t + 1) * CONV_W - 1 - back:(t + 1) * CONV_W - back],
                        in1=temp[s % 2][:, b, back:SEQ], op0=ALU.mult, op1=ALU.add).then_inc(tap_done.sem, 1)
        n = s - 1
        if 0 <= n < N_NORMED:
            dve.wait_ge(rstd_done.sem, rstd_done.at(n + 1))
            for b in range(2):
                t = 2 * n + b
                dve.scalar_tensor_tensor(out=qk[:, t], in0=qk[:, t], scalar=128.0 ** -0.5 if t < 4 else 1.0,
                                         in1=temp[n % 2][:, b], op0=ALU.mult, op1=ALU.mult).then_inc(v_step.sem, 1)
        if s == 7:
            dve.wait_ge(bank_free.sem, bank_free.at(32))
            for hf in range(2):
                dve.wait_ge(p_step.sem, p_step.at(hf + 1))
                r = rstd[0:8, halves[hf]]
                dve.tensor_tensor(r, ps[0:8, 4 + hf, :], r, ALU.mult).then_inc(v_step.sem, 1)
            dve.wait_ge(p_step.sem, p_step.at(3))
            dve.tensor_copy(logits, ps[:, 6, 0:64])

    def pool_beside(pool, s):
        if s < N_NORMED:
            for b in range(2):
                pool.wait_ge(conv_done.sem, conv_done.at(2 * s + b + 1))
                pool.tensor_tensor(temp[s % 2][:, b], qk[:, 2 * s + b], qk[:, 2 * s + b], ALU.mult)\
                    .then_inc(g_step.sem, 1)

    def pe_beside(pe, s):
        n = s - 1
        if 0 <= n < N_NORMED:
            pe.wait_ge(log_done.sem, log_done.at(4 * n))
            for u in range(4):
                pe.wait_ge(g_step.sem, g_step.at(2 * n + u // 2 + 1))
                pe.matmul(ps[:, 4 + u, :], ones[:], temp[n % 2][:, u // 2, halves[u % 2]], start=True, stop=True)\
                  .then_inc(sum_done.sem, 1)
        if s == 7:
            pe.wait_ge(log_done.sem, log_done.at(4 * N_NORMED))
            pe.wait_ge(v_step.sem, v_step.at(1))
            for hf in range(2):
                for i, (wp, ap) in enumerate(PASSES):
                    for k in range(KT):
                        mm = pe.matmul(ps[0:8, 4 + hf, :], (wl_hi, wl_lo)[wp][:, k * 8:k * 8 + 8],
                                       h[ap][:, k, halves[hf]],
                                       start=(i == 0 and k == 0), stop=(i == 2 and k == KT - 1))
                mm.then_inc(p_step.sem, 1)
            pe.wait_ge(v_step.sem, v_step.at(2 * N_NORMED + 3))
            for t in range(NB):
                mm = pe.transpose(ps[:, 6, t * 8:t * 8 + 8], rstd[0:8, t * P:(t + 1) * P], ident[0:8, 0:8])
            mm.then_inc(p_step.sem, 1)

    dense(h, [dict(n=4, dst=qk), dict(n=2, dst=vv),
              dict(n=2, dst=gate, func=ACT.Silu,
                   wait=lambda dve: dve.wait_ge(conv_done.sem, conv_done.at(2 * N_PAIRS)))],
          rstd=(rstd, rcol), beside=dict(act=act_beside, dve=dve_beside, pool=pool_beside, pe=pe_beside))
    for c, n in ((a_step, 1), (v_step, 2 * N_NORMED + 3), (g_step, 2 * N_NORMED), (p_step, 3),
                 (conv_started, 2 * N_PAIRS), (tap_done, TAPS * N_PAIRS), (conv_done, 2 * N_PAIRS),
                 (sum_done, 4 * N_NORMED), (log_done, 4 * N_NORMED), (rstd_done, N_NORMED)):
        c.advance(n)
    h_stack.close()

    st = main.enter_context(ExitStack())
    W = HEADS * P
    tri = sb(st, "tri", [P, P])
    strict = sb(st, "strict", [P, P])
    levels = sb(st, "levels", [P, 7, P])
    state = sb(st, "state", [P, W])
    resid = sb(st, "resid", [P, W])
    v_new = sb(st, "v_new", [P, W])

    def per_slot(name, n=1):
        return [sb(st, f"{name}{s}", [P, n, W] if n > 1 else [P, W]) for s in range(2)]

    decay = per_slot("decay")
    q_dec = per_slot("q_dec")
    n_mat = per_slot("n_mat")
    qk_mat = per_slot("qk_mat")
    n_lev = per_slot("n_lev", 2)
    k_dec = per_slot("k_dec")
    v_tok = per_slot("v_tok")
    k_cur = per_slot("k_cur")
    x_mat = per_slot("x_mat")
    t_mat = per_slot("t_mat")
    tt_mat = per_slot("tt_mat")
    v_cur = t_mat

    def col(n):
        return small[:, 64 + 32 * n:96 + 32 * n]

    beta, g_log, dec, neg_ed, cd, kd, nbeta, t_abs, t_exp = (col(n) for n in range(9))
    a_exp = small[:, 400:404]

    lg = logits.rearrange("p (b c) -> p b c", c=8)
    with nc.Block() as block:
        three = lambda x: x.rearrange("p (b h) -> p b h", h=4)

        @block.sync
        def _(sp):
            sp.dma_start(tri[:], const("tri")).then_inc(loaded.sem, 16)
            sp.dma_start(strict[:], const("strict")).then_inc(loaded.sem, 16)
            sp.dma_start(levels[:].rearrange("p l n -> p (l n)"), const("levels")).then_inc(loaded.sem, 16)
            sp.wait_ge(loaded.sem, loaded.at(48))

        @block.scalar
        def _(act):
            n = [0]

            def then(ins):
                n[0] += 1
                ins.then_inc(a_step.sem, 1)
                act.wait_ge(a_step.sem, a_step.at(n[0]))

            then(act.activation(three(beta), lg[:, :, 0:4], ACT.Sigmoid))
            act.wait_ge(v_step.sem, v_step.at(1))
            then(act.activation(t_abs, g_log, ACT.Abs))
            then(act.activation(t_exp, t_abs, ACT.Exp, scale=-1.0))
            then(act.activation(t_exp, t_exp, ACT.Ln, bias=1.0))
            then(act.activation(a_exp, param("dn_a_log"), ACT.Exp))
            act.wait_ge(v_step.sem, v_step.at(6))
            then(act.activation(neg_ed, dec, ACT.Exp))
            then(act.activation(cd, ps[:, 1, 0:32], ACT.Exp))
            then(act.activation(kd, kd, ACT.Exp))

        @block.vector
        def _(dve):
            n = [0]

            def then(ins):
                n[0] += 1
                ins.then_inc(v_step.sem, 1)
                dve.wait_ge(v_step.sem, v_step.at(n[0]))

            then(dve.tensor_tensor(three(g_log), lg[:, :, 4:8],
                                   param("dn_dt_bias").unsqueeze(1).to_broadcast([P, NB, 4]), ALU.add))
            dve.wait_ge(a_step.sem, a_step.at(4))
            then(dve.scalar_tensor_tensor(out=g_log, in0=g_log, scalar=0.0, in1=t_exp, op0=ALU.max, op1=ALU.add))
            dve.wait_ge(a_step.sem, a_step.at(5))
            then(dve.scalar_tensor_tensor(out=three(g_log), in0=three(g_log), scalar=-1.0,
                                          in1=a_exp.unsqueeze(1).to_broadcast([P, NB, 4]),
                                          op0=ALU.mult, op1=ALU.mult))
            then(dve.tensor_scalar(nbeta, beta, -1.0, None, ALU.mult))
            dve.wait_ge(p_step.sem, p_step.at(1))
            then(dve.tensor_copy(dec, ps[:, 0, 0:32]))
            then(dve.scalar_tensor_tensor(out=kd, in0=dec, scalar=-1.0, in1=ps[:, 1, 0:32],
                                          op0=ALU.mult, op1=ALU.add))
            dve.wait_ge(a_step.sem, a_step.at(6))
            then(dve.tensor_scalar(neg_ed, neg_ed, -1.0, None, ALU.mult))
            then(dve.memset(state[:], 0.0))

        @block.tensor
        def _(pe):
            pe.wait_ge(v_step.sem, v_step.at(3))
            pe.wait_ge(loaded.sem, loaded.at(48))
            pe.matmul(ps[:, 0, 0:32], tri[:], g_log, start=True, stop=True)
            pe.matmul(ps[:, 1, 0:32], ones[:], g_log, start=True, stop=True).then_inc(p_step.sem, 1)
    loaded.advance(48)
    a_step.advance(8)
    v_step.advance(8)
    p_step.advance(1)


    hs = lambda h: slice(h * P, (h + 1) * P)
    heads = lambda ap: ap.rearrange("p (h n) -> p h n", h=HEADS)
    over_heads = lambda ap: ap.unsqueeze(1).to_broadcast([P, HEADS, P])
    n_it = NB // 2

    def head_block(it, s, h):
        return qk[:, h, bass.ds(it * 256 + s * P, P)]

    def blk(z, it, s):
        return z[:, 0:4, bass.ds(it * 256 + s * P, P)]

    def scal(c, it, s, h):
        return c[:, bass.ds(it * 8 + s * 4 + h, 1)]

    with nc.Block() as block:
        @block.vector
        def _(dve):
            with dve.Fori(0, n_it) as it:
                for s in range(2):
                    dve.wait_ge(o_ready.sem, o_ready.at(it * 2))
                    g4 = g_log[:, bass.ds(it * 8 + s * 4, 4)]
                    dve.tensor_tensor(heads(decay[s][:]), over_heads(tri[:]),
                                      g4.unsqueeze(2).to_broadcast([P, HEADS, P]), ALU.mult)\
                       .then_inc(gtri_ready[s].sem, 1)
                for s in range(2):
                    dve.wait_ge(exp_done[s].sem, exp_done[s].at(it * 2 + 1))
                    for h in range(HEADS):
                        last = dve.tensor_scalar(decay[s][:, hs(h)], ps[:, 3 * s, hs(h)], scal(dec, it, s, h), 0.0,
                                                 ALU.subtract, ALU.min)
                    last.then_inc(arg_ready[s].sem, 1)
                for s in range(2):
                    dve.wait_ge(exp_done[s].sem, exp_done[s].at(it * 2 + 2))
                    dve.wait_ge(grams_done[s].sem, grams_done[s].at(it + 1))
                    for h in range(HEADS):
                        last = dve.scalar_tensor_tensor(out=n_mat[s][:, hs(h)], in0=ps[:, 3 * s + 1, hs(h)],
                                                        scalar=scal(nbeta, it, s, h), in1=decay[s][:, hs(h)],
                                                        op0=ALU.mult, op1=ALU.mult)
                    last.then_inc(raw_done[s].sem, 1)
                    dve.tensor_tensor(qk_mat[s][:], ps[:, 3 * s + 2, :], decay[s][:], ALU.mult)\
                       .then_inc(raw_done[s].sem, 1)
                for s in range(2):
                    dve.wait_ge(level_ready[s].sem, level_ready[s].at(it * 7 + 1))
                    dve.tensor_tensor(heads(tt_mat[s][:]), heads(n_lev[s][:, 0]), over_heads(ident[:]), ALU.add)\
                       .then_inc(tt_ready[s].sem, 1)
                for s in range(2):
                    dve.wait_ge(first_turned[s].sem, first_turned[s].at(it + 1))
                    dve.tensor_copy(t_mat[s][:], ps[:, 3 * s + 2, :]).then_inc(t_ready[s].sem, 1)
                for lev in range(1, 7):
                    for s in range(2):
                        dve.wait_ge(prod_done[s].sem, prod_done[s].at(it * 6 + lev))
                        if lev < 6:
                            dve.tensor_tensor(t_mat[s][:], ps[:, 3 * s + 1, :], t_mat[s][:], ALU.add)\
                               .then_inc(t_ready[s].sem, 1)
                        dve.tensor_tensor(tt_mat[s][:], ps[:, 3 * s + 2, :], tt_mat[s][:], ALU.add)\
                           .then_inc(tt_ready[s].sem, 1)
                for s in range(2):
                    n = it * 2 + s
                    dve.wait_ge(by_token[s].sem, by_token[s].at(it * 2 + 2))
                    dve.wait_ge(ks_done.sem, ks_done.at(n + 1))
                    for h in range(HEADS):
                        last = dve.scalar_tensor_tensor(out=resid[:, hs(h)], in0=ps[:, 6, hs(h)],
                                                        scalar=scal(neg_ed, it, s, h), in1=v_tok[s][:, hs(h)],
                                                        op0=ALU.mult, op1=ALU.add)
                    last.then_inc(resid_ready.sem, 1)
                    dve.wait_ge(step_done.sem, step_done.at(n + 1))
                    for h in range(HEADS):
                        last = dve.scalar_tensor_tensor(out=state[:, hs(h)], in0=state[:, hs(h)],
                                                        scalar=scal(cd, it, s, h), in1=ps[:, 7, hs(h)],
                                                        op0=ALU.mult, op1=ALU.add)
                    last.then_inc(state_ready.sem, 1)

        @block.scalar
        def _(act):
            with act.Fori(0, n_it) as it:
                for s in range(2):
                    act.wait_ge(rows_done[s].sem, rows_done[s].at(it + 1))
                    act.activation(q_dec[s][:], ps[:, 3 * s, :], ACT.Exp).then_inc(exp_done[s].sem, 1)
                    act.wait_ge(arg_ready[s].sem, arg_ready[s].at(it + 1))
                    act.activation(decay[s][:], decay[s][:], ACT.Exp).then_inc(exp_done[s].sem, 1)
                for s in range(2):
                    act.wait_ge(turned[s].sem, turned[s].at(it * 2 + 1))
                    for h in range(HEADS):
                        last = act.activation(k_dec[s][:, hs(h)], ps[:, 3 * s, hs(h)], ACT.Copy,
                                              scale=scal(kd, it, s, h))
                    last.then_inc(by_token[s].sem, 1)
                    act.wait_ge(turned[s].sem, turned[s].at(it * 2 + 2))
                    act.activation(v_tok[s][:], ps[:, 3 * s + 1, :], ACT.Copy).then_inc(by_token[s].sem, 1)
                for lev in range(1, 7):
                    for s in range(2):
                        act.wait_ge(x_done[s].sem, x_done[s].at(it * 6 + lev))
                        act.activation(x_mat[s][:], ps[:, 3 * s, :], ACT.Copy).then_inc(x_ready[s].sem, 1)
                for s in range(2):
                    n = it * 2 + s
                    act.wait_ge(tr_done.sem, tr_done.at(n + 1))
                    for h in range(HEADS):
                        last = act.activation(v_new[:, hs(h)], ps[:, 7, hs(h)], ACT.Copy, scale=scal(beta, it, s, h))
                    last.then_inc(vnew_ready.sem, 1)
                    act.wait_ge(o_done.sem, o_done.at(n + 1))
                    act.activation(blk(qk, it, s), heads(ps[:, 3 * s + 2, :]), ACT.Copy).then_inc(o_ready.sem, 1)

        @block.gpsimd
        def _(pool):
            with pool.Fori(0, n_it) as it:
                for s in range(2):
                    pool.wait_ge(raw_done[s].sem, raw_done[s].at(it * 2 + 1))
                    pool.tensor_tensor(heads(n_mat[s][:]), heads(n_mat[s][:]), over_heads(strict[:]), ALU.mult)\
                        .then_inc(masked[s].sem, 1)
                    pool.wait_ge(masked[s].sem, masked[s].at(it * 3 + 1))
                    pool.tensor_tensor(heads(n_lev[s][:, 0]), heads(n_mat[s][:]), over_heads(levels[:, 0]), ALU.mult)\
                        .then_inc(level_ready[s].sem, 1)
                for s in range(2):
                    pool.wait_ge(raw_done[s].sem, raw_done[s].at(it * 2 + 2))
                    pool.tensor_tensor(heads(n_lev[s][:, 1]), heads(n_mat[s][:]), over_heads(levels[:, 1]), ALU.mult)\
                        .then_inc(level_ready[s].sem, 1)
                for s in range(2):
                    pool.tensor_tensor(heads(qk_mat[s][:]), heads(qk_mat[s][:]), over_heads(tri[:]), ALU.mult)\
                        .then_inc(masked[s].sem, 1)
                for lev in range(2, 7):
                    for s in range(2):
                        if lev == 2:
                            pool.wait_ge(tt_ready[s].sem, tt_ready[s].at(it * 7 + 1))
                        else:
                            pool.wait_ge(x_done[s].sem, x_done[s].at(it * 6 + lev - 2))
                        pool.tensor_tensor(heads(n_lev[s][:, lev % 2]), heads(n_mat[s][:]), over_heads(levels[:, lev]),
                                           ALU.mult).then_inc(level_ready[s].sem, 1)
                for s in range(2):
                    pool.wait_ge(exp_done[s].sem, exp_done[s].at(it * 2 + 1))
                    pool.tensor_tensor(heads(q_dec[s][:]), heads(q_dec[s][:]), blk(qk, it, s), ALU.mult)\
                        .then_inc(masked[s].sem, 1)

        @block.tensor
        def _(pe):
            with pe.Fori(0, n_it) as it:
                for s in range(2):
                    pe.wait_ge(gtri_ready[s].sem, gtri_ready[s].at(it + 1))
                    pe.matmul(ps[:, 3 * s, :], ones[:], decay[s][:], start=True, stop=True).then_inc(rows_done[s].sem, 1)
                for s in range(2):
                    pe.wait_ge(block_loaded[s].sem, block_loaded[s].at(it * 32 + 32))
                    for h in range(HEADS):
                        pe.matmul(ps[:, 3 * s + 1, hs(h)], k_cur[s][:, hs(h)], k_cur[s][:, hs(h)],
                                  start=True, stop=True)
                    for h in range(HEADS):
                        mm = pe.matmul(ps[:, 3 * s + 2, hs(h)], k_cur[s][:, hs(h)], head_block(it, s, h),
                                       start=True, stop=True)
                    mm.then_inc(grams_done[s].sem, 1)
                for s in range(2):
                    pe.wait_ge(arg_ready[s].sem, arg_ready[s].at(it + 1))
                    pe.wait_ge(exp_done[s].sem, exp_done[s].at(it * 2 + 1))
                    for h in range(HEADS):
                        mm = pe.transpose(ps[:, 3 * s, hs(h)], k_cur[s][:, hs(h)], ident[:])
                    mm.then_inc(turned[s].sem, 1)
                    pe.wait_ge(raw_done[s].sem, raw_done[s].at(it * 2 + 1))
                    for h in range(HEADS):
                        mm = pe.transpose(ps[:, 3 * s + 1, hs(h)], v_cur[s][:, hs(h)], ident[:])
                    mm.then_inc(turned[s].sem, 1)
                for s in range(2):
                    pe.wait_ge(tt_ready[s].sem, tt_ready[s].at(it * 7 + 1))
                    pe.wait_ge(raw_done[s].sem, raw_done[s].at(it * 2 + 2))
                    for h in range(HEADS):
                        mm = pe.transpose(ps[:, 3 * s + 2, hs(h)], tt_mat[s][:, hs(h)], ident[:])
                    mm.then_inc(first_turned[s].sem, 1)
                for lev in range(1, 7):
                    for s in range(2):
                        pe.wait_ge(level_ready[s].sem, level_ready[s].at(it * 7 + lev + 1))
                        pe.wait_ge(t_ready[s].sem, t_ready[s].at(it * 6 + lev))
                        if lev == 1:
                            pe.wait_ge(by_token[s].sem, by_token[s].at(it * 2 + 2))
                        for h in range(HEADS):
                            mm = pe.matmul(ps[:, 3 * s, hs(h)], n_lev[s][:, lev % 2, hs(h)], t_mat[s][:, hs(h)],
                                           start=True, stop=True)
                        mm.then_inc(x_done[s].sem, 1)
                    for s in range(2):
                        pe.wait_ge(x_ready[s].sem, x_ready[s].at(it * 6 + lev))
                        pe.wait_ge(tt_ready[s].sem, tt_ready[s].at(it * 7 + lev))
                        if lev < 6:
                            for h in range(HEADS):
                                pe.matmul(ps[:, 3 * s + 1, hs(h)], tt_mat[s][:, hs(h)], x_mat[s][:, hs(h)],
                                          start=True, stop=True)
                        for h in range(HEADS):
                            mm = pe.matmul(ps[:, 3 * s + 2, hs(h)], x_mat[s][:, hs(h)], tt_mat[s][:, hs(h)],
                                           start=True, stop=True)
                        mm.then_inc(prod_done[s].sem, 1)
                for s in range(2):
                    n = it * 2 + s
                    pe.wait_ge(state_ready.sem, state_ready.at(n))
                    pe.wait_ge(o_done.sem, o_done.at(n))
                    for h in range(HEADS):
                        mm = pe.matmul(ps[:, 6, hs(h)], k_cur[s][:, hs(h)], state[:, hs(h)], start=True, stop=True)
                    mm.then_inc(ks_done.sem, 1)
                    pe.wait_ge(masked[s].sem, masked[s].at(it * 3 + 3))
                    pe.wait_ge(tt_ready[s].sem, tt_ready[s].at(it * 7 + 7))
                    for h in range(HEADS):
                        pe.matmul(ps[:, 3 * s + 2, hs(h)], state[:, hs(h)], q_dec[s][:, hs(h)],
                                  start=(h == 0), stop=False)
                    pe.wait_ge(resid_ready.sem, resid_ready.at(n + 1))
                    for h in range(HEADS):
                        mm = pe.matmul(ps[:, 7, hs(h)], tt_mat[s][:, hs(h)], resid[:, hs(h)], start=True, stop=True)
                    mm.then_inc(tr_done.sem, 1)
                    pe.wait_ge(vnew_ready.sem, vnew_ready.at(n + 1))
                    for h in range(HEADS):
                        mm = pe.matmul(ps[:, 7, hs(h)], k_dec[s][:, hs(h)], v_new[:, hs(h)], start=True, stop=True)
                    mm.then_inc(step_done.sem, 1)
                    for h in range(HEADS):
                        mm = pe.matmul(ps[:, 3 * s + 2, hs(h)], v_new[:, hs(h)], qk_mat[s][:, hs(h)],
                                       start=False, stop=(h == HEADS - 1))
                    mm.then_inc(o_done.sem, 1)

        @block.sync
        def _(sp):
            with sp.Fori(0, n_it) as it:
                for s in range(2):
                    sp.wait_ge(o_ready.sem, o_ready.at(it * 2))
                    sp.wait_ge(state_ready.sem, state_ready.at(it * 2))
                    sp.dma_start(heads(k_cur[s][:]), qk[:, 4:8, bass.ds(it * 256 + s * P, P)])\
                      .then_inc(block_loaded[s].sem, 16)
                    sp.dma_start(heads(v_cur[s][:]), vv[:, 0:4, bass.ds(it * 256 + s * P, P)])\
                      .then_inc(block_loaded[s].sem, 16)
    st.close()

    y_stack = main.enter_context(ExitStack())
    y = (sb(y_stack, "y1_hi", [P, KT, SEQ], F32R), sb(y_stack, "y1_lo", [P, KT, SEQ], F32R))

    def reload_x(src):
        def start(sp):
            sp.wait_ge(lo_done.sem, lo_done.at(KT))
            for k in range(KT):
                sp.dma_start(xr[:, k, :], src[:, k, :]).then_inc(loaded.sem, 16)

        def wait(dve):
            dve.wait_ge(loaded.sem, loaded.at(16 * KT))
        return start, wait

    root = vv

    def norm_pool(pool):
        for t in range(HEADS):
            pool.tensor_tensor(root[:, t], qk[:, t], qk[:, t], ALU.mult).then_inc(g_step.sem, 1)

    def norm_pe(pe):
        for u in range(2 * HEADS):
            pe.wait_ge(g_step.sem, g_step.at(u // 2 + 1))
            if u >= 4:
                pe.wait_ge(log_done.sem, log_done.at(u - 3))
            pe.matmul(ps[:, 4 + u % 4, :], ones[:], root[:, u // 2, halves[u % 2]], start=True, stop=True)\
              .then_inc(sum_done.sem, 1)

    def norm_act(act):
        for u in range(2 * HEADS):
            act.wait_ge(sum_done.sem, sum_done.at(u + 1))
            act.activation(root[:, u // 2, halves[u % 2]], ps[:, 4 + u % 4, :], ACT.Ln, scale=1.0 / P, bias=eps_col)\
               .then_inc(log_done.sem, 1)
        for t in range(HEADS):
            act.wait_ge(log_done.sem, log_done.at(2 * HEADS))
            act.activation(root[:, t], root[:, t], ACT.Exp, scale=-0.5).then_inc(rstd_done.sem, 1)

    def norm_dve(dve):
        for t in range(HEADS):
            dve.wait_ge(rstd_done.sem, rstd_done.at(t + 1))
            dve.tensor_tensor(root[:, t], root[:, t], gate[:, t], ALU.mult).then_inc(value_done.sem, 1)
            dve.wait_ge(value_done.sem, value_done.at(t + 1))
            dve.scalar_tensor_tensor(out=qk[:, t], in0=qk[:, t], scalar=param("dn_onorm"), in1=root[:, t],
                                     op0=ALU.mult, op1=ALU.mult).then_inc(v_step.sem, 1)

    start, wait = reload_x(x_t)
    dense(y, [dict(n=4, dst=xr, add=True, wait=wait)], before=start,
          feed=Feed(y, [(ya if t < 4 else qk)[:, t % 4] for t in range(KT)],
                    late=dict(first=4, pe_after=3, ready=lambda eng, k: eng.wait_ge(v_step.sem, v_step.at(k - 3)),
                              act=norm_act, dve=norm_dve, pool=norm_pool, pe=norm_pe)))
    for c, n in ((g_step, HEADS), (sum_done, 2 * HEADS), (log_done, 2 * HEADS), (rstd_done, HEADS),
                 (value_done, HEADS), (v_step, HEADS)):
        c.advance(n)
    loaded.advance(16 * KT)
    y_stack.close()
    mix_stack.close()

    def scope():
        return main.enter_context(ExitStack())

    xa = scope()
    q_t = sb(xa, "xa_q", [P, KT, SEQ])
    k_t = sb(xa, "xa_k", [P, KT, MEM])
    v_m = sb(xa, "xa_v", [P, 2, D])
    mem = scope()
    mem_x = sb(mem, "mem_x", [P, KT, MEM])
    m = (sb(mem, "mem_hi", [P, KT, MEM], F32R), sb(mem, "mem_lo", [P, KT, MEM], F32R))
    with nc.Block() as block:
        @block.sync
        def _(sp):
            sp.dma_start(mem_x[:], mem_t).then_inc(loaded.sem, 16)
            sp.wait_ge(loaded.sem, loaded.at(16))
    loaded.advance(16)
    mem_rstd = sb(mem, "mem_rstd", [P, MEM])
    mem_rcol = sb(mem, "mem_rcol", [P, 2])
    dense(m, [dict(n=4, dst=k_t), dict(n=4, dst=v_m, token_major=True)], tokens=MEM,
          feed=Feed(m, [mem_x[:, k] for k in range(KT)], param("norm_mem"),
                    dict(squares=q_t[:, 6:8, 0:MEM], sum=q_t[:, 5, 0:MEM], rstd=mem_rstd[:], rcol=mem_rcol[:]),
                    tokens=MEM))
    mem.close()

    h_stack = scope()
    h = (sb(h_stack, "h2_hi", [P, KT, SEQ], F32R), sb(h_stack, "h2_lo", [P, KT, SEQ], F32R))
    rstd = sb(h_stack, "h2_rstd", [P, SEQ])
    dense(h, [dict(n=4, dst=q_t)],
          feed=Feed(h, x_tiles, param("norm_xa"),
                    dict(squares=q_t[:, 6:8], sum=q_t[:, 5], rstd=rstd[:], rcol=None)))
    h_stack.close()

    at = scope()
    q_h = sb(at, "q_h", [P, 2, 2, SEQ])
    k_h = sb(at, "k_h", [P, 2, 2, MEM])
    v_h = sb(at, "v_h", [P, 2, 2, XA_D])
    prob = sb(at, "prob", [P, 2, 2, MEM])
    prob_t = sb(at, "prob_t", [P, 2, 2, HALF])
    stat = sb(at, "stat", [P, 2, 4, 2])

    scale = XA_D ** -0.5
    with nc.Block() as block:
        @block.sync
        def _(sp):
            with sp.Fori(0, 2) as it:
                for s in range(2):
                    sp.wait_ge(xa_o_copied.sem, xa_o_copied.at(it * 8 + (4 * s - 4)))
                    sp.dma_start(q_h[:, s], q_t[:, bass.ds(it * 4 + s * 2, 2), :]).then_inc(xa_head_loaded[s].sem, 16)
                    sp.dma_start(k_h[:, s], k_t[:, bass.ds(it * 4 + s * 2, 2), :]).then_inc(xa_head_loaded[s].sem, 16)
                    sp.dma_start(v_h[:, s], v_m[:, :, bass.ds(it * 512 + s * 256, 256)])\
                      .then_inc(xa_v_loaded[s].sem, 16)

        @block.tensor
        def _(pe):
            with pe.Fori(0, 2) as it:
                for s in range(2):
                    pe.wait_ge(xa_head_loaded[s].sem, xa_head_loaded[s].at(it * 32 + 32))
                    n0 = it * 8 + s * 4

                    def scores(v):
                        pe.wait_ge(xa_exp_done.sem, xa_exp_done.at(n0 + v - 1 if v >= 1 else n0))
                        for j in range(2):
                            u = 2 * v + j
                            for t in range(2):
                                mm = pe.matmul(ps[:, v % 2, j * MEM:(j + 1) * MEM], q_h[:, s, t, u * P:(u + 1) * P],
                                               k_h[:, s, t, :], start=(t == 0), stop=(t == 1))
                        mm.then_inc(xa_score_done.sem, 1)

                    def outputs(hf):
                        pe.wait_ge(xa_v_loaded[s].sem, xa_v_loaded[s].at(it * 16 + 16))
                        pe.wait_ge(xa_pt_ready.sem, xa_pt_ready.at(n0 + hf * 2 + 2))
                        pe.wait_ge(xa_o_copied.sem, xa_o_copied.at(it * 8 + s * 4))
                        for dt in range(2):
                            for t in range(2):
                                mm = pe.matmul(ps[:, 4 + 2 * hf + dt, :], v_h[:, s, t, dt * P:(dt + 1) * P],
                                               prob_t[:, hf, t, :], start=(t == 0), stop=(t == 1))
                            mm.then_inc(xa_o_done.sem, 1)

                    scores(0)
                    for v in range(4):
                        if v < 3:
                            scores(v + 1)
                        if v == 3:
                            outputs(0)
                        pe.wait_ge(xa_p_ready.sem, xa_p_ready.at(n0 + v + 1))
                        pe.wait_ge(xa_pt_ready.sem, xa_pt_ready.at(n0 + v - 1 if v >= 1 else n0))
                        for t in range(2):
                            for j in range(2):
                                mm = pe.transpose(ps[:, 2 + v % 2, (2 * t + j) * P:(2 * t + j + 1) * P],
                                                  prob[:, v % 2, j, t * P:(t + 1) * P], ident[:])
                        mm.then_inc(xa_pt_done.sem, 1)
                    outputs(1)

        @block.vector
        def _(dve):
            with dve.Fori(0, 2) as it:
                for s in range(2):
                    def soft(v):
                        n = it * 8 + s * 4 + v
                        st = stat[:, v % 2]
                        dve.wait_ge(xa_score_done.sem, xa_score_done.at(n + 1))
                        dve.tensor_reduce(st[:, 0], ps[:, v % 2, :].rearrange("p (j m) -> p j m", j=2), AX.X, ALU.max)\
                           .then_inc(xa_max_done.sem, 1)
                        dve.wait_ge(xa_max_done.sem, xa_max_done.at(n + 1))
                        dve.tensor_scalar(st[:, 1], st[:, 0], -scale, None, ALU.mult).then_inc(xa_bias_done.sem, 1)

                    def combine(v):
                        n = it * 8 + s * 4 + v
                        st = stat[:, v % 2]
                        dve.wait_ge(xa_exp_done.sem, xa_exp_done.at(n + 1))
                        dve.reciprocal(st[:, 3], st[:, 2]).then_inc(xa_inv_done.sem, 1)
                        dve.wait_ge(xa_inv_done.sem, xa_inv_done.at(n + 1))
                        dve.tensor_tensor(prob[:, v % 2], prob[:, v % 2], st[:, 3].unsqueeze(2)
                                          .to_broadcast([P, 2, MEM]), ALU.mult).then_inc(xa_p_ready.sem, 1)

                    def store(hf):
                        for dt in range(2):
                            dve.wait_ge(xa_o_done.sem, xa_o_done.at(it * 8 + s * 4 + 2 * hf + dt + 1))
                            dve.tensor_copy(q_t[:, bass.ds(it * 4 + s * 2 + dt, 1), halves[hf]]
                                            .rearrange("p o n -> p (o n)"), ps[:, 4 + 2 * hf + dt, :])\
                               .then_inc(xa_o_copied.sem, 1)

                    soft(0)
                    for v in range(4):
                        combine(v)
                        if v < 3:
                            soft(v + 1)
                    store(0)
                    store(1)

        @block.scalar
        def _(act):
            with act.Fori(0, 2) as it:
                for s in range(2):
                    def exps(v):
                        n = it * 8 + s * 4 + v
                        st = stat[:, v % 2]
                        act.wait_ge(xa_bias_done.sem, xa_bias_done.at(n + 1))
                        act.wait_ge(xa_pt_done.sem, xa_pt_done.at(n - 1 if v >= 1 else it * 8 + s * 4))
                        for j in range(2):
                            last = act.activation(prob[:, v % 2, j], ps[:, v % 2, j * MEM:(j + 1) * MEM], ACT.Exp,
                                                  bias=st[:, 1, j:j + 1], scale=scale, accum_out=st[:, 2, j:j + 1])
                        last.then_inc(xa_exp_done.sem, 1)

                    exps(0)
                    for v in range(4):
                        n = it * 8 + s * 4 + v
                        if v < 3:
                            exps(v + 1)
                        act.wait_ge(xa_pt_done.sem, xa_pt_done.at(n + 1))
                        if v % 2 == 0:
                            act.wait_ge(xa_o_done.sem, xa_o_done.at(it * 8 + s * 4))
                        act.activation(prob_t[:, v // 2, :, (v % 2) * 2 * P:(v % 2 + 1) * 2 * P],
                                       ps[:, 2 + v % 2, :].rearrange("p (t n) -> p t n", t=2), ACT.Copy)\
                           .then_inc(xa_pt_ready.sem, 1)
    at.close()
    y_stack = scope()
    y = (sb(y_stack, "y2_hi", [P, KT, SEQ], F32R), sb(y_stack, "y2_lo", [P, KT, SEQ], F32R))
    dense(y, [dict(n=4, dst=xr, add=True)], feed=Feed(y, [q_t[:, t] for t in range(KT)]))
    y_stack.close()
    xa.close()


    def mlp(gain, n_chunks, gated, name):
        st = scope()
        h = (sb(st, name + "_hi", [P, KT, SEQ], F32R), sb(st, name + "_lo", [P, KT, SEQ], F32R))
        rstd = sb(st, name + "_rstd", [P, SEQ])
        hid = [[sb(st, f"{name}_hid{p}{c}", [P, 2, SEQ], F32R) for c in range(2)] for p in range(2)]
        val = sb(st, f"{name}_val", [P, 4, HALF])
        feed = Feed(h, x_tiles, gain, dict(squares=val[:].rearrange("p (a b) n -> p a (b n)", a=2), sum=rstd[:],
                                           rstd=rstd[:], rcol=None))
        per = 3 if gated else 2
        base = slab_at[0]
        total = per * n_chunks
        ends = base + total == n_slabs
        loops = (n_chunks - 1) // 2 - (1 if ends and (n_chunks - 1) % 2 == 0 else 0)

        def sequence(eng, step):
            def chunk(c0, s0, it, kc, ks):
                for n, (op, dc) in enumerate(([("gate", 0)] if gated else []) + [("up", 0), ("down", -1)]):
                    step(eng, op, kc * it + (c0 + dc), ks * it + (s0 + n), c0 + dc, s0 + n, it)
            if gated:
                step(eng, "gate", 0, 0, 0, 0, 0)
            step(eng, "up", 0, per - 2, 0, per - 2, 0)
            with eng.Fori(0, loops) as it:
                for cc in range(2):
                    chunk(1 + cc, per - 1 + cc * per, it, 2, 2 * per)
            for c in range(1 + 2 * loops, n_chunks):
                chunk(c, per - 1 + (c - 1) * per, 0, 0, 0)
            step(eng, "down", n_chunks - 1, total - 1, n_chunks - 1, total - 1, 0)

        def wait_group(eng, op, c, j):
            sem, n = {"gate": (gate_done, 4), "up": (up_done, 4), "down": (down_done, 16)}[op]
            eng.wait_ge(sem.sem, sem.at(c * n + j + 1))

        def hidden(part, cf, j):
            return hid[part][cf % 2][:, j // 2, halves[j % 2]]

        def act_step(act, op, c, s, cf, sf, it):
            if sf == 0:
                feed.act_split(act)
                split_hi(act, base + 1, (base + 1) // 2, (base + 1) % 2)
                feed.act_squares(act)
                feed.act_root(act)
            if op == "gate":
                for j in range(4):
                    act.wait_ge(gate_read.sem, gate_read.at(c * 4 + j + 1))
                    act.activation(val[:, j], val[:, j], ACT.Silu).then_inc(silu_done.sem, 1)
            if op == "up":
                if not gated:
                    for j in range(4):
                        act.wait_ge(relu_done.sem, relu_done.at(c * 4 + j + 1))
                        act.activation(val[:, j], val[:, j], ACT.Square).then_inc(square_done.sem, 1)
                for j in range(4):
                    act.wait_ge(square_done.sem, square_done.at(c * 4 + j + 1))
                    act.activation(hidden(0, cf, j), val[:, j], ACT.Copy).then_inc(hid_hi.sem, 1)
            if sf < total - 1 and sf + base + 2 < n_slabs:
                wait_group(act, op, c, 15 if op == "down" else 3)
                g = base + sf + 2
                split_hi(act, base + 2 + s, it * per + g // 2, g % 2)

        def dve_step(dve, op, c, s, cf, sf, it):
            if sf == 0:
                feed.dve_split(dve)
                feed.dve_wait_root(dve)
            if op == ("gate" if gated else "up"):
                dve.wait_ge(hid_ready.sem, hid_ready.at(c * 4))
            if op == "gate":
                for j in range(4):
                    wait_group(dve, op, c, j)
                    dve.tensor_tensor(val[:, j], ps[:, j, :], rstd[:, halves[j % 2]], ALU.mult)\
                       .then_inc(gate_read.sem, 1)
            if op == "up":
                for j in range(4):
                    wait_group(dve, op, c, j)
                    if gated:
                        dve.wait_ge(silu_scaled.sem, silu_scaled.at(c * 4 + j + 1))
                        dve.tensor_tensor(val[:, j], ps[:, j, :], val[:, j], ALU.mult).then_inc(square_done.sem, 1)
                    else:
                        dve.scalar_tensor_tensor(out=val[:, j], in0=ps[:, j, :], scalar=0.0,
                                                 in1=rstd[:, halves[j % 2]], op0=ALU.max, op1=ALU.mult)\
                           .then_inc(relu_done.sem, 1)
                for j in range(4):
                    dve.wait_ge(hid_hi.sem, hid_hi.at(c * 4 + j + 1))
                    dve.tensor_tensor(hidden(1, cf, j), val[:, j], hidden(0, cf, j).bitcast(F32), ALU.subtract)\
                       .then_inc(hid_ready.sem, 1)
            if op == "down":
                for j in range(16):
                    wait_group(dve, op, c, j)
                    t = xr[:, j // 2, halves[j % 2]]
                    dve.tensor_tensor(t, ps[:, 4 + j % 4, :], t, ALU.add).then_inc(bank_free.sem, 1)

        def pe_step(pe, op, c, s, cf, sf, it):
            slot = (base + sf) % 2
            pe.wait_ge(slab_split.sem, base + 1 + s)
            if sf == 0:
                feed.pe_first(pe, slot, [(ps[:, j, :], j // 2, j % 2) for j in range(4)],
                              gate_done if gated else up_done)
                feed.pe_sums(pe)
            elif op != "down":
                done = gate_done if op == "gate" else up_done
                for j in range(4):
                    if op == "up" and gated:
                        pe.wait_ge(gate_read.sem, gate_read.at(c * 4 + j + 1))
                    elif cf > 0:
                        last = square_done if gated else relu_done
                        pe.wait_ge(last.sem, last.at(c * 4 + j - 3))
                    m, hf = j // 2, j % 2
                    for i, (wp, ap) in enumerate(((0, 0), (0, 1), (1, 0))):
                        for k in range(KT):
                            mm = pe.matmul(ps[:, j, :], slab_of(wp, slot)[:, k * CB + m * P:k * CB + (m + 1) * P],
                                           h[ap][:, k, halves[hf]],
                                           start=(i == 0 and k == 0), stop=(i == 2 and k == KT - 1))
                    mm.then_inc(done.sem, 1)
            else:
                pe.wait_ge(hid_ready.sem, hid_ready.at(c * 4 + 4))
                if cf == 0:
                    feed.pe_wait_sums_read(pe)
                for j in range(16):
                    pe.wait_ge(bank_free.sem, bank_free.at(c * 16 + j - 3))
                    m, hf = j // 2, j % 2
                    for i, (wp, ap) in enumerate(((0, 0), (0, 1), (1, 0))):
                        for k in range(2):
                            mm = pe.matmul(ps[:, 4 + j % 4, :], slab_of(wp, slot)[:, k * D + m * P:k * D + (m + 1) * P],
                                           hid[ap][cf % 2][:, k, halves[hf]],
                                           start=(i == 0 and k == 0), stop=(i == 2 and k == 1))
                    mm.then_inc(down_done.sem, 1)

        def pool_step(pool, op, c, s, cf, sf, it):
            if sf == 0:
                split_lo(pool, base + 1, (base + 1) % 2)
            if op == "gate":
                for j in range(4):
                    pool.wait_ge(silu_done.sem, silu_done.at(c * 4 + j + 1))
                    pool.tensor_tensor(val[:, j], val[:, j], rstd[:, halves[j % 2]], ALU.mult)\
                        .then_inc(silu_scaled.sem, 1)
            if sf < total - 1 and sf + base + 2 < n_slabs:
                split_lo(pool, base + 2 + s, (base + sf) % 2)

        def sync_step(sp, op, c, s, cf, sf, it):
            if sf == 0:
                load_slab(sp, base + 3, (base + 1) % 2)
            if sf < total - 1 and sf + base + 4 < n_slabs:
                load_slab(sp, base + 4 + s, (base + sf) % 2)

        with nc.Block() as block:
            for eng, step in ((block.scalar, act_step), (block.vector, dve_step), (block.tensor, pe_step),
                              (block.gpsimd, pool_step), (block.sync, sync_step)):
                eng(lambda x, step=step: sequence(x, step))
        feed.advance()
        for c, n in ((gate_done, 4 if gated else 0), (gate_read, 4 if gated else 0),
                     (silu_done, 4 if gated else 0), (silu_scaled, 4 if gated else 0), (up_done, 4), (down_done, 16),
                     (relu_done, 0 if gated else 4), (square_done, 4), (hid_hi, 4), (hid_ready, 4), (bank_free, 16)):
            c.advance(n * n_chunks)
        slab_at[0] += total
        st.close()

    mlp(param("norm_ffn"), FF1_CHUNKS, False, "ff1")

    m2 = scope()
    mix = sb(m2, "mix2", [P, 13, SEQ])
    ones64 = sb(m2, "ones64", [P, P])
    lam = sb(m2, "lam", [P, 80])
    neg_lam, q_gain, o_gain = lam[:, 70:71], lam[:, 71:72], lam[:, 72:73]
    zq, zk, c_a, c_g = mix[:, 0:2], mix[:, 2:4], mix[:, 6:8], mix[:, 8:10]
    zv = mix[:, 4:6].rearrange("p a n -> p (a n)").rearrange("p (t c) -> p t c", t=NB)
    attn_out = c_g
    st = scope()
    h = (sb(st, "h5_hi", [P, KT, SEQ], F32R), sb(st, "h5_lo", [P, KT, SEQ], F32R))
    rstd = sb(st, "h5_rstd", [P, SEQ])
    rcol = sb(st, "h5_rcol", [P, NB])

    final_sq, final_total, final_root = mix[:, 0:2], mix[:, 2], mix[:, 3]

    def final_act(act):
        for k in range(KT):
            if k >= 2:
                act.wait_ge(final_added.sem, final_added.at(max(k - 2, 1)))
            act.activation(final_sq[:, k % 2], xr[:, k], ACT.Square).then_inc(final_squared.sem, 1)
        for hf in range(2):
            act.wait_ge(final_summed.sem, final_summed.at(hf + 1))
            act.activation(final_root[:, halves[hf]], ps[:, 6 + hf, :], ACT.Ln, scale=1.0 / D, bias=eps_col)\
               .then_inc(final_log.sem, 1)
        act.wait_ge(final_log.sem, final_log.at(2))
        act.activation(final_root, final_root, ACT.Exp, scale=-0.5).then_inc(final_rooted.sem, 1)

    def final_dve(dve):
        for k in range(1, KT):
            dve.wait_ge(final_squared.sem, final_squared.at(k + 1))
            if k > 1:
                dve.wait_ge(final_added.sem, final_added.at(k - 1))
            dve.tensor_tensor(final_total, final_sq[:, 0] if k == 1 else final_total, final_sq[:, k % 2], ALU.add)\
               .then_inc(final_added.sem, 1)
        dve.wait_ge(final_rooted.sem, final_rooted.at(1))
        for k in range(KT):
            dve.scalar_tensor_tensor(out=xr[:, k], in0=xr[:, k], scalar=param("norm_final")[:, k:k + 1],
                                     in1=final_root, op0=ALU.mult, op1=ALU.mult).then_inc(final_written.sem, 1)

    def final_pe(pe):
        pe.wait_ge(final_added.sem, final_added.at(KT - 1))
        for hf in range(2):
            pe.matmul(ps[:, 6 + hf, :], ones[:], final_total[:, halves[hf]], start=True, stop=True)\
              .then_inc(final_summed.sem, 1)

    def spill(sp):
        for k in range(KT):
            sp.wait_ge(final_written.sem, final_written.at(k + 1))
            sp.dma_start(x_spill[:, k, :], xr[:, k, :]).then_inc(stored.sem, 16)

    pooled, s_b, s_c, s_h = xr[:, 0:2], xr[:, 2:4], xr[:, 4:6], xr[:, 6:8]
    windows = mix[:, 0:4]
    temp = mix[:, 10:12]
    edge = sb(st, "edge", [P, 2, 16])
    pw = sb(st, "pw", [P, 2, P])

    flat_g = c_g.rearrange("p a n -> p (a n)")
    table = flat_g[:, 0:1600].rearrange("p (h n) -> p h n", h=HEADS)
    causal, ones32 = flat_g[:, 1600:1728], flat_g[:, 1728:1856]
    hot, rel = mix[:, 12, 0:384], mix[:, 12, 384:896].rearrange("p (h n) -> p h n", h=HEADS)
    bias = mix[:, 12].rearrange("p (h n) -> p h n", h=HEADS)

    SIDE_TAPS = {2: 12, 3: 9, 4: 15, 5: 14, 6: 10}
    N_TAPS = 2 * (CONF_K - 1)
    assert sum(SIDE_TAPS.values()) == N_TAPS
    conf_w, sconv_w = param("conf_dw_w"), param("sconv_w")
    ln = temp
    q_root, k_root = s_b, s_h
    root_base, sum_base, value_base = 2, 3, KT - 1

    def start(sp):
        spill(sp)
        sp.dma_start(edge[:].rearrange("p a n -> p (a n)"), const("pool_edge")).then_inc(loaded.sem, 16)
        sp.dma_start(pw[:].rearrange("p a n -> p (a n)"), pool_w).then_inc(loaded.sem, 16)

    def sp_beside(sp, s):
        if s == 2:
            sp.wait_ge(g_step.sem, g_step.at(1))
            sp.wait_ge(sum_done.sem, sum_done.at(3))
            for dst, name in ((causal, "causal"), (hot, "onehot"), (ones32, "ones32"), (ones64[:], "ones64")):
                sp.dma_start(dst, const(name)).then_inc(loaded.sem, 16)
        if s == 6:
            sp.wait_ge(bias_step.sem, bias_step.at(10))
            sp.dma_start(bias_skew.rearrange("h p n -> p h n"), table).then_inc(stored.sem, 16)
            sp.wait_ge(stored.sem, stored.at(16 * KT + 16))
            for hd in range(HEADS):
                skewed = bias_skew[hd].rearrange("p n -> (p n)")[127:127 + P * 399]\
                    .rearrange("(p n) -> p n", n=399)[:, 0:256]
                sp.dma_start(bias[:, hd, :], skewed).then_inc(loaded.sem, 16)

    def root_of(act, into, units, psum_at, log_from, scale):
        for n in range(units[0], units[1]):
            u = n - units[0]
            act.wait_ge(sum_done.sem, sum_done.at(sum_base + n + 1))
            act.activation(into[:, u // 2, halves[u % 2]], ps[:, psum_at + u, :], ACT.Ln, scale=scale, bias=eps_col)\
               .then_inc(log_done.sem, 1)
        act.wait_ge(log_done.sem, log_done.at(sum_base + log_from + units[1] - units[0]))
        used = into[:, 0:(units[1] - units[0]) // 2]
        act.activation(used, used, ACT.Exp, scale=-0.5).then_inc(rstd_done.sem, 1)

    def act_beside(act, s):
        if s == 1:
            act.wait_ge(bank_free.sem, bank_free.at(8))
            act.activation(c_g, c_g, ACT.Sigmoid).then_inc(a_step.sem, 1)
            act.wait_ge(g_step.sem, g_step.at(1))
            for b in range(2):
                act.activation(temp[:, b], c_a[:, b], ACT.Copy, scale=conf_w[:, (b + 1) * CONF_K - 1:(b + 1) * CONF_K])\
                   .then_inc(conv_started.sem, 1)
        if s == 4:
            for t in range(2):
                for hf in range(2):
                    act.wait_ge(p_step.sem, p_step.at(2 * t + hf + 1))
                    act.activation(pooled[:, t, halves[hf]], ps[:, 4 + 2 * t + hf, :], ACT.Copy,
                                   scale=param("pool_scale")[:, t:t + 1]).then_inc(a_step.sem, 1)
            act.wait_ge(bias_step.sem, bias_step.at(4))
            act.activation(lam[:, 66:68], lam[:, 64:66], ACT.Exp).then_inc(a_step.sem, 1)
        if s == 5:
            act.wait_ge(g_step.sem, g_step.at(2))
            for b in range(2):
                act.activation(s_h[:, b], s_c[:, b], ACT.Copy, scale=sconv_w[:, b * 3 + 2:b * 3 + 3])\
                   .then_inc(conv_started.sem, 1)
        if s == 6:
            act.wait_ge(v_step.sem, v_step.at(28))
            act.activation(s_c, s_h, ACT.Copy).then_inc(a_step.sem, 1)
            root_of(act, q_root, (0, 4), 4, 0, 1.0 / QK2)
            act.wait_ge(tap_done.sem, tap_done.at(N_TAPS))
            for b in range(2):
                act.activation(c_a[:, b], temp[:, b], ACT.Identity, bias=param("conf_dw_b")[:, b:b + 1])\
                   .then_inc(conv_done.sem, 1)
        if s == 7:
            root_of(act, k_root, (6, 8), 6, 4, 1.0 / QK2)
        if s == 8:
            root_of(act, k_root[:, 1:2], (10, 12), 6, 6, 1.0 / QK2)

    def pool_beside(pool, s):
        if s == 1:
            pool.wait_ge(a_step.sem, a_step.at(1))
            pool.tensor_tensor(c_a, c_a, c_g, ALU.mult).then_inc(g_step.sem, 1)
        if s == 4:
            pool.wait_ge(bank_free.sem, bank_free.at(20))
            pool.tensor_tensor(s_c, s_c, s_h, ALU.mult).then_inc(g_step.sem, 1)
        if s == 5:
            pool.wait_ge(bank_free.sem, bank_free.at(24))
            pool.tensor_tensor(q_root, zq, zq, ALU.mult).then_inc(g_step.sem, 1)
        if s == 6:
            pool.wait_ge(bank_free.sem, bank_free.at(28))
            pool.wait_ge(a_step.sem, a_step.at(7))
            pool.tensor_tensor(k_root, zk, zk, ALU.mult).then_inc(g_step.sem, 1)
        if s == 7:
            for hf in range(2):
                pool.wait_ge(value_done.sem, value_done.at(value_base + 2 * hf + 2))
                pool.tensor_tensor(ln[:, :, halves[hf]], c_a[:, :, halves[hf]], c_a[:, :, halves[hf]], ALU.mult)\
                    .then_inc(g_step.sem, 1)
        if s == 8:
            pool.wait_ge(v_step.sem, v_step.at(30))
            pool.wait_ge(bank_free.sem, bank_free.at(40))
            pool.tensor_tensor(s_c, s_c, s_b, ALU.mult)

    window_steps = [0]

    def window_tile(dve, t):
        def then(ins):
            window_steps[0] += 1
            ins.then_inc(v_step.sem, 1)
            dve.wait_ge(v_step.sem, v_step.at(window_steps[0]))

        u = pooled[:, t]
        src, bufs = u, [windows[:, 0], windows[:, 1]]
        for d in range(4 if t else 2):
            w, o = 2 ** d, bufs[d % 2]
            then(dve.tensor_copy(o[:, 0:w], src[:, 0:w]))
            then(dve.tensor_tensor(o[:, w:SEQ], src[:, w:SEQ], src[:, 0:SEQ - w], ALU.add))
            src = o
        for half in range(2):
            c = slice(64 * half, 64 * half + 64)
            o = bufs[half]
            then(dve.scalar_tensor_tensor(out=windows[c, 2 + t, :], in0=o[c], scalar=edge[c, t, 15:16], in1=u[c],
                                          op0=ALU.mult, op1=ALU.subtract))
            then(dve.tensor_tensor(o[c, 0:16], o[c, 0:16], edge[c, t, :], ALU.mult))
            then(dve.tensor_tensor(windows[c, 2 + t, 0:16], o[c, 0:16], u[c, 0:16], ALU.subtract))

    def taps(dve, s):
        first = sum(n for step, n in SIDE_TAPS.items() if step < s)
        for n in range(first, first + SIDE_TAPS.get(s, 0)):
            back, b = n // 2 + 1, n % 2
            if back == 1:
                dve.wait_ge(conv_started.sem, conv_started.at(b + 1))
            else:
                dve.wait_ge(tap_done.sem, tap_done.at(n - 1))
            w = (b + 1) * CONF_K - 1 - back
            dve.scalar_tensor_tensor(out=temp[:, b, back:SEQ], in0=c_a[:, b, 0:SEQ - back], scalar=conf_w[:, w:w + 1],
                                     in1=temp[:, b, back:SEQ], op0=ALU.mult, op1=ALU.add).then_inc(tap_done.sem, 1)

    def short_conv(dve):
        for back in range(1, 3):
            for b in range(2):
                if back == 1:
                    dve.wait_ge(conv_started.sem, conv_started.at(3 + b))
                else:
                    dve.wait_ge(v_step.sem, v_step.at(25 + b))
                dve.scalar_tensor_tensor(out=s_h[:, b, back:SEQ], in0=s_c[:, b, 0:SEQ - back],
                                         scalar=sconv_w[:, b * 3 + 2 - back:b * 3 + 3 - back],
                                         in1=s_h[:, b, back:SEQ], op0=ALU.mult, op1=ALU.add).then_inc(v_step.sem, 1)

    def bias_table(dve, s):
        if s == 4:
            lam_v = param("lam").rearrange("p (a b n) -> p a b n", a=2, b=2)
            prod = lam[:, 0:64].rearrange("p (a n) -> p a n", a=2)
            dve.wait_ge(loaded.sem, loaded.at(16 * 6))
            dve.memset(table, 0.0).then_inc(bias_step.sem, 1)
            dve.tensor_copy(rel[0:32], param("rel_bias")[0:32].unsqueeze(2).to_broadcast([32, HEADS, P]))\
               .then_inc(bias_step.sem, 1)
            dve.tensor_tensor(prod, lam_v[:, :, 0], lam_v[:, :, 1], ALU.mult).then_inc(bias_step.sem, 1)
            dve.wait_ge(bias_step.sem, bias_step.at(3))
            dve.tensor_reduce(lam[:, 64:66], prod, AX.X, ALU.add).then_inc(bias_step.sem, 1)
            dve.tensor_scalar(q_gain, param("q_norm"), QK2 ** -0.5, None, ALU.mult).then_inc(bias_step.sem, 1)
            dve.tensor_scalar(o_gain, param("subln"), 1.0 - LAM_INIT, None, ALU.mult)
        if s == 5:
            for hd in range(HEADS):
                dve.wait_ge(p_step.sem, p_step.at(4 + hd + 1))
                dve.tensor_copy(lam[:, 74 + hd:75 + hd], ps[:, 4 + hd, 0:1]).then_inc(bias_step.sem, 1)
            dve.wait_ge(bias_step.sem, bias_step.at(9))
            for hd in range(HEADS):
                last = dve.tensor_scalar(table[:, hd, 0:384], ps[:, 4 + hd, 0:384], lam[:, 74 + hd:75 + hd], None,
                                         ALU.subtract)
            last.then_inc(bias_step.sem, 1)
            dve.wait_ge(a_step.sem, a_step.at(6))
            dve.tensor_tensor(lam[:, 68:69], lam[:, 67:68], lam[:, 66:67], ALU.subtract).then_inc(bias_step.sem, 1)
            dve.wait_ge(bias_step.sem, bias_step.at(11))
            dve.tensor_scalar(neg_lam, lam[:, 68:69], -LAM_INIT, None, ALU.add)
        if s == 8:
            dve.wait_ge(loaded.sem, loaded.at(16 * 10))
            d = bias[:, :, P:2 * P]
            dve.tensor_tensor(d, d, causal.unsqueeze(1).to_broadcast([P, HEADS, P]), ALU.add)

    def times_root(dve, z, root, gain, n_root):
        dve.wait_ge(rstd_done.sem, rstd_done.at(root_base + n_root))
        dve.scalar_tensor_tensor(out=z, in0=z, scalar=gain, in1=root, op0=ALU.mult, op1=ALU.mult)\
           .then_inc(v_step.sem, 1)

    def dve_beside(dve, s):
        if s in (2, 3):
            if s == 2:
                dve.wait_ge(loaded.sem, loaded.at(32))
                dve.wait_ge(bank_free.sem, bank_free.at(12))
            window_tile(dve, s - 2)
        if s == 6:
            short_conv(dve)
        taps(dve, s)
        bias_table(dve, s)
        if s == 6:
            dve.wait_ge(bias_step.sem, bias_step.at(5))
            for t in range(2):
                times_root(dve, zq[:, t], q_root[:, t], q_gain, 1)
        if s == 7:
            for hf in range(2):
                dve.wait_ge(sum_done.sem, sum_done.at(sum_base + 4 + hf + 1))
                for t in range(2):
                    dve.scalar_tensor_tensor(out=c_a[:, t, halves[hf]], in0=ps[:, 4 + hf, :], scalar=-1.0 / 256,
                                             in1=c_a[:, t, halves[hf]], op0=ALU.mult, op1=ALU.add)\
                       .then_inc(value_done.sem, 1)
            times_root(dve, zk[:, 0], k_root[:, 0], param("k_norm"), 2)
        if s == 8:
            times_root(dve, zk[:, 1], k_root[:, 1], param("k_norm"), 3)

    def pe_beside(pe, s):
        def sums(pairs, n0, joined, psum_at):
            for n, tiles in enumerate(pairs):
                for i, z in enumerate(tiles):
                    mm = pe.matmul(ps[:, psum_at + n, :], joined, z, start=(i == 0), stop=(i == len(tiles) - 1))
                mm.then_inc(sum_done.sem, 1)

        if s == 4:
            pe.wait_ge(log_done.sem, log_done.at(3))
            for t in range(2):
                pe.wait_ge(v_step.sem, v_step.at(24 if t else 10))
                for hf in range(2):
                    pe.matmul(ps[:, 4 + 2 * t + hf, :], pw[:, t, :], windows[:, 2 + t, halves[hf]],
                              start=True, stop=True).then_inc(p_step.sem, 1)
        if s == 5:
            pe.wait_ge(a_step.sem, a_step.at(5))
            pe.wait_ge(loaded.sem, loaded.at(16 * 6))
            pe.wait_ge(bias_step.sem, bias_step.at(2))
            for hd in range(HEADS):
                pe.matmul(ps[:, 4 + hd, 0:384], rel[0:32, hd, :], hot[0:32, :], start=True, stop=True)\
                  .then_inc(p_step.sem, 1)
        if s == 6:
            pe.wait_ge(bias_step.sem, bias_step.at(10))
            pe.wait_ge(g_step.sem, g_step.at(3))
            sums([[q_root[:, t, c]] for t in range(2) for c in halves], 0, ones32, 4)
        if s == 7:
            pe.wait_ge(log_done.sem, log_done.at(sum_base + 4))
            pe.wait_ge(conv_done.sem, conv_done.at(2))
            sums([[c_a[:, 0, c], c_a[:, 1, c]] for c in halves], 4, ones[:], 4)
            pe.wait_ge(g_step.sem, g_step.at(4))
            sums([[k_root[:, 0, c]] for c in halves], 6, ones32, 6)
        if s == 8:
            pe.wait_ge(value_done.sem, value_done.at(value_base + 4))
            pe.wait_ge(g_step.sem, g_step.at(6))
            sums([[ln[:, 0, c], ln[:, 1, c]] for c in halves], 8, ones[:], 4)
            pe.wait_ge(log_done.sem, log_done.at(sum_base + 6))
            sums([[k_root[:, 1, c]] for c in halves], 10, ones32, 6)

    dense(h, [dict(n=1, dst=c_a), dict(n=1, dst=c_g),
              dict(n=1, dst=pooled, wait=lambda dve: dve.wait_ge(stored.sem, stored.at(16 * KT))),
              dict(n=1, dst=s_c), dict(n=1, dst=s_h),
              dict(n=2, dst=mix[:, 0:4], wait=lambda dve: dve.wait_ge(p_step.sem, p_step.at(4))),
              dict(n=1, dst=zv, token_major=True),
              dict(n=1, dst=s_b)],
          before=start, beside=dict(sp=sp_beside, act=act_beside, dve=dve_beside, pool=pool_beside, pe=pe_beside),
          feed=Feed(h, x_tiles, param("norm1_2"),
                    dict(squares=mix[:, 10:12], sum=mix[:, 12], rstd=rstd[:], rcol=rcol[:]),
                    late=dict(first=0, pe_after=0, act=final_act, dve=final_dve, pool=lambda pool: None, pe=final_pe,
                              ready=lambda eng, k: eng.wait_ge(final_written.sem, final_written.at(k + 1)))))
    for c, n in ((stored, 16 * KT + 16), (loaded, 160), (a_step, 7), (v_step, 32), (g_step, 6), (p_step, 8),
                 (conv_started, 4), (tap_done, N_TAPS), (conv_done, 2), (bias_step, 11), (sum_done, 12),
                 (log_done, 8), (rstd_done, 3), (value_done, 4)):
        c.advance(n)
    st.close()
    st = scope()
    q_s = sb(st, "q_s", [96, 4, SEQ])
    k_s = sb(st, "k_s", [96, 4, SEQ])
    q_hi, k_hi = sb(st, "q_hi", [P, 2, SEQ], F32R)[:], s_h.bitcast(F32R)
    q_lo, k_lo = zq.bitcast(F32R), zk.bitcast(F32R)
    v_p = sb(st, "v_p", [P, NB, P])
    bias_p = sb(st, "bias_p", [P, 2, 256])
    prob = [sb(st, f"diff_prob{b}", [P, 2, SEQ]) for b in range(2)]
    a_t = sb(st, "a_t", [P, 2, NB, P])
    diag = sb(st, "diag", [P, 2, 2, P])
    stat = sb(st, "diff_stat", [P, 2, 2, 4])
    units = [(hd, qb) for hd in range(2) for qb in range(NB)]
    NU = len(units)
    turn_groups = [(qb + 4) // 4 for _, qb in units]
    turns_before = [sum(turn_groups[:u]) for u in range(NU + 1)]
    NT = turns_before[-1]
    with nc.Block() as block:
        @block.sync
        def _(sp):
            with sp.Fori(0, 2) as it:
                sp.wait_ge(lo_done.sem, lo_done.at(it * 2 + 2))
                for hd in range(2):
                    sp.wait_ge(d_scores.sem, d_scores.at(it * 2 * NU + (hd * NU - NU)))
                    for hm in (2 * hd, 2 * hd + 1):
                        rows = slice(32 * hm, 32 * hm + 32)
                        for part, (q_part, k_part) in enumerate(((q_hi, k_hi), (q_hi, k_lo), (q_lo, k_hi))):
                            for dst, src in ((q_s, q_part), (k_s, k_part)):
                                sp.dma_start(dst[32 * part:32 * part + 32, hm, :],
                                             src.bitcast(F32)[rows, bass.ds(it, 1), :]
                                             .rearrange("p o n -> p (o n)"))\
                                  .then_inc(d_head_loaded[hd].sem, 16)
                    if hd == 0:
                        sp.wait_ge(d_biased.sem, d_biased.at(it * 2 * NU))
                        sp.dma_start(bias_p[:], bias[:, bass.ds(it * 2, 2), :]).then_inc(pair_loaded.sem, 16)
                sp.wait_ge(d_out.sem, d_out.at(it * NU))
                sp.dma_start(v_p[:], zv[:, :, bass.ds(it * P, P)]).then_inc(pair_v_loaded.sem, 16)

        @block.tensor
        def _(pe):
            pe.wait_ge(log_done.sem, log_done.at(2))
            with pe.Fori(0, 2) as it:
                def scores(u):
                    hd, qb = units[u]
                    if qb == 0:
                        pe.wait_ge(d_head_loaded[hd].sem, d_head_loaded[hd].at(it * 192 + 192))
                    w = (qb + 1) * P
                    for m in range(2):
                        pe.wait_ge(d_exp.sem, d_exp.at(it * 2 * NU + (2 * (u - 1) + m + 1 if u else 0)))
                        hm = 2 * hd + m
                        for a in range(0, w, HALF):
                            b = min(w, a + HALF)
                            mm = pe.matmul(ps[:, 2 * m + a // HALF, 0:b - a], q_s[:, hm, qb * P:(qb + 1) * P].bitcast(F32R),
                                           k_s[:, hm, a:b].bitcast(F32R), start=True, stop=True)
                        mm.then_inc(d_scores.sem, 1)

                def outputs(u):
                    hd, qb = units[u]
                    if u == 0:
                        pe.wait_ge(pair_v_loaded.sem, pair_v_loaded.at(it * 16 + 16))
                    pe.wait_ge(d_copied.sem, d_copied.at(it * NT + turns_before[u + 1]))
                    pe.wait_ge(d_stored.sem, d_stored.at(it * NU + max(u - 1, 0)))
                    for kb in range(qb + 1):
                        mm = pe.matmul(ps[64 * hd:64 * hd + 64, 6 + u % 2, 0:P], v_p[:, kb, 64 * hd:64 * hd + 64],
                                       a_t[:, u % 2, kb, :], start=(kb == 0), stop=(kb == qb))
                    mm.then_inc(d_out.sem, 1)

                scores(0)
                for u, (hd, qb) in enumerate(units):
                    if u + 1 < NU:
                        scores(u + 1)
                    pe.wait_ge(d_diff.sem, d_diff.at(it * NU + u + 1))
                    for a in range(0, qb + 1, 4):
                        n = turns_before[u] + a // 4
                        pe.wait_ge(d_copied.sem, d_copied.at(it * NT + max(n - 1, 0)))
                        for kb in range(a, min(a + 4, qb + 1)):
                            for m in range(2):
                                mm = pe.matmul(ps[:, 4 + n % 2, (kb - a) * P:(kb - a + 1) * P],
                                               prob[u % 2][:, m, kb * P:(kb + 1) * P], diag[:, u % 2, m, :],
                                               start=(m == 0), stop=(m == 1))
                        mm.then_inc(d_turned.sem, 1)
                    if u:
                        outputs(u - 1)
                outputs(NU - 1)

        @block.vector
        def _(dve):
            for n in range(4):
                z, hi = ((zq, q_hi), (zk, k_hi))[n % 2]
                dve.wait_ge(hi_done.sem, hi_done.at(n + 1))
                dve.tensor_tensor(z[:, n // 2].bitcast(F32R), z[:, n // 2], hi[:, n // 2].bitcast(F32), ALU.subtract)\
                   .then_inc(lo_done.sem, 1)
            dve.wait_ge(rstd_done.sem, rstd_done.at(1))
            for t in range(2):
                dve.scalar_tensor_tensor(out=c_a[:, t], in0=c_a[:, t], scalar=param("conf_ln_g")[:, t:t + 1],
                                         in1=ln[:, 0], op0=ALU.mult, op1=ALU.mult).then_inc(value_done.sem, 1)
            with dve.Fori(0, 2) as it:
                def soft(u):
                    hd, qb = units[u]
                    w, near = (qb + 1) * P, min(qb + 1, 2) * P
                    for m in range(2):
                        n = it * 2 * NU + 2 * u + m + 1
                        sc = ps[:, 2 * m:2 * m + 2, :].rearrange("p a n -> p (a n)")
                        dve.wait_ge(d_scores.sem, d_scores.at(n))
                        dve.wait_ge(pair_loaded.sem, pair_loaded.at(it * 16 + 16))
                        dve.tensor_tensor(sc[:, w - near:w], sc[:, w - near:w], bias_p[:, hd, 256 - near:256],
                                          ALU.add).then_inc(d_biased.sem, 1)
                        dve.wait_ge(d_biased.sem, d_biased.at(n))
                        dve.tensor_reduce(stat[:, u % 2, m, 0:1], sc[:, 0:w], AX.X, ALU.max, negate=True)\
                           .then_inc(d_max.sem, 1)

                def combine(u):
                    s = stat[:, u % 2]
                    dve.wait_ge(d_exp.sem, d_exp.at(it * 2 * NU + 2 * u + 2))
                    dve.reciprocal(s[:, :, 2:3], s[:, :, 1:2]).then_inc(d_inv.sem, 1)
                    dve.wait_ge(d_inv.sem, d_inv.at(it * NU + u + 1))
                    dve.tensor_scalar(s[:, 1, 3:4], s[:, 1, 2:3], neg_lam, None, ALU.mult).then_inc(d_inv2.sem, 1)
                    dve.wait_ge(d_inv2.sem, d_inv2.at(it * NU + u + 1))
                    dve.wait_ge(d_turned.sem, d_turned.at(it * NT + (turns_before[u - 1] if u >= 2 else 0)))
                    dve.tensor_scalar(diag[:, u % 2, 0], ident[:], s[:, 0, 2:3], None, ALU.mult)
                    dve.tensor_scalar(diag[:, u % 2, 1], ident[:], s[:, 1, 3:4], None, ALU.mult)\
                       .then_inc(d_diff.sem, 1)

                def store(u):
                    hd, qb = units[u]
                    r = slice(64 * hd, 64 * hd + 64)
                    dve.wait_ge(d_out.sem, d_out.at(it * NU + u + 1))
                    dve.tensor_copy(attn_out[r, bass.ds(it, 1), qb * P:(qb + 1) * P].rearrange("p o n -> p (o n)"),
                                    ps[r, 6 + u % 2, 0:P]).then_inc(d_stored.sem, 1)

                soft(0)
                for u in range(NU):
                    combine(u)
                    if u + 1 < NU:
                        soft(u + 1)
                    if u >= 2:
                        store(u - 2)
                store(NU - 2)
                store(NU - 1)

        @block.scalar
        def _(act):
            for n in range(4):
                z, hi = ((zq, q_hi), (zk, k_hi))[n % 2]
                act.activation(hi[:, n // 2], z[:, n // 2], ACT.Copy).then_inc(hi_done.sem, 1)
            for hf in range(2):
                act.activation(ln[:, 0, halves[hf]], ps[:, 4 + hf, :], ACT.Ln, scale=1.0 / 256, bias=eps_col)\
                   .then_inc(log_done.sem, 1)
            act.wait_ge(log_done.sem, log_done.at(2))
            act.activation(ln[:, 0], ln[:, 0], ACT.Exp, scale=-0.5).then_inc(rstd_done.sem, 1)
            for t in range(2):
                act.wait_ge(value_done.sem, value_done.at(t + 1))
                act.activation(c_a[:, t], c_a[:, t], ACT.Silu, bias=param("conf_ln_b")[:, t:t + 1])
            with act.Fori(0, 2) as it:
                def exps(u):
                    hd, qb = units[u]
                    w = (qb + 1) * P
                    for m in range(2):
                        sc = ps[:, 2 * m:2 * m + 2, :].rearrange("p a n -> p (a n)")
                        act.wait_ge(d_max.sem, d_max.at(it * 2 * NU + 2 * u + m + 1))
                        act.wait_ge(d_turned.sem, d_turned.at(it * NT + (turns_before[u - 1] if u >= 2 else 0)))
                        act.activation(prob[u % 2][:, m, 0:w], sc[:, 0:w], ACT.Exp, bias=stat[:, u % 2, m, 0:1],
                                       accum_out=stat[:, u % 2, m, 1:2]).then_inc(d_exp.sem, 1)

                exps(0)
                for u, (hd, qb) in enumerate(units):
                    if u + 1 < NU:
                        exps(u + 1)
                    act.wait_ge(d_out.sem, d_out.at(it * NU + max(u - 1, 0)))
                    for a in range(0, qb + 1, 4):
                        n = turns_before[u] + a // 4
                        b = min(a + 4, qb + 1)
                        act.wait_ge(d_turned.sem, d_turned.at(it * NT + n + 1))
                        act.activation(a_t[:, u % 2, a:b, :].rearrange("p a n -> p (a n)"),
                                       ps[:, 4 + n % 2, 0:(b - a) * P], ACT.Copy).then_inc(d_copied.sem, 1)
    for c, n in ((hi_done, 4), (lo_done, 4), (log_done, 2), (rstd_done, 1), (value_done, 2)):
        c.advance(n)
    st.close()

    y_stack = scope()
    y = (sb(y_stack, "y3_hi", [P, KT, SEQ], F32R), sb(y_stack, "y3_lo", [P, KT, SEQ], F32R))
    parts = [xr[:, 0], xr[:, 1], s_c[:, 0], s_c[:, 1], c_a[:, 0], c_a[:, 1], attn_out[:, 0], attn_out[:, 1]]
    start, wait = reload_x(x_spill)

    root2 = zq

    def norm2_pool(pool):
        for t in range(2):
            pool.tensor_tensor(root2[:, t], attn_out[:, t], attn_out[:, t], ALU.mult).then_inc(g_step.sem, 1)

    def norm2_pe(pe):
        for u in range(4):
            pe.wait_ge(g_step.sem, g_step.at(u // 2 + 1))
            pe.matmul(ps[:, 4 + u, :], ones64[:], root2[:, u // 2, halves[u % 2]], start=True, stop=True)\
              .then_inc(sum_done.sem, 1)

    def norm2_act(act):
        for u in range(4):
            act.wait_ge(sum_done.sem, sum_done.at(u + 1))
            act.activation(root2[:, u // 2, halves[u % 2]], ps[:, 4 + u, :], ACT.Sqrt, scale=1.0 / HV2, bias=eps_col)\
               .then_inc(log_done.sem, 1)

    def norm2_dve(dve):
        for u in range(4):
            r, z = (x[:, u // 2, halves[u % 2]] for x in (root2, attn_out))
            dve.wait_ge(log_done.sem, log_done.at(u + 1))
            dve.reciprocal(r, r).then_inc(value_done.sem, 1)
            dve.wait_ge(value_done.sem, value_done.at(u + 1))
            dve.scalar_tensor_tensor(out=z, in0=z, scalar=o_gain, in1=r, op0=ALU.mult, op1=ALU.mult)\
               .then_inc(v_step.sem, 1)

    dense(y, [dict(n=4, dst=xr, add=True, wait=wait)], before=start,
          feed=Feed(y, parts, late=dict(first=6, pe_after=2, act=norm2_act, dve=norm2_dve, pool=norm2_pool,
                                        pe=norm2_pe,
                                        ready=lambda eng, k: eng.wait_ge(v_step.sem, v_step.at(2 * (k - 5))))))
    for c, n in ((g_step, 2), (sum_done, 4), (log_done, 4), (value_done, 4), (v_step, 4)):
        c.advance(n)
    loaded.advance(16 * KT)
    y_stack.close()
    m2.close()

    mlp(param("norm2_2"), FF2_CHUNKS, True, "ff2")
    with nc.Block() as block:
        @block.sync
        def _(sp):
            for k in range(KT):
                sp.dma_start(out_t[:, k, :], xr[:, k, :]).then_inc(stored.sem, 16)
            sp.wait_ge(stored.sem, stored.at(16 * KT))


def slab_up(w, c):
    return w[:, c:c + CB].reshape(KT, P, CB).transpose(1, 0, 2).reshape(P, SLAB)


def slab_down(w, r):
    return w[r:r + CB].reshape(2, P, D).transpose(1, 0, 2).reshape(P, SLAB)


def feature_columns(v, n):
    return np.reshape(v, (n, P)).T


def lay_out(a):
    a = {k: np.asarray(v) for k, v in a.items()}
    m = {k: (v[0] if v.ndim > 1 and v.shape[0] == 1 else v) for k, v in a.items()}

    def ups(w, c0=0, c1=None):
        return [slab_up(w, c) for c in range(c0, w.shape[1] if c1 is None else c1, CB)]

    slabs = ups(m["w_in"], 0, 3072)
    for name in ("w_out", "xa_wk", "xa_wv", "xa_wq", "xa_wo"):
        slabs += ups(m[name])
    up, down = ups(m["ffn_w1"]), [slab_down(m["ffn_w2"], r) for r in range(0, 4096, CB)]
    slabs.append(up[0])
    for c in range(1, FF1_CHUNKS):
        slabs += [up[c], down[c - 1]]
    slabs.append(down[-1])
    pool, s_b, s_c, s_h, c_a, c_g, zq, zk, zv = ups(m["w_in_2"])
    slabs += [c_a, c_g, pool, s_c, s_h, zq, zk, zv, s_b] + ups(m["w_out_2"])
    gate, up = ups(m["w_gate_2"]), ups(m["w_up_2"])
    down = [slab_down(m["w_down_2"], r) for r in range(0, 2816, CB)]
    slabs += [gate[0], up[0]]
    for c in range(1, FF2_CHUNKS):
        slabs += [gate[c], up[c], down[c - 1]]
    slabs.append(down[-1])

    params = np.zeros((P, N_PARAMS), np.float32)

    def put(name, v):
        lo, hi = PARAM_COLS[name]
        params[:v.shape[0], lo:hi] = v

    for name, src in (("norm_mix", "norm_mix"), ("norm_xa", "norm_xa"), ("norm_mem", "norm_mem"),
                      ("norm_ffn", "norm_ffn"), ("norm_final", "norm_final"), ("norm1_2", "norm1_g_2"),
                      ("norm2_2", "norm2_g_2")):
        put(name, feature_columns(m[src], 8))
    put("gm_ln_g", m["gm_ln_g"].T)
    put("dn_conv", m["dn_conv"].reshape(CONV_W, 12, P).transpose(2, 1, 0).reshape(P, 48))
    put("dn_a_log", np.tile(np.reshape(m["dn_a_log"], (1, 4)), (P, 1)))
    put("dn_dt_bias", np.tile(np.reshape(m["dn_dt_bias"], (1, 4)), (P, 1)))
    put("dn_onorm", np.reshape(m["dn_onorm"], (P, 1)))
    put("w_logits", m["w_in"][:, 3072:3080].reshape(KT, P, 8).transpose(1, 0, 2).reshape(P, 64))
    put("pool_scale", feature_columns(m["pool_scale_2"], 2))
    put("sconv_w", m["sconv_w_2"].reshape(3, 2, P).transpose(2, 1, 0).reshape(P, 6))
    put("conf_dw_w", m["conf_dw_w_2"].reshape(CONF_K, 2, P).transpose(2, 1, 0).reshape(P, 62))
    put("conf_dw_b", feature_columns(m["conf_dw_b_2"], 2))
    put("conf_ln_g", feature_columns(m["conf_ln_g_2"], 2))
    put("conf_ln_b", feature_columns(m["conf_ln_b_2"], 2))
    put("q_norm", np.tile(np.reshape(m["q_norm_g_2"], (QK2, 1)), (4, 1)))
    put("k_norm", np.tile(np.reshape(m["k_norm_g_2"], (QK2, 1)), (4, 1)))
    put("subln", np.tile(np.reshape(m["subln_g_2"], (HV2, 1)), (2, 1)))
    put("lam", np.tile(np.concatenate([np.reshape(m[n], (1, QK2)) for n in
                                       ("lam_q1_2", "lam_k1_2", "lam_q2_2", "lam_k2_2")], 1), (P, 1)))
    put("rel_bias", m["rel_bias_2"])

    pool_w = np.zeros((P, 2, P), np.float32)
    for g in range(4):
        o = (g % 2) * 64
        pool_w[o:o + 64, g // 2, o:o + 64] = m["pool_w_2"][g]
    return {
        "x_t": m["x"].T.reshape(KT, P, SEQ).transpose(1, 0, 2),
        "mem_t": m["mem"].T.reshape(KT, P, MEM).transpose(1, 0, 2),
        "slabs": np.stack(slabs),
        "params": params,
        "row_params": np.concatenate([m["gm_ln_b"].reshape(1, 512), m["gm_bs"].reshape(1, 512)], 1),
        "gm_ws_t": m["gm_ws"].transpose(2, 0, 1).reshape(P, 512),
        "pool_w": pool_w.reshape(P, 2 * P),
        "consts": constant_tables(),
    }


def kernel(**inputs):
    import concourse.bacc as bacc
    from concourse.bass_utils import run_bass_kernel_spmd

    arrays = {f"in_{k}_dram": np.ascontiguousarray(v) for k, v in lay_out(inputs).items()}
    nc = bacc.Bacc("TRN2", target_bir_lowering=False, num_devices=1)
    ins = {k[3:-5]: nc.dram_tensor(k, v.shape, F32, kind="ExternalInput").ap() for k, v in arrays.items()}
    out_t = nc.dram_tensor("out_0_dram", (P, KT, SEQ), F32, kind="ExternalOutput").ap()
    x_spill = nc.dram_tensor("x_spill", (P, KT, SEQ), F32, kind="Internal").ap()
    bias_skew = nc.dram_tensor("bias_skew", (HEADS, P, 400), F32, kind="Internal").ap()
    with ExitStack() as main:
        build(nc, main, **ins, x_spill=x_spill, bias_skew=bias_skew, out_t=out_t)
    r = run_bass_kernel_spmd(nc, [arrays], core_ids=[0])
    return np.ascontiguousarray(r.results[0]["out_0_dram"].transpose(2, 1, 0).reshape(1, SEQ, D))
```
